# Optimizing a Trainium2 kernel written in Bass

```python
import math
import jax, jax.numpy as jnp
from jax import lax
import numpy as np

D_MODEL = 1024
BATCH = 1
SEQ = 512
DEPTH = 1

N_HEADS = 16
HEAD_DIM = D_MODEL // N_HEADS
N_MIXERS = 2
CHUNK = 64
LEFT_CHUNKS = 8
BAND = (LEFT_CHUNKS + 1) * CHUNK
REL_CLIP = 128
N_REL = (CHUNK - 1) + REL_CLIP + 1
Q_BLOCK = 128
D_FF = int(math.ceil(D_MODEL * 8 / 3 / 256) * 256)
N_A_LAYERS = (DEPTH + N_MIXERS - 1) // N_MIXERS
RMS_EPS = 1e-6


def rms_norm(x, g):
    xf = x.astype(jnp.float32)
    y = xf * lax.rsqrt(jnp.mean(xf * xf, axis=-1, keepdims=True) + RMS_EPS)
    return (y * g.astype(jnp.float32)).astype(x.dtype)

def split_heads(h, w_qkv):
    b, s, _ = h.shape
    qkv = (h @ w_qkv).reshape(b, s, 3, N_HEADS, HEAD_DIM)
    qkv = jnp.transpose(qkv, (2, 0, 3, 1, 4))
    return qkv[0], qkv[1], qkv[2]

def merge_heads(o):
    b, h, s, d = o.shape
    return jnp.transpose(o, (0, 2, 1, 3)).reshape(b, s, h * d)

def chunk_relpos_attention(h, w_qkv, w_o, rel_bias):
    b, s, _ = h.shape
    n_chunks = s // CHUNK
    q, k, v = split_heads(h, w_qkv)
    i_idx = np.arange(CHUNK)[:, None]
    j_idx = np.arange(BAND)[None, :]
    rel = np.clip(LEFT_CHUNKS * CHUNK + i_idx - j_idx, -(CHUNK - 1), REL_CLIP) + (CHUNK - 1)
    bias = jnp.take(rel_bias, jnp.asarray(rel, dtype=jnp.int32), axis=1).astype(jnp.float32)
    scale = 1.0 / math.sqrt(HEAD_DIM)
    outs = []
    for c in range(n_chunks):
        k0 = max(0, (c - LEFT_CHUNKS) * CHUNK)
        k1 = (c + 1) * CHUNK
        n_keys = k1 - k0
        q_blk = q[:, :, c * CHUNK:(c + 1) * CHUNK]
        sc = jnp.einsum('bhqd,bhkd->bhqk', q_blk, k[:, :, k0:k1]).astype(jnp.float32) * scale
        sc = sc + bias[None, :, :, BAND - n_keys:]
        p = jax.nn.softmax(sc, axis=-1).astype(v.dtype)
        outs.append(jnp.einsum('bhqk,bhkd->bhqd', p, v[:, :, k0:k1]))
    o = jnp.concatenate(outs, axis=2)
    return merge_heads(o) @ w_o

def stick_breaking_attention(h, w_qkv, w_o):
    b, s, _ = h.shape
    q, k, v = split_heads(h, w_qkv)
    scale = 1.0 / math.sqrt(HEAD_DIM)
    outs = []
    for qb in range(s // Q_BLOCK):
        n_keys = (qb + 1) * Q_BLOCK
        q_blk = q[:, :, qb * Q_BLOCK:(qb + 1) * Q_BLOCK]
        z = jnp.einsum('bhqd,bhkd->bhqk', q_blk, k[:, :, :n_keys]).astype(jnp.float32) * scale
        t_pos = qb * Q_BLOCK + np.arange(Q_BLOCK)
        causal = jnp.asarray((np.arange(n_keys)[None, :] < t_pos[:, None])[None, None])
        log_keep = jnp.where(causal, jax.nn.log_sigmoid(-z), 0.0)
        suffix = lax.cumsum(log_keep, axis=3, reverse=True) - log_keep
        a = jnp.where(causal, jnp.exp(jax.nn.log_sigmoid(z) + suffix), 0.0).astype(v.dtype)
        outs.append(jnp.einsum('bhqk,bhkd->bhqd', a, v[:, :, :n_keys]))
    o = jnp.concatenate(outs, axis=2)
    return merge_heads(o) @ w_o

def swiglu(h, w_gate, w_up, w_down):
    return (jax.nn.silu(h @ w_gate) * (h @ w_up)) @ w_down

def first_inputs(seed: int = 0) -> dict:
    key = jax.random.key(seed)
    ks = jax.random.split(key, 12)
    d, f = D_MODEL, D_FF
    nrm = lambda k, shape, fan: jax.random.normal(k, shape, jnp.float32) * (fan ** -0.5)
    gain = lambda k: 1.0 + 0.02 * jax.random.normal(k, (DEPTH, d), jnp.float32)
    return {
        "x": jax.random.normal(ks[0], (BATCH, SEQ, d), jnp.float32),
        "g_pre_mix": gain(ks[1]),
        "g_post_mix": gain(ks[2]),
        "w_qkv": nrm(ks[3], (DEPTH, d, 3 * d), d),
        "w_o": nrm(ks[4], (DEPTH, d, d), d),
        "rel_bias": 0.5 * jax.random.normal(ks[5], (N_A_LAYERS, N_HEADS, N_REL), jnp.float32),
        "g_pre_ffn": gain(ks[6]),
        "g_post_ffn": gain(ks[7]),
        "w_gate": nrm(ks[8], (DEPTH, d, f), d),
        "w_up": nrm(ks[9], (DEPTH, d, f), d),
        "w_down": nrm(ks[10], (DEPTH, f, d), f),
    }

def first_block(x, g_pre_mix, g_post_mix, w_qkv, w_o, rel_bias, g_pre_ffn, g_post_ffn, w_gate, w_up, w_down):
    for i in range(DEPTH):
        h = rms_norm(x, g_pre_mix[i])
        if i % N_MIXERS == 0:
            m = chunk_relpos_attention(h, w_qkv[i], w_o[i], rel_bias[i // N_MIXERS])
        else:
            m = stick_breaking_attention(h, w_qkv[i], w_o[i])
        x = x + rms_norm(m, g_post_mix[i])
        h = rms_norm(x, g_pre_ffn[i])
        x = x + rms_norm(swiglu(h, w_gate[i], w_up[i], w_down[i]), g_post_ffn[i])
    return x


N_BRANCH = 4
BRANCH_WIDTH = 512
EPS = 1e-6
GM_GROUPS = 4
GM_CHUNK = 128
GM_GROUP_DIM = BRANCH_WIDTH // GM_GROUPS
DSA_HEADS = 4
DSA_HEAD_DIM = BRANCH_WIDTH // DSA_HEADS
DSA_LATENT = 128
IDX_HEADS = 4
IDX_DIM = 64
TOPK_MAX = 256
CONV_WIDTH = 3
FOX_HEADS = 4
FOX_HEAD_DIM = BRANCH_WIDTH // FOX_HEADS

W = BRANCH_WIDTH
IN_SPLITS = (
    W, W, W,
    W, DSA_LATENT, IDX_HEADS * IDX_DIM, IDX_DIM, IDX_HEADS, W,
    W, W, W, W,
    W, W, W, FOX_HEADS, W,
    N_BRANCH * D_MODEL,
)
IN_WIDTH = sum(IN_SPLITS)


def rms_norm_2(x, g):
    xf = x.astype(jnp.float32)
    y = xf * lax.rsqrt(jnp.mean(xf * xf, axis=-1, keepdims=True) + EPS)
    return (y * g.astype(jnp.float32)).astype(x.dtype)

def layer_norm(x, g, b):
    xf = x.astype(jnp.float32)
    mu = jnp.mean(xf, axis=-1, keepdims=True)
    var = jnp.mean(jnp.square(xf - mu), axis=-1, keepdims=True)
    y = (xf - mu) * lax.rsqrt(var + EPS)
    return (y * g.astype(jnp.float32) + b.astype(jnp.float32)).astype(x.dtype)

def to_blocks(a):
    b, s = a.shape[0], a.shape[1]
    return jnp.moveaxis(a.reshape(b, s // Q_BLOCK, Q_BLOCK, *a.shape[2:]), 1, 0)

def from_blocks(a):
    nb, b = a.shape[0], a.shape[1]
    return jnp.moveaxis(a, 0, 1).reshape(b, nb * Q_BLOCK, a.shape[-1])

def chunked_spatial_gating(u, v, ln_g, ln_b, w_s, b_s):
    bsz, s, _ = v.shape
    v = layer_norm(v, ln_g, ln_b)
    vc = v.reshape(bsz, s // GM_CHUNK, GM_CHUNK, GM_GROUPS, GM_GROUP_DIM)
    mask = jnp.tril(jnp.ones((GM_CHUNK, GM_CHUNK), dtype=bool))
    w = jnp.where(mask[None], w_s, jnp.zeros_like(w_s))
    mixed = jnp.einsum('gts,bcsge->bctge', w, vc) + jnp.transpose(b_s)[None, None, :, :, None]
    return u * mixed.reshape(bsz, s, W)

def dsa_attention(q, c_kv, q_idx, k_idx, w_idx, kv_g, w_uk, w_uv):
    bsz, s, _ = q.shape
    k_sel = min(TOPK_MAX, s // 4)
    c = rms_norm_2(c_kv, kv_g)
    qh = q.reshape(bsz, s, DSA_HEADS, DSA_HEAD_DIM)
    q_lat = jnp.einsum('bshd,hld->bshl', qh, w_uk)
    qi = q_idx.reshape(bsz, s, IDX_HEADS, IDX_DIM)
    wi = w_idx * (IDX_HEADS ** -0.5)
    key_pos = jnp.arange(s)
    gather = jax.vmap(lambda cb, ib: cb[ib])

    def block(args):
        qlb, qib, wib, blk = args
        pos_q = blk * Q_BLOCK + jnp.arange(Q_BLOCK)
        dots = jnp.einsum('bqhd,bsd->bqhs', qib, k_idx).astype(jnp.float32) * (IDX_DIM ** -0.5)
        score = jnp.einsum('bqh,bqhs->bqs', wib.astype(jnp.float32), jax.nn.relu(dots))
        causal = key_pos[None, :] <= pos_q[:, None]
        score = jnp.where(causal[None], score, -jnp.inf)
        _, idx = lax.top_k(score, k_sel)
        valid = idx <= pos_q[None, :, None]
        c_sel = gather(c, idx)
        logits = jnp.einsum('bqhl,bqkl->bqhk', qlb, c_sel).astype(jnp.float32) * (DSA_HEAD_DIM ** -0.5)
        logits = jnp.where(valid[:, :, None, :], logits, -jnp.inf)
        p = jax.nn.softmax(logits, axis=-1).astype(c.dtype)
        o_lat = jnp.einsum('bqhk,bqkl->bqhl', p, c_sel)
        o = jnp.einsum('bqhl,hld->bqhd', o_lat, w_uv)
        return o.reshape(bsz, Q_BLOCK, W)

    nb = s // Q_BLOCK
    out = lax.map(block, (to_blocks(q_lat), to_blocks(qi), to_blocks(wi), jnp.arange(nb)))
    return from_blocks(out)

def short_gated_conv(b_gate, c_gate, x_in, conv_w):
    s = x_in.shape[1]
    y = c_gate * x_in
    yp = jnp.pad(y, ((0, 0), (CONV_WIDTH - 1, 0), (0, 0)))
    conv = conv_w[0] * yp[:, 0:s]
    for j in range(1, CONV_WIDTH):
        conv = conv + conv_w[j] * yp[:, j:j + s]
    return b_gate * conv

def forgetting_attention(q, k, v, f_logit, b_f):
    bsz, s, _ = q.shape
    qh = q.reshape(bsz, s, FOX_HEADS, FOX_HEAD_DIM)
    kh = k.reshape(bsz, s, FOX_HEADS, FOX_HEAD_DIM)
    vh = v.reshape(bsz, s, FOX_HEADS, FOX_HEAD_DIM)
    cum = jnp.cumsum(jax.nn.log_sigmoid((f_logit + b_f).astype(jnp.float32)), axis=1)
    cum_k = jnp.transpose(cum, (0, 2, 1))
    key_pos = jnp.arange(s)

    def block(args):
        qb, cq, blk = args
        pos_q = blk * Q_BLOCK + jnp.arange(Q_BLOCK)
        logits = jnp.einsum('bqhd,bshd->bhqs', qb, kh).astype(jnp.float32) * (FOX_HEAD_DIM ** -0.5)
        logits = logits + jnp.transpose(cq, (0, 2, 1))[..., None] - cum_k[:, :, None, :]
        logits = jnp.where((key_pos[None, :] <= pos_q[:, None])[None, None], logits, -jnp.inf)
        p = jax.nn.softmax(logits, axis=-1).astype(vh.dtype)
        o = jnp.einsum('bhqs,bshd->bqhd', p, vh)
        return o.reshape(bsz, Q_BLOCK, W)

    nb = s // Q_BLOCK
    out = lax.map(block, (to_blocks(qh), to_blocks(cum), jnp.arange(nb)))
    return from_blocks(out)

def hybrid_layer(x, norm_g, w_in, gm_ln_g, gm_ln_b, gm_w_s, gm_b_s, dsa_kv_g, dsa_w_uk, dsa_w_uv,
                 conv_w, fox_b_f, w_branch, w_out):
    bsz, s, d = x.shape
    h = rms_norm_2(x, norm_g)
    proj = h @ w_in
    points = [int(p) for p in np.cumsum(np.array(IN_SPLITS))[:-1]]
    (a_u, a_v, a_z,
     b_q, b_c, b_qi, b_ki, b_wi, b_z,
     c_b, c_c, c_x, c_z,
     d_q, d_k, d_v, d_f, d_z,
     gates) = jnp.split(proj, points, axis=-1)
    y_a = chunked_spatial_gating(a_u, a_v, gm_ln_g, gm_ln_b, gm_w_s, gm_b_s) * jax.nn.silu(a_z)
    y_b = dsa_attention(b_q, b_c, b_qi, b_ki, b_wi, dsa_kv_g, dsa_w_uk, dsa_w_uv) * jax.nn.silu(b_z)
    y_c = short_gated_conv(c_b, c_c, c_x, conv_w) * jax.nn.silu(c_z)
    y_d = forgetting_attention(d_q, d_k, d_v, d_f, fox_b_f) * jax.nn.silu(d_z)
    ys = jnp.stack([y_a, y_b, y_c, y_d], axis=0)
    branch_d = jnp.einsum('nbsw,nwd->bsnd', ys, w_branch)
    g = jax.nn.sigmoid(gates.reshape(bsz, s, N_BRANCH, d))
    merged = jnp.sum(g * branch_d, axis=2)
    return x + merged @ w_out

def second_inputs(seed: int = 0) -> dict:
    key = jax.random.key(seed)
    ks = jax.random.split(key, 16)
    f32 = jnp.float32
    nrm = lambda k, shp, sc: jax.random.normal(k, shp, f32) * sc
    return {
        'x': nrm(ks[0], (BATCH, SEQ, D_MODEL), 1.0),
        'norm_g': 1.0 + nrm(ks[1], (DEPTH, D_MODEL), 0.05),
        'w_in': nrm(ks[2], (DEPTH, D_MODEL, IN_WIDTH), D_MODEL ** -0.5),
        'gm_ln_g': 1.0 + nrm(ks[3], (DEPTH, W), 0.05),
        'gm_ln_b': nrm(ks[4], (DEPTH, W), 0.02),
        'gm_w_s': nrm(ks[5], (DEPTH, GM_GROUPS, GM_CHUNK, GM_CHUNK), GM_CHUNK ** -0.5),
        'gm_b_s': 1.0 + nrm(ks[6], (DEPTH, GM_GROUPS, GM_CHUNK), 0.1),
        'dsa_kv_g': 1.0 + nrm(ks[7], (DEPTH, DSA_LATENT), 0.05),
        'dsa_w_uk': nrm(ks[8], (DEPTH, DSA_HEADS, DSA_LATENT, DSA_HEAD_DIM), DSA_LATENT ** -0.5),
        'dsa_w_uv': nrm(ks[9], (DEPTH, DSA_HEADS, DSA_LATENT, DSA_HEAD_DIM), DSA_LATENT ** -0.5),
        'conv_w': nrm(ks[10], (DEPTH, CONV_WIDTH, W), CONV_WIDTH ** -0.5),
        'fox_b_f': jax.random.uniform(ks[11], (DEPTH, FOX_HEADS), f32, minval=1.0, maxval=4.0),
        'w_branch': nrm(ks[12], (DEPTH, N_BRANCH, W, D_MODEL), W ** -0.5),
        'w_out': nrm(ks[13], (DEPTH, D_MODEL, D_MODEL), 0.5 * D_MODEL ** -0.5),
        'final_g': 1.0 + nrm(ks[14], (D_MODEL,), 0.05),
    }

def second_block(x, norm_g, w_in, gm_ln_g, gm_ln_b, gm_w_s, gm_b_s, dsa_kv_g, dsa_w_uk, dsa_w_uv,
              conv_w, fox_b_f, w_branch, w_out, final_g):
    h = x
    for l in range(DEPTH):
        h = hybrid_layer(h, norm_g[l], w_in[l], gm_ln_g[l], gm_ln_b[l], gm_w_s[l], gm_b_s[l],
                         dsa_kv_g[l], dsa_w_uk[l], dsa_w_uv[l], conv_w[l], fox_b_f[l],
                         w_branch[l], w_out[l])
    return rms_norm_2(h, final_g)


def setup_inputs(seed=0):
    out = dict(first_inputs(seed))
    for name, value in second_inputs(seed + 1).items():
        if name != "x":
            out[name + "_2"] = value
    return out


def reference(
    x, g_pre_mix, g_post_mix, w_qkv, w_o, rel_bias, g_pre_ffn, g_post_ffn, w_gate, w_up, w_down,
    norm_g_2, w_in_2, gm_ln_g_2, gm_ln_b_2, gm_w_s_2, gm_b_s_2, dsa_kv_g_2, dsa_w_uk_2,
    dsa_w_uv_2, conv_w_2, fox_b_f_2, w_branch_2, w_out_2, final_g_2,
):
    x = first_block(
        x, g_pre_mix, g_post_mix, w_qkv, w_o, rel_bias, g_pre_ffn, g_post_ffn, w_gate, w_up,
        w_down,
    )
    return second_block(
        x, norm_g_2, w_in_2, gm_ln_g_2, gm_ln_b_2, gm_w_s_2, gm_b_s_2, dsa_kv_g_2, dsa_w_uk_2,
        dsa_w_uv_2, conv_w_2, fox_b_f_2, w_branch_2, w_out_2, final_g_2,
    )


_drawn_inputs = setup_inputs


def setup_inputs(seed=0):
    import zlib

    import numpy as np

    out = dict(_drawn_inputs(seed))
    spreads = {}
    factors = {'g_post_mix': 3.314,
     'g_pre_ffn': 3.199,
     'g_post_ffn': 4.819,
     'norm_g_2': 4.023,
     'gm_ln_g_2': 28.183,
     'gm_ln_b_2': 64.0,
     'gm_b_s_2': 6.193,
     'dsa_kv_g_2': 22.882,
     'dsa_w_uk_2': 4.159,
     'fox_b_f_2': 50.424}
    for name, (base, spread) in spreads.items():
        noise = np.random.default_rng([zlib.crc32(name.encode()), seed]).standard_normal(out[name].shape)
        drawn = base * np.exp(spread * noise) if base else spread * noise
        out[name] = __import__('jax').numpy.asarray(drawn.astype(out[name].dtype))
    for name, factor in factors.items():
        out[name] = (out[name] * factor).astype(out[name].dtype)
    return out
```

```python
from contextlib import ExitStack

import numpy as np

import concourse.bass as bass
from concourse import mybir

F32 = mybir.dt.float32
F32R = mybir.dt.float32r
ACT = mybir.ActivationFunctionType
ALU = mybir.AluOpType
AX_X = mybir.AxisListType.X

P = 128
S = 512
TT = S // P
D = 1024
KD = D // P
HEADS, HD = 16, 64
CHUNK = 64
REL_CLIP = 128
BIAS_W = 2 * P
FF = 2816
FC = FF // P
FH = FC // 2
W = 512
KW = W // P
BH, BD = 4, 128
IDX_H, IDX_D = 4, 64
TOPK = min(256, S // 4)
N_BRANCH = 4
EPS = 1e-6
NEG = -1e30
TAKEN, ACAUSAL = -3.4e38, -3.0e38
BLK = 2048
RING = 2

_SPLITS = [("a_u", W), ("a_v", W), ("a_z", W), ("b_q", W), ("b_c", P), ("b_qi", IDX_H * IDX_D), ("b_ki", IDX_D),
           ("b_wi", IDX_H), ("b_z", W), ("c_b", W), ("c_c", W), ("c_x", W), ("c_z", W), ("d_q", W), ("d_k", W),
           ("d_v", W), ("d_f", BH), ("d_z", W), ("gates", N_BRANCH * D)]
COL = {}
_at = 0
for _name, _width in _SPLITS:
    COL[_name] = (_at, _at + _width)
    _at += _width
IN_W = _at

ORDER = "dbac"
BRANCH = {"a": 0, "b": 1, "c": 2, "d": 3}


FEATURE_MAJOR = {"b_q", "d_q", "d_k", "d_z", "b_z"} | {f"gate_{br}{i}" for br in ORDER for i in range(2)}


def plan():
    first, use, done, n, e, open_blocks = {}, {}, [], 0, 0, 0

    def add(name, blocks, uses):
        nonlocal n, e, open_blocks
        first[name], use[name] = n, e
        for i in range(blocks):
            if uses % blocks or (uses == TT and name not in FEATURE_MAJOR and i < blocks - 1):
                open_blocks += 1
                done.append(("w_used", open_blocks))
            else:
                done.append(("bank_full", e + uses * (i + 1) // blocks))
        if done[-1][0] == "w_used":
            open_blocks -= 1
            done[-1] = ("bank_full", e + uses)
        n += blocks
        e += uses

    add("q", 4, 8)
    add("k", 4, 8)
    for h in range(2):
        add(f"v{h}", 2, TT)
    for h in range(2):
        add(f"wo{h}", 2, TT)
    for f in range(2):
        add(f"gu{f}", FH, 2 * FH)
        for h in range(2):
            add(f"down{f}{h}", 3, TT)
    add("qi", 1, 2)
    add("ki", 1, 1)
    add("cwf", 1, TT)
    add("b_q", 2, 4)
    add("d_q", 2, 4)
    add("d_k", 2, 4)
    add("d_v", 2, TT)
    add("d_z", 2, 4)
    for br in ORDER:
        if br == "b":
            add("b_z", 2, 4)
        if br == "a":
            add("a_v", 2, TT)
            add("a_uz", 4, 8)
        if br == "c":
            add("c", 8, 16)
        for half in range(2):
            add(f"gate_{br}{half}", 2, 4)
            add(f"branch_{br}{half}", 1, 4)
    for h in range(2):
        add(f"out{h}", 2, TT)
    return first, use, done


FIRST, USE, DONE = plan()
N_BLOCKS = len(DONE)

UNITS = [("mha", h, t) for h in range(HEADS) for t in range(TT)]
UNITS += [("fox", h, t) for h in range(BH) for t in range(TT)]
UNITS += [("dsa", h, t) for h in range(BH) for t in range(TT)]
U_FOX = HEADS * TT
U_DSA = U_FOX + BH * TT
N_UNITS = len(UNITS)

NORMS = [("pre0", t) for t in range(TT)]
for _r in (1, 2):
    _seq = [(f"post{_r}", 0)]
    for _t in range(1, TT):
        _seq += [(f"post{_r}", _t), (f"pre{_r}", _t - 1)]
    NORMS += _seq + [(f"pre{_r}", TT - 1)]
NORMS += [("c", t) for t in range(TT)] + [("ln", t) for t in range(TT)] + [("final", t) for t in range(TT)]
NCOL = {n: i for i, n in enumerate(NORMS)}


def build(nc, dram, out):
    ctx = ExitStack()
    with ctx:
        def sb(name, shape, dt=F32):
            return ctx.enter_context(nc.sbuf_tensor(name, shape, dt))

        def sem(name):
            return ctx.enter_context(nc.semaphore(name))

        w_raw = [sb(f"w_raw{i}", [P, BLK]) for i in range(RING)]
        w_hi = [sb(f"w_hi{i}", [P, BLK], F32R) for i in range(RING)]
        w_lo = [sb(f"w_lo{i}", [P, BLK], F32R) for i in range(RING)]
        xT_hi = sb("xT_hi", [P, KD, S], F32R)
        xT_lo = sb("xT_lo", [P, KD, S], F32R)
        act_hi = sb("act_hi", [P, FH, S], F32R)
        act_lo = sb("act_lo", [P, FH, S], F32R)
        x_sb = sb("x_sb", [P, TT, D])
        g_pre = sb("g_pre", [P, D])
        g_post = sb("g_post", [P, D])
        arena = sb("arena", [P, 12800])
        ident = sb("ident", [P, P])
        cmask = sb("cmask", [P, P])
        wukT = sb("wukT", [P, BH, P])
        wuv = sb("wuv", [P, BH, P])
        kvg = sb("kvg", [P, P])
        convw = sb("convw", [P, KW, 3])
        bf = sb("bf", [P, BH])
        minus_half = sb("minus_half", [P, 1])
        sumsq = sb("sumsq", [P, len(NORMS)])
        var = sb("var", [P, len(NORMS)])
        rstd = sb("rstd", [P, len(NORMS)])
        mean = sb("mean", [P, TT])
        negmax = sb("negmax", [P, 4])
        psums = sb("psums", [P, 4])
        rinv = sb("rinv", [P, 4])
        wi = sb("wi", [P, TT, IDX_H])
        fb = sb("fb", [P, TT, BH])
        fna = sb("fna", [P, TT, BH])
        fl = sb("fl", [P, TT, BH])
        ls = sb("ls", [P, TT, BH])
        cumq = sb("cumq", [P, TT, BH])
        top8 = sb("top8", [P, 8])

        def view(at, *shape):
            n = int(np.prod(shape))
            v = arena[:, at:at + n]
            if len(shape) == 2:
                v = v.rearrange("p (a b) -> p a b", b=shape[1])
            if len(shape) == 3:
                v = v.rearrange("p (a b c) -> p a b c", b=shape[1], c=shape[2])
            return v

        qkT = view(0, 2 * KD, S)
        v_sb = x_sb
        biases = view(8192, 4, BIAS_W)
        s_ring = view(9728, 4, S)
        pT = view(9728 + 4 * S, 2, S)
        m_sb = view(0, TT, D)
        xn = view(4096, 2, D)
        junk = view(6144, D)
        sg = view(7168, 2, S)
        a_sb = view(8192, 2, S)
        qlat = view(0, BH, S)
        dv = view(2048, TT, W)
        negcumk = view(4096, BH, S)
        qi = view(4096, 2, S)
        ki = view(4096 + 2 * S, S)
        sz = view(6144, KW, S)
        bq = sz
        sel_at = [8192 + P * (t * (t + 1) // 2) for t in range(TT)]
        sel = [view(sel_at[t], P * (t + 1)) for t in range(TT)]
        relu_d = view(9728, 2, S)
        lsx = view(9728, BH, TT, P)
        c_raw = view(9728 + 4 * S, TT, P)
        tri = view(9728 + 5 * S, S)
        c_sb = g_pre[:, 0:S].rearrange("p (a b) -> p a b", b=P)
        cT = g_pre[:, S:2 * S]
        dqk = x_sb[:, :, :].rearrange("p t (a s) -> p (t a) s", s=S)
        merged = dqk
        sig = view(2048, 4, S)
        tmp = view(9728, 2, S)
        av = view(0, TT, W)
        a_mix = view(4096, KW, S)
        a_sz = view(6144, 2, S)
        a_y = view(6144 + 2 * S, 2, S)
        a_bs = view(8192, KW, P)
        a_ws = view(8192 + KW * P, KW, P)
        a_junk = view(9728, TT, W)
        c_y = view(0, 2, S + 4)
        c_cc = view(4096, 2, S)
        c_acc = view(4096 + 2 * S, 2, S)
        c_sz, c_o = a_sz, a_y
        y_hi = [act_hi[:, KW * i:KW * i + KW, :] for i in range(2)]
        y_lo = [act_lo[:, KW * i:KW * i + KW, :] for i in range(2)]
        slot = {br: i % 2 for i, br in enumerate(ORDER)}

        bank = [ctx.enter_context(nc.psum_tensor(f"bank{i}", [P, S], F32)) for i in range(4)]
        sc = [ctx.enter_context(nc.psum_tensor(f"sc{i}", [P, S], F32)) for i in range(2)]
        tp = ctx.enter_context(nc.psum_tensor("tp", [P, S], F32))
        ob = ctx.enter_context(nc.psum_tensor("ob", [P, S], F32))

        x2_dram = nc.dram_tensor("x2_dram", (S, D), F32, kind="Internal").ap()

        w_loaded = [sem(f"w_loaded{i}") for i in range(RING)]
        w_rounded, w_split, w_used = sem("w_rounded"), sem("w_split"), sem("w_used")
        bank_full = sem("bank_full")
        bank_free = [sem(f"bank_free{i}") for i in range(4)]
        x_loaded, gpre_loaded, gpost_loaded, const_loaded = sem("x_loaded"), sem("gpre_loaded"), sem("gpost_loaded"), sem("const_loaded")
        x2_spilled, aconst_loaded, out_stored = sem("x2_spilled"), sem("aconst_loaded"), sem("out_stored")
        masks_made, ident_made, tri_made = sem("masks_made"), sem("ident_made"), sem("tri_made")
        sumsq_done, var_done, rstd_done = sem("sumsq_done"), sem("var_done"), sem("rstd_done")
        scaled, x_updated, xn_done = sem("scaled"), sem("x_updated"), sem("xn_done")
        xpose_done, xT_rounded, xT_split = sem("xpose_done"), sem("xT_rounded"), sem("xT_split")
        bias_loaded = [sem(f"bias_loaded{i}") for i in range(4)]
        bias_ready = sem("bias_ready")
        sc_ready, sc_free, part_done, s_ready = sem("sc_ready"), sem("sc_free"), sem("part_done"), sem("s_ready")
        max_ready, p_ready, rinv_ready, pn_ready = sem("max_ready"), sem("p_ready"), sem("rinv_ready"), sem("pn_ready")
        tp_ready, pT_ready, pv_done = sem("tp_ready"), sem("pT_ready"), sem("pv_done")
        o_free, o_rounded = sem("o_free"), sem("o_rounded")
        olat_ready, ydsa_ready = sem("olat_ready"), sem("ydsa_ready")
        act_rounded, act_split = sem("act_rounded"), sem("act_split")
        c_copied, wi_ready, f_abs, f_exp, f_log, f_ls, lsx_ready = (sem(n) for n in ("c_copied", "wi_ready", "f_abs", "f_exp", "f_log", "f_ls", "lsx_ready"))
        c_ready, prep_ready, prep_free = sem("c_ready"), sem("prep_ready"), sem("prep_free")
        score_added, score_masked, topk_step = sem("score_added"), sem("score_masked"), sem("topk_step")
        y_ready, y_rounded, y_split = sem("y_ready"), sem("y_rounded"), sem("y_split")
        gate_add = sem("gate_add")
        merged_rounded, merged_split = sem("merged_rounded"), sem("merged_split")
        mean_ready, av_centred, ln_scaled, ln_done = (sem(n) for n in ("mean_ready", "av_centred", "ln_scaled", "ln_done"))
        mix_masked = sem("mix_masked")
        conv_step, conv_zero = sem("conv_step"), sem("conv_zero")
        out_ready = sem("out_ready")

        def freed(e):
            return bank_free[e % 4], e // 4 + 1

        def block_done(eng, b):
            what, count = DONE[b]
            eng.wait_ge(w_used if what == "w_used" else bank_full, count)

        stream = dram["weights"]
        pre_use = {"pre0": 0, "pre1": 1, "pre2": 2}

        block = ctx.enter_context(nc.Block())

        @block.sync
        def _(sp):
            def load(b):
                if b >= RING:
                    sp.wait_ge(w_split, b - RING + 1)
                sp.dma_start(w_raw[b % RING][:, :], stream[b, :, :]).then_inc(w_loaded[b % RING], 16)

            x_tok = dram["x"].rearrange("(t p) d -> p t d", p=P)
            sp.dma_start(x_sb[:, :, :], x_tok).then_inc(x_loaded, 16)
            sp.dma_start(g_pre[:, :], dram["g_pre_mix"].partition_broadcast(P)).then_inc(gpre_loaded, 16)
            consts = 0
            for b in range(N_BLOCKS):
                if b == 2:
                    sp.dma_start(g_post[:, :], dram["g_post_mix"].partition_broadcast(P)).then_inc(gpost_loaded, 16)
                    for dst, src in ((kvg[:, :], dram["kvg"].partition_broadcast(P)), (bf[:, :], dram["bf"].partition_broadcast(P)),
                                     (wukT[:, :, :], dram["wukT"]), (wuv[:, :, :], dram["wuv"]), (convw[:, :, :], dram["convw"])):
                        sp.dma_start(dst, src).then_inc(const_loaded, 16)
                        consts += 1
                if b == FIRST["k"]:
                    sp.wait_ge(xn_done, TT)
                    sp.dma_start(g_pre[:, :], dram["g_pre_ffn"].partition_broadcast(P)).then_inc(gpre_loaded, 16)
                if b == FIRST["wo1"]:
                    sp.wait_ge(pv_done, U_FOX)
                    sp.dma_start(x_sb[:, :, :], x_tok).then_inc(x_loaded, 16)
                if b == FIRST["gu0"] + 4:
                    sp.wait_ge(x_updated, TT)
                    sp.dma_start(g_post[:, :], dram["g_post_ffn"].partition_broadcast(P)).then_inc(gpost_loaded, 16)
                    sp.wait_ge(xn_done, 2 * TT)
                    sp.dma_start(g_pre[:, :], dram["norm_g"].partition_broadcast(P)).then_inc(gpre_loaded, 16)
                if b == FIRST["qi"] + 4:
                    sp.wait_ge(x_updated, 2 * TT)
                    sp.dma_start(x2_dram.rearrange("(t p) d -> p t d", p=P), x_sb[:, :, :]).then_inc(x2_spilled, 16)
                    sp.dma_start(g_post[:, 0:W], dram["ln_g"].partition_broadcast(P)).then_inc(gpost_loaded, 16)
                    sp.dma_start(g_post[:, W:2 * W], dram["ln_b"].partition_broadcast(P)).then_inc(gpost_loaded, 16)
                if b == FIRST["a_v"]:
                    sp.wait_ge(pv_done, N_UNITS)
                    sp.dma_start(a_bs, dram["gm_b"].partition_broadcast(P)).then_inc(aconst_loaded, 16)
                    sp.dma_start(a_ws, dram["gm_wT"]).then_inc(aconst_loaded, 16)
                if b == FIRST["gate_c0"]:
                    sp.wait_ge(ln_done, TT)
                    sp.dma_start(g_post[:, :], dram["final_g"].partition_broadcast(P)).then_inc(gpost_loaded, 16)
                if b == N_BLOCKS - 2:
                    sp.wait_ge(merged_split, KD)
                    sp.wait_ge(x2_spilled, 16)
                    sp.dma_start(x_sb[:, :, :], x2_dram.rearrange("(t p) d -> p t d", p=P)).then_inc(x_loaded, 16)
                load(b)
            out_tok = out.rearrange("(t p) d -> p t d", p=P)
            for t in range(TT):
                sp.wait_ge(out_ready, t + 1)
                sp.dma_start(out_tok[:, t, :], m_sb[:, t, :]).then_inc(out_stored, 16)
            sp.wait_ge(out_stored, 16 * TT)

        @block.gpsimd
        def _(pool):
            nc.gpsimd.memset(minus_half[:, :], -0.5).then_inc(masks_made, 1)
            nc.gpsimd.memset(ident[:, :], 0.0).then_inc(ident_made, 1)
            nc.gpsimd.memset(cmask[:, :], 0.0).then_inc(masks_made, 1)
            pool.wait_ge(ident_made, 1)
            nc.gpsimd.affine_select(out=ident[:, :], in_=ident[:, :], compare_op=ALU.not_equal, fill=1.0, base=0,
                                    pattern=[[-1, P]], channel_multiplier=1).then_inc(ident_made, 1)
            pool.wait_ge(masks_made, 2)
            nc.gpsimd.affine_select(out=cmask[:, :], in_=cmask[:, :], compare_op=ALU.is_ge, fill=NEG, base=0,
                                    pattern=[[-1, P]], channel_multiplier=1).then_inc(masks_made, 1)

            def reciprocal_roots(names):
                for name in names:
                    for n in [i for i, (what, _) in enumerate(NORMS) if what in name]:
                        pool.wait_ge(var_done, n + 1)
                        nc.gpsimd.tensor_tensor(rstd[:, n:n + 1], var[:, n:n + 1], minus_half[:, :], ALU.pow).then_inc(rstd_done, 1)

            reciprocal_roots([("pre0",)])
            for h in range(HEADS):
                pool.wait_ge(bias_loaded[h % 4], 16 * (h // 4 + 1))
                nc.gpsimd.memset(biases[0:CHUNK, h % 4, BIAS_W - CHUNK:BIAS_W], NEG).then_inc(bias_ready, 1)
            reciprocal_roots([("post1", "pre1"), ("post2", "pre2")])
            pool.wait_ge(pv_done, U_FOX)
            nc.gpsimd.memset(tri, 1.0).then_inc(tri_made, 1)
            pool.wait_ge(tri_made, 1)
            nc.gpsimd.affine_select(out=tri[:, 0:P], in_=tri[:, 0:P], compare_op=ALU.is_ge, fill=0.0, base=0,
                                    pattern=[[1, P]], channel_multiplier=-1).then_inc(tri_made, 1)
            reciprocal_roots([("c",)])
            for t in range(1, TT):
                pool.wait_ge(score_added, IDX_H * t)
                nc.gpsimd.affine_select(out=sel[t][:, P * t:P * (t + 1)], in_=sel[t][:, P * t:P * (t + 1)], compare_op=ALU.is_ge,
                                        fill=ACAUSAL, base=0, pattern=[[-1, P]], channel_multiplier=1).then_inc(score_masked, 1)
            pool.wait_ge(aconst_loaded, 32)
            nc.gpsimd.affine_select(out=a_ws, in_=a_ws, compare_op=ALU.is_ge, fill=0.0, base=0, pattern=[[0, KW], [1, P]],
                                    channel_multiplier=-1).then_inc(mix_masked, 1)
            reciprocal_roots([("ln",), ("final",)])

        @block.scalar
        def _(act):
            def split(b):
                if b >= N_BLOCKS:
                    return
                act.wait_ge(w_loaded[b % RING], 16 * (b // RING + 1))
                if b >= RING:
                    block_done(act, b - RING)
                nc.scalar.activation(w_hi[b % RING][:, :], w_raw[b % RING][:, :], ACT.Copy).then_inc(w_rounded, 1)

            def read_out(dst, e, func=ACT.Copy, src=None):
                act.wait_ge(bank_full, e + 1)
                nc.scalar.activation(dst, bank[e % 4][:, :] if src is None else src, func).then_inc(bank_free[e % 4], 1)

            def sum_squares(name, t):
                n = NCOL[name, t]
                if name == "pre0":
                    act.wait_ge(x_loaded, 16)
                    src = x_sb[:, t, :]
                elif name in ("post1", "post2", "final"):
                    key = {"post1": "wo", "post2": "down1", "final": "out"}[name]
                    if name == "final":
                        for h in range(2):
                            act.wait_ge(*freed(USE[f"out{h}"] + t))
                        src = x_sb[:, t, :]
                    else:
                        for h in range(2):
                            act.wait_ge(*freed(USE[f"{key}{h}"] + t))
                        src = m_sb[:, t, :]
                else:
                    act.wait_ge(x_updated, TT * (pre_use[name] - 1) + t + 1)
                    src = x_sb[:, t, :]
                if n:
                    act.wait_ge(sumsq_done, n)
                nc.scalar.activation(junk, src, ACT.Square, accum_out=sumsq[:, n:n + 1]).then_inc(sumsq_done, 1)

            def round_xT(name, t):
                for j in range(2):
                    q = 2 * (TT * pre_use[name] + t) + j
                    act.wait_ge(xpose_done, q + 1)
                    nc.scalar.activation(xT_hi[:, 4 * j:4 * j + 4, P * t:P * t + P], sc[q % 2][:, :].rearrange("p (c s) -> p c s", s=P),
                                         ACT.Copy).then_inc(xT_rounded, 1)

            def norms(names):
                seq = [n for n in NORMS if n[0] in names]
                for i in range(len(seq) + 2):
                    if i < len(seq):
                        sum_squares(*seq[i])
                    if i >= 2 and seq[i - 2][0] in pre_use:
                        round_xT(*seq[i - 2])

            def attention(lo, hi, o_done):
                for i in range(lo, hi + 5):
                    if i < hi:
                        kind, h, t = UNITS[i]
                        nk = P * (t + 1)
                        if kind == "mha" and h % 1 == 0 and t == 0:
                            bias_load(h + 2)
                        if kind == "fox" or (kind == "mha" and t >= 2):
                            act.wait_ge(sc_ready, i + 1)
                            if i >= 4:
                                act.wait_ge(tp_ready, i - 3)
                        if kind == "mha" and t >= 2:
                            act.wait_ge(bias_ready, h + 1)
                            nc.scalar.activation(s_ring[:, i % 4, 0:nk - BIAS_W], sc[i % 2][:, 0:nk - BIAS_W], ACT.Identity,
                                                 bias=biases[:, h % 4, 0:1], scale=HD ** -0.5).then_inc(part_done, 1)
                        if kind == "fox":
                            nc.scalar.activation(s_ring[:, i % 4, 0:nk], sc[i % 2][:, 0:nk], ACT.Identity,
                                                 bias=cumq[:, t, h:h + 1], scale=BD ** -0.5).then_inc(sc_free, 1)
                    if lo <= i - 1 < hi:
                        u = i - 1
                        nk = P * (UNITS[u][2] + 1)
                        act.wait_ge(max_ready, u + 1)
                        if u >= 4:
                            act.wait_ge(rinv_ready, u - 3)
                        nc.scalar.activation(s_ring[:, u % 4, 0:nk], s_ring[:, u % 4, 0:nk], ACT.Exp, bias=negmax[:, u % 4:u % 4 + 1],
                                             accum_out=psums[:, u % 4:u % 4 + 1]).then_inc(p_ready, 1)
                    if lo <= i - 2 < hi:
                        u = i - 2
                        nk = P * (UNITS[u][2] + 1)
                        act.wait_ge(tp_ready, u + 1)
                        if u >= 2:
                            act.wait_ge(pv_done, u - 1)
                        nc.scalar.activation(pT[:, u % 2, 0:nk], tp[:, 0:nk], ACT.Copy).then_inc(pT_ready, 1)
                    if lo <= i - 4 < hi:
                        o_done(i - 4)

            def bias_load(h):
                if h < HEADS:
                    if h >= 4:
                        act.wait_ge(s_ready, TT * (h - 3))
                        act.wait_ge(part_done, 2 * (h - 3))
                    act.dma_start(biases[:, h % 4, :], dram["bias"][h, :, :]).then_inc(bias_loaded[h % 4], 16)

            bias_done = False
            seq = [n for n in NORMS if n[0] == "pre0"]
            for name in seq:
                sum_squares(*name)
            split(0)
            split(1)
            for name in seq:
                round_xT(*name)
            for b in range(8):
                for c in range(2):
                    read_out(qkT[:, 2 * b + c, :], 2 * b + c)
                split(b + 2)
            for h in range(2):
                b = FIRST[f"v{h}"]
                split(b + 2)
                for t in range(TT):
                    read_out(v_sb[:, t, W * h:W * h + W], USE[f"v{h}"] + t)
                split(b + 3)

            def pair_out(u):
                if u % (2 * TT) == 2 * TT - 1:
                    act.wait_ge(pv_done, u + 1)
                    nc.scalar.activation(xT_hi[:, u // (2 * TT), :], ob[:, :], ACT.Copy).then_inc(o_rounded, 1)

            bias_load(0)
            bias_load(1)
            attention(0, U_FOX, pair_out)

            for h in range(2):
                b = FIRST[f"wo{h}"]
                split(b + 2)
                for t in range(TT):
                    read_out(m_sb[:, t, W * h:W * h + W], USE[f"wo{h}"] + t)
                split(b + 3)
            norms(("post1", "pre1"))

            for f in range(2):
                for i in range(FH):
                    n = FH * f + i
                    b, e = FIRST[f"gu{f}"] + i, USE[f"gu{f}"] + 2 * i
                    if n >= 2:
                        act.wait_ge(act_split, n - 1)
                    read_out(sg[:, n % 2, :], e, ACT.Silu)
                    act.wait_ge(*freed(e + 1))
                    nc.scalar.activation(act_hi[:, i, :], a_sb[:, n % 2, :], ACT.Copy).then_inc(act_rounded, 1)
                    split(b + 2)
                for h in range(2):
                    b = FIRST[f"down{f}{h}"]
                    split(b + 2)
                    split(b + 3)
                    if f == 0:
                        for t in range(TT):
                            read_out(m_sb[:, t, W * h:W * h + W], USE[f"down{f}{h}"] + t)
                    split(b + 4)
            norms(("post2", "pre2"))

            for c in range(2):
                read_out(qi[:, c, :], USE["qi"] + c)
            split(FIRST["qi"] + 2)
            read_out(ki, USE["ki"])
            split(FIRST["ki"] + 2)
            for t in range(TT):
                e = USE["cwf"] + t
                act.wait_ge(bank_full, e + 1)
                nc.scalar.activation(c_raw[:, t, :], bank[e % 4][:, 0:P], ACT.Copy).then_inc(c_copied, 1)
            split(FIRST["cwf"] + 2)
            for t in range(TT):
                n = NCOL["c", t]
                act.wait_ge(c_copied, t + 1)
                nc.scalar.activation(a_junk[:, t, 0:P], c_raw[:, t, :], ACT.Square, accum_out=sumsq[:, n:n + 1]).then_inc(sumsq_done, 1)
            act.wait_ge(f_abs, 1)
            nc.scalar.activation(fl[:, :, :], fna[:, :, :], ACT.Exp).then_inc(f_exp, 1)
            act.wait_ge(f_exp, 1)
            nc.scalar.activation(fl[:, :, :], fl[:, :, :], ACT.Ln, bias=1.0).then_inc(f_log, 1)
            for i in range(2):
                for c in range(2):
                    read_out(bq[:, 2 * i + c, :], USE["b_q"] + 2 * i + c)
                split(FIRST["b_q"] + i + 2)
            prep = 0

            def prep_out(dst, func, src, scale=1.0):
                nonlocal prep
                act.wait_ge(prep_ready, prep + 1)
                nc.scalar.activation(dst, src(sc[prep % 2]), func, scale=scale).then_inc(prep_free, 1)
                prep += 1

            prep_out(cT, ACT.Copy, lambda z: z[:, :])
            for t in range(1, TT):
                for h in range(IDX_H):
                    j = IDX_H * (t - 1) + h
                    if j >= 2:
                        act.wait_ge(score_added, j - 1)
                    prep_out(relu_d[:, j % 2, 0:P * (t + 1)], ACT.Relu, lambda z: z[:, 0:P * (t + 1)], IDX_D ** -0.5)
            for h in range(BH):
                prep_out(negcumk[:, h, :], ACT.Copy, lambda z: z[:, :], -1.0)
            prep_out(cumq[:, :, :], ACT.Copy, lambda z: z[:, 0:TT * BH].rearrange("p (t h) -> p t h", h=BH))
            for h in range(BH):
                prep_out(qlat[:, h, :], ACT.Copy, lambda z: z[:, :])
            act.wait_ge(x2_spilled, 16)
            for key, base in (("d_q", 0), ("d_k", 4)):
                for i in range(2):
                    for c in range(2):
                        read_out(dqk[:, base + 2 * i + c, :], USE[key] + 2 * i + c)
                    split(FIRST[key] + i + 2)
            split(FIRST["d_v"] + 2)
            for t in range(TT):
                read_out(dv[:, t, :], USE["d_v"] + t)
            split(FIRST["d_v"] + 3)
            for i in range(2):
                for c in range(2):
                    read_out(sz[:, 2 * i + c, :], USE["d_z"] + 2 * i + c, ACT.Silu)
                split(FIRST["d_z"] + i + 2)

            n_y = {br: 4 * i for i, br in enumerate(ORDER)}

            def round_y(br, j, src):
                ready = {"d": (o_free, HEADS // 2), "b": (o_free, HEADS // 2 + BH), "a": (y_ready, 0), "c": (y_ready, KW)}
                act.wait_ge(ready[br][0], ready[br][1] + j + 1)
                nc.scalar.activation(y_hi[slot[br]][:, j, :], src, ACT.Copy).then_inc(y_rounded, 1)

            def fox_out(u):
                if u % TT == TT - 1:
                    h = (u - U_FOX) // TT
                    round_y("d", h, sz[:, h, :])

            attention(U_FOX, U_DSA, fox_out)

            def gates(br):
                r = ORDER.index(br)
                for half in range(2):
                    b, e = FIRST[f"gate_{br}{half}"], USE[f"gate_{br}{half}"]
                    for i in range(2):
                        for c in range(2):
                            if half or r:
                                last = f"branch_{br}0" if half else f"branch_{ORDER[r - 1]}1"
                                act.wait_ge(*freed(USE[last] + 2 * i + c))
                            read_out(sig[:, 2 * i + c, :], e + 2 * i + c, ACT.Sigmoid)
                        split(b + i + 2)
                    split(FIRST[f"branch_{br}{half}"] + 2)

            gates("d")
            for i in range(2):
                for c in range(2):
                    read_out(sz[:, 2 * i + c, :], USE["b_z"] + 2 * i + c, ACT.Silu)
                split(FIRST["b_z"] + i + 2)

            def dsa_out(u):
                if u % TT == TT - 1:
                    h = (u - U_DSA) // TT
                    act.wait_ge(pv_done, u + 1)
                    if h >= 1:
                        act.wait_ge(ydsa_ready, h)
                    nc.scalar.activation(tmp_olat, ob[:, :], ACT.Copy).then_inc(olat_ready, 1)
                    round_y("b", h, sz[:, h, :])

            tmp_olat = negcumk[:, 0, :]
            attention(U_DSA, N_UNITS, dsa_out)
            gates("b")
            split(FIRST["a_v"] + 2)
            for t in range(TT):
                e = USE["a_v"] + t
                act.wait_ge(bank_full, e + 1)
                nc.scalar.activation(av[:, t, :], bank[e % 4][:, :], ACT.Copy, accum_out=mean[:, t:t + 1]).then_inc(bank_free[e % 4], 1)
            split(FIRST["a_v"] + 3)
            for t in range(TT):
                n = NCOL["ln", t]
                act.wait_ge(av_centred, t + 1)
                nc.scalar.activation(a_junk[:, t, :], av[:, t, :], ACT.Square, accum_out=sumsq[:, n:n + 1]).then_inc(sumsq_done, 1)
            for j in range(KW):
                e = USE["a_uz"] + 2 * j
                if j >= 2:
                    act.wait_ge(y_split, n_y["a"] + j - 1)
                read_out(a_sz[:, j % 2, :], e + 1, ACT.Silu)
                round_y("a", j, a_y[:, j % 2, :])
                split(FIRST["a_uz"] + j + 2)
            gates("a")
            for j in range(KW):
                e = USE["c"] + 4 * j
                if j >= 2:
                    act.wait_ge(y_split, n_y["c"] + j - 1)
                read_out(c_cc[:, j % 2, :], e)
                split(FIRST["c"] + 2 * j + 2)
                read_out(c_sz[:, j % 2, :], e + 3, ACT.Silu)
                round_y("c", j, c_o[:, j % 2, :])
                split(FIRST["c"] + 2 * j + 3)
            gates("c")
            for j in range(KD):
                act.wait_ge(gate_add, KD * (N_BRANCH - 2) + j + 1)
                if j == 0:
                    block_done(act, FIRST["branch_c1"])
                nc.scalar.activation(xT_hi[:, j, :], merged[:, j, :], ACT.Copy).then_inc(merged_rounded, 1)
            for h in range(2):
                split(FIRST[f"out{h}"] + 2)
                split(FIRST[f"out{h}"] + 3)
            for t in range(TT):
                sum_squares("final", t)

        @block.vector
        def _(dve):
            def split(b):
                if b >= N_BLOCKS:
                    return
                dve.wait_ge(w_rounded, b + 1)
                nc.vector.tensor_tensor(w_lo[b % RING][:, :], w_raw[b % RING][:, :], w_hi[b % RING][:, :].bitcast(F32),
                                        ALU.subtract).then_inc(w_split, 1)

            def variance(name, t, width):
                n = NCOL[name, t]
                dve.wait_ge(sumsq_done, n + 1)
                nc.vector.tensor_scalar(var[:, n:n + 1], sumsq[:, n:n + 1], 1.0 / width, EPS, ALU.mult, ALU.add).then_inc(var_done, 1)

            def scale_rows(out_, in_, name, t, gains):
                n = NCOL[name, t]
                dve.wait_ge(rstd_done, n + 1)
                return nc.vector.scalar_tensor_tensor(out=out_, in0=in_, scalar=rstd[:, n:n + 1], in1=gains, op0=ALU.mult, op1=ALU.mult)

            def apply_norm(name, t):
                if name in pre_use:
                    use = pre_use[name]
                    dve.wait_ge(gpre_loaded, 16 * (use + 1))
                    q = TT * use + t
                    if q >= 2:
                        dve.wait_ge(xpose_done, 2 * (q - 1))
                    scale_rows(xn[:, t % 2, :], x_sb[:, t, :], name, t, g_pre[:, :]).then_inc(xn_done, 1)
                else:
                    r = {"post1": 0, "post2": 1}[name]
                    dve.wait_ge(gpost_loaded, 16 * (r + 1))
                    dve.wait_ge(x_loaded, 32)
                    scale_rows(m_sb[:, t, :], m_sb[:, t, :], name, t, g_post[:, :]).then_inc(scaled, 1)
                    dve.wait_ge(scaled, TT * r + t + 1)
                    nc.vector.tensor_tensor(x_sb[:, t, :], x_sb[:, t, :], m_sb[:, t, :], ALU.add).then_inc(x_updated, 1)

            def split_xT(name, t):
                for j in range(2):
                    q = 2 * (TT * pre_use[name] + t) + j
                    dve.wait_ge(xT_rounded, q + 1)
                    part = (slice(None), slice(4 * j, 4 * j + 4), slice(P * t, P * t + P))
                    nc.vector.tensor_tensor(xT_lo[part], sc[q % 2][:, :].rearrange("p (c s) -> p c s", s=P), xT_hi[part].bitcast(F32),
                                            ALU.subtract).then_inc(xT_split, 1)

            def norms(names):
                seq = [n for n in NORMS if n[0] in names]
                for i in range(len(seq) + 3):
                    if i < len(seq):
                        variance(*seq[i], D)
                    if 1 <= i <= len(seq):
                        apply_norm(*seq[i - 1])
                    if i >= 3 and seq[i - 3][0] in pre_use:
                        split_xT(*seq[i - 3])

            def attention(lo, hi, o_done):
                for i in range(lo, hi + 5):
                    if i < hi:
                        kind, h, t = UNITS[i]
                        nk = P * (t + 1)
                        s = s_ring[:, i % 4, 0:nk]
                        if kind == "fox":
                            dve.wait_ge(sc_free, i - U_FOX + 1)
                            ins = nc.vector.tensor_tensor(s, s, negcumk[:, h, 0:nk], ALU.add)
                            ins.then_inc(part_done, 1)
                            dve.wait_ge(part_done, HEADS * 2 + i - U_FOX + 1)
                            nc.vector.tensor_tensor(s[:, nk - P:nk], s[:, nk - P:nk], cmask[:, :], ALU.add).then_inc(s_ready, 1)
                        else:
                            dve.wait_ge(sc_ready, i + 1)
                            if i >= 4:
                                dve.wait_ge(tp_ready, i - 3)
                        if kind == "mha":
                            w = min(nk, BIAS_W)
                            dve.wait_ge(bias_ready, h + 1)
                            if t >= 2:
                                dve.wait_ge(part_done, 2 * h + t - 1)
                            nc.vector.scalar_tensor_tensor(out=s[:, nk - w:nk], in0=sc[i % 2][:, nk - w:nk], scalar=HD ** -0.5,
                                                           in1=biases[:, h % 4, BIAS_W - w:BIAS_W], op0=ALU.mult,
                                                           op1=ALU.add).then_inc(s_ready, 1)
                        if kind == "dsa":
                            nc.vector.scalar_tensor_tensor(out=s, in0=sc[i % 2][:, 0:nk], scalar=BD ** -0.5,
                                                           in1=cmask[:, :] if t == 0 else sel[t], op0=ALU.mult,
                                                           op1=ALU.add).then_inc(s_ready, 1)
                        dve.wait_ge(s_ready, i + 1)
                        if i >= 4:
                            dve.wait_ge(p_ready, i - 3)
                        nc.vector.reduce_max(negmax[:, i % 4:i % 4 + 1], s, AX_X, negate=True).then_inc(max_ready, 1)
                    if lo <= i - 1 < hi:
                        u = i - 1
                        nk = P * (UNITS[u][2] + 1)
                        dve.wait_ge(p_ready, u + 1)
                        nc.vector.reciprocal(rinv[:, u % 4:u % 4 + 1], psums[:, u % 4:u % 4 + 1]).then_inc(rinv_ready, 1)
                        dve.wait_ge(rinv_ready, u + 1)
                        nc.vector.tensor_scalar(s_ring[:, u % 4, 0:nk], s_ring[:, u % 4, 0:nk], rinv[:, u % 4:u % 4 + 1], None,
                                                ALU.mult).then_inc(pn_ready, 1)
                    if lo <= i - 4 < hi:
                        o_done(i - 4)

            norms(("pre0",))
            for b in range(FIRST["wo0"] + 2):
                split(b)

            def pair_out(u):
                if u % (2 * TT) == 2 * TT - 1:
                    hp = u // (2 * TT)
                    dve.wait_ge(o_rounded, hp + 1)
                    nc.vector.tensor_tensor(xT_lo[:, hp, :], ob[:, :], xT_hi[:, hp, :].bitcast(F32), ALU.subtract).then_inc(o_free, 1)

            attention(0, U_FOX, pair_out)
            for b in range(FIRST["wo0"] + 2, FIRST["gu0"] + 2):
                split(b)
            norms(("post1", "pre1"))

            for f in range(2):
                for i in range(FH):
                    n = FH * f + i
                    e = USE[f"gu{f}"] + 2 * i
                    dve.wait_ge(*freed(e))
                    dve.wait_ge(bank_full, e + 2)
                    nc.vector.tensor_tensor(a_sb[:, n % 2, :], sg[:, n % 2, :], bank[(e + 1) % 4][:, :], ALU.mult).then_inc(bank_free[(e + 1) % 4], 1)
                    dve.wait_ge(act_rounded, n + 1)
                    nc.vector.tensor_tensor(act_lo[:, i, :], a_sb[:, n % 2, :], act_hi[:, i, :].bitcast(F32), ALU.subtract).then_inc(act_split, 1)
                    split(FIRST[f"gu{f}"] + i + 2)
                for h in range(2):
                    b, e = FIRST[f"down{f}{h}"], USE[f"down{f}{h}"]
                    split(b + 2)
                    split(b + 3)
                    if f == 1:
                        for t in range(TT):
                            dve.wait_ge(*freed(USE[f"down0{h}"] + t))
                            dve.wait_ge(bank_full, e + t + 1)
                            part = m_sb[:, t, W * h:W * h + W]
                            nc.vector.tensor_tensor(part, part, bank[(e + t) % 4][:, :], ALU.add).then_inc(bank_free[(e + t) % 4], 1)
                    split(b + 4)
            norms(("post2", "pre2"))

            split(FIRST["qi"] + 2)
            split(FIRST["ki"] + 2)
            dve.wait_ge(const_loaded, 16 * 5)
            for t in range(TT):
                e = USE["cwf"] + t
                dve.wait_ge(c_copied, t + 1)
                nc.vector.tensor_scalar(wi[:, t, :], bank[e % 4][:, P:P + IDX_H], IDX_H ** -0.5, None, ALU.mult).then_inc(wi_ready, 1)
                nc.vector.tensor_tensor(fb[:, t, :], bank[e % 4][:, P + IDX_H:P + IDX_H + BH], bf[:, :], ALU.add)\
                    .then_inc(bank_free[e % 4], 1)
            split(FIRST["cwf"] + 2)
            for t in range(TT):
                dve.wait_ge(*freed(USE["cwf"] + t))
            nc.vector.scalar_tensor_tensor(out=fna[:, :, :], in0=fb[:, :, :], scalar=-1.0, in1=fb[:, :, :], op0=ALU.mult, op1=ALU.min).then_inc(f_abs, 1)
            for t in range(TT):
                variance("c", t, P)
            for t in range(TT):
                scale_rows(c_sb[:, t, :], c_raw[:, t, :], "c", t, kvg[:, :]).then_inc(c_ready, 1)
            dve.wait_ge(f_log, 1)
            nc.vector.scalar_tensor_tensor(out=ls[:, :, :], in0=fb[:, :, :], scalar=0.0, in1=fl[:, :, :], op0=ALU.min, op1=ALU.subtract).then_inc(f_ls, 1)
            split(FIRST["b_q"] + 2)
            split(FIRST["b_q"] + 3)
            dve.wait_ge(wi_ready, TT)
            for t in range(1, TT):
                for h in range(IDX_H):
                    j = IDX_H * (t - 1) + h
                    dve.wait_ge(prep_free, 1 + j + 1)
                    r = relu_d[:, j % 2, 0:P * (t + 1)]
                    if h == 0:
                        ins = nc.vector.tensor_scalar(sel[t], r, wi[:, t, h:h + 1], None, ALU.mult)
                    else:
                        dve.wait_ge(score_added, j)
                        ins = nc.vector.scalar_tensor_tensor(out=sel[t], in0=r, scalar=wi[:, t, h:h + 1], in1=sel[t], op0=ALU.mult, op1=ALU.add)
                    ins.then_inc(score_added, 1)
            dve.wait_ge(f_ls, 1)
            dve.wait_ge(score_added, IDX_H * (TT - 1))
            for h in range(BH):
                nc.vector.tensor_copy(lsx[:, h, :, :], ls[:, :, h:h + 1].broadcast_to([P, TT, P])).then_inc(lsx_ready, 1)

            def selection():
                n = 0
                for t in range(1, TT):
                    dve.wait_ge(score_masked, t)
                    for r in range(TOPK // 8):
                        nc.vector.max(top8[:, :], sel[t]).then_inc(topk_step, 1)
                        n += 1
                        dve.wait_ge(topk_step, n)
                        nc.vector.match_replace(sel[t], top8[:, :], sel[t], TAKEN).then_inc(topk_step, 1)
                        n += 1
                        dve.wait_ge(topk_step, n)
                        if r == TOPK // 8 - 1:
                            nc.vector.tensor_scalar(sel[t], sel[t], TAKEN, NEG, ALU.not_equal, ALU.mult).then_inc(topk_step, 1)
                            n += 1
                            dve.wait_ge(topk_step, n)
                        yield

            rounds = selection()

            def select_some(n):
                for _ in range(n):
                    next(rounds, None)

            for b in range(FIRST["d_q"], FIRST["d_z"] + 2):
                split(b + 2)
                select_some(3)

            n_y = {br: 4 * i for i, br in enumerate(ORDER)}

            def split_y(br, j, src):
                dve.wait_ge(y_rounded, n_y[br] + j + 1)
                nc.vector.tensor_tensor(y_lo[slot[br]][:, j, :], src, y_hi[slot[br]][:, j, :].bitcast(F32), ALU.subtract).then_inc(y_split, 1)

            def fox_out(u):
                if u % TT == TT - 1:
                    h = (u - U_FOX) // TT
                    dve.wait_ge(pv_done, u + 1)
                    if h == 0:
                        for c in range(KW):
                            dve.wait_ge(*freed(USE["d_z"] + c))
                    nc.vector.tensor_tensor(sz[:, h, :], ob[:, :], sz[:, h, :], ALU.mult).then_inc(o_free, 1)
                    split_y("d", h, sz[:, h, :])

            attention(U_FOX, U_DSA, fox_out)

            def gates(br, rounds_per_block=0):
                r = ORDER.index(br)
                for half in range(2):
                    for i in range(2):
                        split(FIRST[f"gate_{br}{half}"] + i + 2)
                        select_some(rounds_per_block)
                    e = USE[f"branch_{br}{half}"]
                    for c in range(4):
                        j = 4 * half + c
                        dve.wait_ge(*freed(USE[f"gate_{br}{half}"] + c))
                        dve.wait_ge(bank_full, e + c + 1)
                        dst = merged[:, j, :] if r == 0 else tmp[:, c % 2, :]
                        nc.vector.tensor_tensor(dst, sig[:, c, :], bank[(e + c) % 4][:, :], ALU.mult).then_inc(bank_free[(e + c) % 4], 1)
                        dve.wait_ge(*freed(e + c))
                        if r:
                            nc.vector.tensor_tensor(merged[:, j, :], merged[:, j, :], tmp[:, c % 2, :], ALU.add).then_inc(gate_add, 1)
                    split(FIRST[f"branch_{br}{half}"] + 2)
                    select_some(rounds_per_block)

            gates("d", 3)
            for i in range(2):
                split(FIRST["b_z"] + i + 2)
                select_some(3)
            select_some(100)

            def dsa_out(u):
                if u % TT == TT - 1:
                    h = (u - U_DSA) // TT
                    dve.wait_ge(ydsa_ready, h + 1)
                    if h == 0:
                        for c in range(KW):
                            dve.wait_ge(*freed(USE["b_z"] + c))
                    nc.vector.tensor_tensor(sz[:, h, :], ob[:, :], sz[:, h, :], ALU.mult).then_inc(o_free, 1)
                    split_y("b", h, sz[:, h, :])

            attention(U_DSA, N_UNITS, dsa_out)
            gates("b")
            split(FIRST["a_v"] + 2)
            split(FIRST["a_v"] + 3)
            for t in range(TT):
                dve.wait_ge(*freed(USE["a_v"] + t))
                nc.vector.tensor_scalar(mean[:, t:t + 1], mean[:, t:t + 1], 1.0 / W, None, ALU.mult).then_inc(mean_ready, 1)
                dve.wait_ge(mean_ready, t + 1)
                nc.vector.tensor_scalar(av[:, t, :], av[:, t, :], mean[:, t:t + 1], None, ALU.subtract).then_inc(av_centred, 1)
            for t in range(TT):
                variance("ln", t, W)
            dve.wait_ge(gpost_loaded, 16 * 4)
            for t in range(TT):
                scale_rows(av[:, t, :], av[:, t, :], "ln", t, g_post[:, 0:W]).then_inc(ln_scaled, 1)
                dve.wait_ge(ln_scaled, t + 1)
                nc.vector.tensor_tensor(av[:, t, :], av[:, t, :], g_post[:, W:2 * W], ALU.add).then_inc(ln_done, 1)
            dve.wait_ge(aconst_loaded, 32)
            n_prep = 1 + IDX_H * (TT - 1) + BH + 1 + BH
            for g in range(KW):
                dve.wait_ge(prep_ready, n_prep + g + 1)
                nc.vector.tensor_tensor(a_mix[:, g, :].rearrange("p (c t) -> p c t", t=P),
                                        sc[(n_prep + g) % 2][:, :].rearrange("p (c t) -> p c t", t=P),
                                        a_bs[:, g:g + 1, :].broadcast_to([P, TT, P]), ALU.add).then_inc(prep_free, 1)
            for j in range(KW):
                e = USE["a_uz"] + 2 * j
                dve.wait_ge(prep_free, n_prep + j + 1)
                dve.wait_ge(bank_full, e + 1)
                nc.vector.tensor_tensor(a_mix[:, j, :], a_mix[:, j, :], bank[e % 4][:, :], ALU.mult).then_inc(bank_free[e % 4], 1)
                dve.wait_ge(*freed(e))
                dve.wait_ge(*freed(e + 1))
                nc.vector.tensor_tensor(a_y[:, j % 2, :], a_mix[:, j, :], a_sz[:, j % 2, :], ALU.mult).then_inc(y_ready, 1)
                split_y("a", j, a_y[:, j % 2, :])
                split(FIRST["a_uz"] + j + 2)
            gates("a")
            for i in range(2):
                nc.vector.memset(c_y[:, i, 0:2], 0.0).then_inc(conv_zero, 1)
            dve.wait_ge(conv_zero, 2)
            for j in range(KW):
                e = USE["c"] + 4 * j
                y = c_y[:, j % 2, :]
                acc = c_acc[:, j % 2, :]
                dve.wait_ge(*freed(e))
                dve.wait_ge(bank_full, e + 2)
                nc.vector.tensor_tensor(y[:, 2:2 + S], c_cc[:, j % 2, :], bank[(e + 1) % 4][:, :], ALU.mult).then_inc(bank_free[(e + 1) % 4], 1)
                dve.wait_ge(*freed(e + 1))
                nc.vector.tensor_scalar(acc, y[:, 0:S], convw[:, j, 0:1], None, ALU.mult).then_inc(conv_step, 1)
                for i in (1, 2):
                    dve.wait_ge(conv_step, 3 * j + i)
                    nc.vector.scalar_tensor_tensor(out=acc, in0=y[:, i:i + S], scalar=convw[:, j, i:i + 1], in1=acc, op0=ALU.mult,
                                                   op1=ALU.add).then_inc(conv_step, 1)
                split(FIRST["c"] + 2 * j + 2)
                dve.wait_ge(conv_step, 3 * j + 3)
                dve.wait_ge(bank_full, e + 3)
                nc.vector.tensor_tensor(acc, acc, bank[(e + 2) % 4][:, :], ALU.mult).then_inc(bank_free[(e + 2) % 4], 1)
                dve.wait_ge(*freed(e + 2))
                dve.wait_ge(*freed(e + 3))
                nc.vector.tensor_tensor(c_o[:, j % 2, :], acc, c_sz[:, j % 2, :], ALU.mult).then_inc(y_ready, 1)
                split_y("c", j, c_o[:, j % 2, :])
                split(FIRST["c"] + 2 * j + 3)
            gates("c")
            for j in range(KD):
                dve.wait_ge(merged_rounded, j + 1)
                nc.vector.tensor_tensor(xT_lo[:, j, :], merged[:, j, :], xT_hi[:, j, :].bitcast(F32), ALU.subtract).then_inc(merged_split, 1)
            dve.wait_ge(x_loaded, 48)
            for h in range(2):
                split(FIRST[f"out{h}"] + 2)
                split(FIRST[f"out{h}"] + 3)
                for t in range(TT):
                    e = USE[f"out{h}"] + t
                    dve.wait_ge(bank_full, e + 1)
                    part = x_sb[:, t, W * h:W * h + W]
                    nc.vector.tensor_tensor(part, part, bank[e % 4][:, :], ALU.add).then_inc(bank_free[e % 4], 1)
            dve.wait_ge(gpost_loaded, 16 * 5)
            for i in range(TT + 1):
                if i < TT:
                    variance("final", i, D)
                if i >= 1:
                    scale_rows(m_sb[:, i - 1, :], x_sb[:, i - 1, :], "final", i - 1, g_post[:, :]).then_inc(out_ready, 1)

        @block.tensor
        def _(pe):
            def product(ps, hi_l, lo_l, hi_r, lo_r, first, last):
                nc.tensor.matmul(ps, hi_l, hi_r, start=first, stop=False)
                nc.tensor.matmul(ps, hi_l, lo_r, start=False, stop=False)
                return nc.tensor.matmul(ps, lo_l, hi_r, start=False, stop=last)

            def open_bank(e):
                if e >= 4:
                    pe.wait_ge(bank_free[e % 4], e // 4)

            def feature_major(b, e, chunks, kc, rhs_hi, rhs_lo):
                pe.wait_ge(w_split, b + 1)
                wid = P * chunks
                for c in range(chunks):
                    open_bank(e + c)
                    for k in range(kc):
                        w = slice(wid * k + P * c, wid * k + P * c + P)
                        last = product(bank[(e + c) % 4][:, :], w_hi[b % RING][:, w], w_lo[b % RING][:, w], rhs_hi[:, k, :], rhs_lo[:, k, :],
                                       k == 0, k == kc - 1)
                    last.then_inc(bank_full, 1)

            def token_major(b, e, counts, wid, lhs_hi, lhs_lo):
                k0, total = 0, sum(counts)
                for i, kc in enumerate(counts):
                    pe.wait_ge(w_split, b + i + 1)
                    for t in range(TT):
                        if i == 0:
                            open_bank(e + t)
                        for k in range(kc):
                            w = slice(wid * k, wid * k + wid)
                            tok = slice(P * t, P * t + P)
                            last = product(bank[(e + t) % 4][:, 0:wid], lhs_hi[:, k0 + k, tok], lhs_lo[:, k0 + k, tok], w_hi[(b + i) % RING][:, w],
                                           w_lo[(b + i) % RING][:, w], k0 + k == 0, k0 + k == total - 1)
                        if i == len(counts) - 1:
                            last.then_inc(bank_full, 1)
                    if i < len(counts) - 1:
                        last.then_inc(w_used, 1)
                    k0 += kc

            def transpose_normed(name):
                for t in range(TT):
                    T = TT * pre_use[name] + t
                    pe.wait_ge(xn_done, T + 1)
                    for j in range(2):
                        q = 2 * T + j
                        if q >= 2:
                            pe.wait_ge(xT_split, q - 1)
                        for i in range(4):
                            last = nc.tensor.transpose(sc[q % 2][:, P * i:P * i + P], xn[:, t % 2, P * (4 * j + i):P * (4 * j + i) + P], ident[:, :])
                        last.then_inc(xpose_done, 1)
                pe.wait_ge(xT_split, 2 * TT * (pre_use[name] + 1))

            def attention(lo, hi, operands, group, begin, finish):
                for i in range(lo, hi + 4):
                    if i < hi:
                        kind, h, t = UNITS[i]
                        q, k, _ = operands(h, t)
                        if i >= 2:
                            if UNITS[i - 2][0] == "fox":
                                pe.wait_ge(sc_free, i - 2 - U_FOX + 1)
                            else:
                                pe.wait_ge(s_ready, i - 1)
                        nc.tensor.matmul(sc[i % 2][:, 0:P * (t + 1)], q, k, start=True, stop=True).then_inc(sc_ready, 1)
                    if lo <= i - 2 < hi:
                        u = i - 2
                        t = UNITS[u][2]
                        pe.wait_ge(pn_ready, u + 1)
                        if u >= 1:
                            pe.wait_ge(pT_ready, u)
                        for j in range(t + 1):
                            last = nc.tensor.transpose(tp[:, P * j:P * j + P], s_ring[:, u % 4, P * j:P * j + P], ident[:, :])
                        last.then_inc(tp_ready, 1)
                    if lo <= i - 4 and (i - 4 - lo) % group == group - 1:
                        finish((i - 4 - lo) // group)
                    if lo <= i - 3 < hi:
                        u = i - 3
                        _, h, t = UNITS[u]
                        vals, dst = operands(h, t)[2]
                        pe.wait_ge(pT_ready, u + 1)
                        if (u - lo) % group == 0:
                            begin((u - lo) // group)
                        for j in range(t + 1):
                            last = nc.tensor.matmul(dst, vals(j), pT[:, u % 2, P * j:P * j + P], start=j == 0, stop=j == t)
                        last.then_inc(pv_done, 1)

            pe.wait_ge(ident_made, 2)
            transpose_normed("pre0")
            for key in ("q", "k"):
                for i in range(4):
                    feature_major(FIRST[key] + i, USE[key] + 2 * i, 2, KD, xT_hi, xT_lo)
            for h in range(2):
                token_major(FIRST[f"v{h}"], USE[f"v{h}"], (4, 4), W, xT_hi, xT_lo)

            for e in range(USE["wo0"] - 4, USE["wo0"]):
                pe.wait_ge(*freed(e))

            def mha(h, t):
                rows = slice(HD * (h % 2), HD * (h % 2) + HD)
                return (qkT[rows, h // 2, P * t:P * t + P], qkT[rows, KD + h // 2, 0:P * (t + 1)],
                        (lambda j: v_sb[:, j, HD * h:HD * h + HD], ob[rows, P * t:P * t + P]))

            def mha_begin(g):
                if g >= 1:
                    pe.wait_ge(o_free, g)

            attention(0, U_FOX, mha, 2 * TT, mha_begin, lambda g: None)
            pe.wait_ge(o_free, HEADS // 2)
            for h in range(2):
                token_major(FIRST[f"wo{h}"], USE[f"wo{h}"], (4, 4), W, xT_hi, xT_lo)
            transpose_normed("pre1")
            for f in range(2):
                for i in range(FH):
                    feature_major(FIRST[f"gu{f}"] + i, USE[f"gu{f}"] + 2 * i, 2, KD, xT_hi, xT_lo)
                pe.wait_ge(act_split, FH * (f + 1))
                for h in range(2):
                    token_major(FIRST[f"down{f}{h}"], USE[f"down{f}{h}"], (4, 4, 3), W, act_hi, act_lo)
            transpose_normed("pre2")

            feature_major(FIRST["qi"], USE["qi"], 2, KD, xT_hi, xT_lo)
            feature_major(FIRST["ki"], USE["ki"], 1, KD, xT_hi, xT_lo)
            token_major(FIRST["cwf"], USE["cwf"], (KD,), P + IDX_H + BH, xT_hi, xT_lo)
            for i in range(2):
                feature_major(FIRST["b_q"] + i, USE["b_q"] + 2 * i, 2, KD, xT_hi, xT_lo)
            prep = 0

            def prep_bank():
                if prep >= 2:
                    pe.wait_ge(prep_free, prep - 1)
                return sc[prep % 2]

            z = prep_bank()
            for t in range(TT):
                pe.wait_ge(c_ready, t + 1)
                last = nc.tensor.transpose(z[:, P * t:P * t + P], c_sb[:, t, :], ident[:, :])
            last.then_inc(prep_ready, 1)
            prep += 1
            for c in range(2):
                pe.wait_ge(*freed(USE["qi"] + c))
            pe.wait_ge(*freed(USE["ki"]))
            for t in range(1, TT):
                for h in range(IDX_H):
                    rows = slice(IDX_D * (h % 2), IDX_D * (h % 2) + IDX_D)
                    z = prep_bank()
                    nc.tensor.matmul(z[:, 0:P * (t + 1)], qi[rows, h // 2, P * t:P * t + P], ki[rows, 0:P * (t + 1)], start=True,
                                     stop=True).then_inc(prep_ready, 1)
                    prep += 1
            pe.wait_ge(tri_made, 2)
            for h in range(BH):
                pe.wait_ge(lsx_ready, h + 1)
                z = prep_bank()
                for t in range(TT):
                    last = nc.tensor.matmul(z[:, P * t:S], lsx[:, h, t, :], tri[:, 0:S - P * t], start=t == 0, stop=t == TT - 1)
                last.then_inc(prep_ready, 1)
                prep += 1
            z = prep_bank()
            for t in range(TT):
                for j in range(t + 1):
                    ones = tri[:, 0:P] if j == t else tri[:, P:2 * P]
                    last = nc.tensor.matmul(z[:, BH * t:BH * t + BH], ones, ls[:, j, :], start=j == 0, stop=j == t)
            last.then_inc(prep_ready, 1)
            prep += 1
            pe.wait_ge(const_loaded, 16 * 5)
            for h in range(BH):
                pe.wait_ge(*freed(USE["b_q"] + h))
                z = prep_bank()
                nc.tensor.matmul(z[:, :], wukT[:, h, :], bq[:, h, :], start=True, stop=True).then_inc(prep_ready, 1)
                prep += 1
            for key in ("d_q", "d_k"):
                for i in range(2):
                    feature_major(FIRST[key] + i, USE[key] + 2 * i, 2, KD, xT_hi, xT_lo)
            token_major(FIRST["d_v"], USE["d_v"], (4, 4), W, xT_hi, xT_lo)
            for i in range(2):
                feature_major(FIRST["d_z"] + i, USE["d_z"] + 2 * i, 2, KD, xT_hi, xT_lo)
            for c in range(4):
                pe.wait_ge(*freed(USE["d_z"] + c))
            pe.wait_ge(prep_free, prep)

            def fox(h, t):
                return (dqk[:, h, P * t:P * t + P], dqk[:, BH + h, 0:P * (t + 1)],
                        (lambda j: dv[:, j, BD * h:BD * h + BD], ob[:, P * t:P * t + P]))

            attention(U_FOX, U_DSA, fox, TT, lambda g: pe.wait_ge(o_free, HEADS // 2 + g), lambda g: None)

            def gates(br):
                ys = slot[br]
                for half in range(2):
                    for i in range(2):
                        feature_major(FIRST[f"gate_{br}{half}"] + i, USE[f"gate_{br}{half}"] + 2 * i, 2, KD, xT_hi, xT_lo)
                    pe.wait_ge(y_split, 4 * ORDER.index(br) + 4)
                    feature_major(FIRST[f"branch_{br}{half}"], USE[f"branch_{br}{half}"], 4, KW, y_hi[ys], y_lo[ys])

            gates("d")
            for i in range(2):
                feature_major(FIRST["b_z"] + i, USE["b_z"] + 2 * i, 2, KD, xT_hi, xT_lo)

            def dsa(h, t):
                return (qlat[:, h, P * t:P * t + P], cT[:, 0:P * (t + 1)], (lambda j: c_sb[:, j, :], ob[:, P * t:P * t + P]))

            def dsa_finish(g):
                pe.wait_ge(olat_ready, g + 1)
                nc.tensor.matmul(ob[:, :], wuv[:, g, :], negcumk[:, 0, :], start=True, stop=True).then_inc(ydsa_ready, 1)

            attention(U_DSA, N_UNITS, dsa, TT, lambda g: pe.wait_ge(o_free, HEADS // 2 + BH + g), dsa_finish)
            gates("b")
            token_major(FIRST["a_v"], USE["a_v"], (4, 4), W, xT_hi, xT_lo)
            pe.wait_ge(mix_masked, 1)
            pe.wait_ge(ln_done, TT)
            for g in range(KW):
                z = prep_bank()
                for t in range(TT):
                    last = nc.tensor.matmul(z[:, P * t:P * t + P], av[:, t, P * g:P * g + P], a_ws[:, g, :], start=True, stop=True)
                last.then_inc(prep_ready, 1)
                prep += 1
            for j in range(KW):
                feature_major(FIRST["a_uz"] + j, USE["a_uz"] + 2 * j, 2, KD, xT_hi, xT_lo)
            gates("a")
            for i in range(2 * KW):
                feature_major(FIRST["c"] + i, USE["c"] + 2 * i, 2, KD, xT_hi, xT_lo)
            gates("c")
            pe.wait_ge(merged_split, KD)
            for h in range(2):
                token_major(FIRST[f"out{h}"], USE[f"out{h}"], (4, 4), W, xT_hi, xT_lo)


def pack_rows(w, rows, cols):
    part = w[rows][:, cols]
    part = part.reshape(-1, P, part.shape[1]).transpose(1, 0, 2).reshape(P, -1)
    out = np.zeros((P, BLK), w.dtype)
    out[:, :part.shape[1]] = part
    return out


def weight_stream(a):
    blocks = []
    r = lambda *x: np.concatenate([np.arange(*p) for p in x])
    w_qkv, w_in = a["w_qkv"][0], a["w_in_2"][0]
    every = np.arange(D)
    for i in range(8):
        blocks.append(pack_rows(w_qkv, every, r((256 * i, 256 * i + 256))))

    def token_blocks(w, rows, cols, step=4):
        for k in range(0, len(rows), step * P):
            blocks.append(pack_rows(w, rows[k:k + step * P], cols))

    for h in range(2):
        token_blocks(w_qkv, every, r((2 * D + W * h, 2 * D + W * h + W)))
    for h in range(2):
        token_blocks(a["w_o"][0], every, r((W * h, W * h + W)))
    gu = np.stack([a["w_gate"][0].reshape(D, FC, P), a["w_up"][0].reshape(D, FC, P)], 2).reshape(D, 2 * FF)
    for f in range(2):
        for i in range(FH * f, FH * f + FH):
            blocks.append(pack_rows(gu, every, r((256 * i, 256 * i + 256))))
        for h in range(2):
            token_blocks(a["w_down"][0], np.arange(FH * f * P, FH * (f + 1) * P), r((W * h, W * h + W)))
    col = {n: np.arange(*c) for n, c in COL.items()}

    def cols(*names):
        c = np.concatenate([col[n] for n in names])
        for i in range(0, len(c), 256):
            blocks.append(pack_rows(w_in, every, c[i:i + 256]))

    cols("b_qi")
    cols("b_ki", "b_ki")
    cols("b_c", "b_wi", "d_f")
    cols("b_q")
    cols("d_q")
    cols("d_k")
    token_blocks(w_in, every, col["d_v"])
    cols("d_z")

    def pairs(x, y, j):
        blocks.append(pack_rows(w_in, every, np.concatenate([col[x][P * j:P * j + P], col[y][P * j:P * j + P]])))

    for br in ORDER:
        n = BRANCH[br]
        if br == "b":
            cols("b_z")
        if br == "a":
            token_blocks(w_in, every, col["a_v"])
            for j in range(KW):
                pairs("a_u", "a_z", j)
        if br == "c":
            for j in range(KW):
                pairs("c_c", "c_x", j)
                pairs("c_b", "c_z", j)
        for half in range(2):
            for i in range(2):
                at = col["gates"][0] + D * n + W * half + 256 * i
                blocks.append(pack_rows(w_in, every, r((at, at + 256))))
            blocks.append(pack_rows(a["w_branch_2"][0, n], np.arange(W), r((W * half, W * half + W))))
    for h in range(2):
        token_blocks(a["w_out_2"][0], every, r((W * h, W * h + W)))
    assert len(blocks) == N_BLOCKS, (len(blocks), N_BLOCKS)
    return np.stack(blocks)


def kernel(**inputs):
    import concourse.bacc as bacc
    from concourse.bass_utils import run_bass_kernel_spmd

    a = {k: np.asarray(v) for k, v in inputs.items()}
    clip = np.clip(P + np.arange(P)[:, None] - np.arange(BIAS_W)[None, :], 1 - CHUNK, REL_CLIP) + CHUNK - 1
    arrays = {
        "weights": weight_stream(a),
        "x": a["x"][0],
        "bias": a["rel_bias"][0][:, clip],
        "g_pre_mix": a["g_pre_mix"][0], "g_post_mix": a["g_post_mix"][0],
        "g_pre_ffn": a["g_pre_ffn"][0], "g_post_ffn": a["g_post_ffn"][0],
        "norm_g": a["norm_g_2"][0], "final_g": a["final_g_2"],
        "ln_g": a["gm_ln_g_2"][0], "ln_b": a["gm_ln_b_2"][0],
        "gm_b": a["gm_b_s_2"][0], "gm_wT": a["gm_w_s_2"][0].transpose(2, 0, 1),
        "kvg": a["dsa_kv_g_2"][0], "bf": a["fox_b_f_2"][0],
        "wukT": a["dsa_w_uk_2"][0].transpose(2, 0, 1), "wuv": a["dsa_w_uv_2"][0].transpose(1, 0, 2),
        "convw": a["conv_w_2"][0].reshape(3, KW, P).transpose(2, 1, 0),
    }
    nc = bacc.Bacc("TRN2", target_bir_lowering=False, num_devices=1)
    feeds, dram = {}, {}
    for name, v in arrays.items():
        v = np.ascontiguousarray(v)
        feeds[f"in_{name}"] = v
        dram[name] = nc.dram_tensor(f"in_{name}", v.shape, mybir.dt.from_np(v.dtype), kind="ExternalInput").ap()
    out = nc.dram_tensor("out_0", (S, D), F32, kind="ExternalOutput").ap()
    build(nc, dram, out)
    r = run_bass_kernel_spmd(nc, [feeds], core_ids=[0])
    return r.results[0]["out_0"].reshape(1, S, D)
```

```python
from contextlib import ExitStack

import numpy as np

import concourse.bass as bass
from concourse import mybir

F32 = mybir.dt.float32
F32R = mybir.dt.float32r
ACT = mybir.ActivationFunctionType
ALU = mybir.AluOpType
AX_X = mybir.AxisListType.X

P = 128
S = 512
TT = S // P
D = 1024
KD = D // P
HEADS, HD = 16, 64
CHUNK = 64
REL_CLIP = 128
BIAS_W = 2 * P
FF = 2816
FC = FF // P
FH = FC // 2
W = 512
KW = W // P
BH, BD = 4, 128
IDX_H, IDX_D = 4, 64
TOPK = min(256, S // 4)
N_BRANCH = 4
EPS = 1e-6
NEG = -1e30
TAKEN, ACAUSAL = -3.4e38, -3.0e38
BLK = 2048
RING = 2
PARTS = 4

_SPLITS = [("a_u", W), ("a_v", W), ("a_z", W), ("b_q", W), ("b_c", P), ("b_qi", IDX_H * IDX_D), ("b_ki", IDX_D),
           ("b_wi", IDX_H), ("b_z", W), ("c_b", W), ("c_c", W), ("c_x", W), ("c_z", W), ("d_q", W), ("d_k", W),
           ("d_v", W), ("d_f", BH), ("d_z", W), ("gates", N_BRANCH * D)]
COL = {}
_at = 0
for _name, _width in _SPLITS:
    COL[_name] = (_at, _at + _width)
    _at += _width
IN_W = _at

ORDER = "adcb"
BRANCH = {"a": 0, "b": 1, "c": 2, "d": 3}


FEATURE_MAJOR = {"b_q", "d_q", "d_k", "d_z", "b_z"} | {f"gate_{br}{i}" for br in ORDER for i in range(2)}
QK_HEADS = P // HD
MHA_AT, MHA_FIRST_AT, MIX_AT, IDX_FIRST_AT, IDX_AT, PAIR_AT, ONE_AT = (1, 3, 5, 7), (4, 6), (4, 5, 6, 7), (0, 3, 6), (0, 4), (0, 4), (0,)


def plan():
    first, use, done, n, e, open_blocks = {}, {}, [], 0, 0, 0

    def add(name, blocks, uses):
        nonlocal n, e, open_blocks
        first[name], use[name] = n, e
        for i in range(blocks):
            if uses % blocks or (uses == TT and name not in FEATURE_MAJOR and i < blocks - 1):
                open_blocks += 1
                done.append(("w_used", open_blocks))
            else:
                done.append(("bank_full", e + uses * (i + 1) // blocks))
        if done[-1][0] == "w_used":
            open_blocks -= 1
            done[-1] = ("bank_full", e + uses)
        n += blocks
        e += uses

    for h in range(2):
        add(f"v{h}", 2, TT)
    for i in range(HEADS // QK_HEADS):
        add(f"qk{i}", 1, 2)
    for h in range(2):
        add(f"wo{h}", 2, TT)
    for f in range(2):
        add(f"gu{f}", FH, 2 * FH)
        for h in range(2):
            add(f"down{f}{h}", 3, TT)
    add("a_v", 2, TT)
    add("cwf", 1, TT)
    add("qi", 1, 2)
    add("ki", 1, 1)
    add("a_uz", 4, 8)
    add("d_q", 2, 4)
    add("d_k", 2, 4)
    add("d_v", 2, TT)
    add("d_z", 2, 4)
    add("c", 8, 16)
    add("b_q", 2, 4)
    add("b_z", 2, 4)
    for br in ORDER:
        for half in range(2):
            add(f"gate_{br}{half}", 2, 4)
            add(f"branch_{br}{half}", 1, 4)
    for h in range(2):
        add(f"out{h}", 2, TT)
    return first, use, done


FIRST, USE, DONE = plan()
N_BLOCKS = len(DONE)

UNITS = [("mha", h, t) for h in range(HEADS) for t in range(TT)]
UNITS += [("fox", h, t) for h in range(BH) for t in range(TT)]
UNITS += [("dsa", h, t) for h in range(BH) for t in range(TT)]
U_FOX = HEADS * TT
U_DSA = U_FOX + BH * TT
N_UNITS = len(UNITS)

NORMS = [("pre0", t) for t in range(TT)]
for _r in (1, 2):
    _seq = [(f"post{_r}", 0)]
    for _t in range(1, TT):
        _seq += [(f"post{_r}", _t), (f"pre{_r}", _t - 1)]
    NORMS += _seq + [(f"pre{_r}", TT - 1)]
NORMS += [("ln", t) for t in range(TT)] + [("c", t) for t in range(TT)] + [("final", t) for t in range(TT)]
NCOL = {n: i for i, n in enumerate(NORMS)}

SQUARES = []
for _name, _t in NORMS:
    if _name in ("post1", "post2", "final") and _t == 0:
        SQUARES += [(_name + "a", t) for t in range(TT)]
    SQUARES.append((_name + "b" if _name in ("post1", "post2", "final") else _name, _t))
SCOL = {n: i for i, n in enumerate(SQUARES)}


def build(nc, dram, out):
    ctx = ExitStack()
    with ctx:
        def sb(name, shape, dt=F32):
            return ctx.enter_context(nc.sbuf_tensor(name, shape, dt))

        def sem(name):
            return ctx.enter_context(nc.semaphore(name))

        w_raw = [sb(f"w_raw{i}", [P, BLK]) for i in range(RING)]
        w_hi = [sb(f"w_hi{i}", [P, BLK], F32R) for i in range(RING)]
        w_lo = [sb(f"w_lo{i}", [P, BLK], F32R) for i in range(RING)]
        xT_hi = sb("xT_hi", [P, KD, S], F32R)
        xT_lo = sb("xT_lo", [P, KD, S], F32R)
        act_hi = sb("act_hi", [P, 3 * KW, S], F32R)
        act_lo = sb("act_lo", [P, 3 * KW, S], F32R)
        x_sb = sb("x_sb", [P, TT, D])
        g_pre = sb("g_pre", [P, D])
        g_post = sb("g_post", [P, D])
        arena = sb("arena", [P, 13576])
        ident = sb("ident", [P, P])
        cmask = sb("cmask", [P, P])
        kvg = sb("kvg", [P, P])
        convw = sb("convw", [P, KW, 3])
        bf = sb("bf", [P, BH])
        minus_half = sb("minus_half", [P, 1])
        sumsq = sb("sumsq", [P, len(SQUARES)])
        var = sb("var", [P, len(NORMS)])
        rstd = sb("rstd", [P, len(NORMS)])
        mean = sb("mean", [P, TT])
        negmax = sb("negmax", [P, 4])
        psums = sb("psums", [P, 4])
        rinv = sb("rinv", [P, 4])
        wi = sb("wi", [P, TT, IDX_H])
        fb = sb("fb", [P, TT, BH])
        fna = sb("fna", [P, TT, BH])
        fl = sb("fl", [P, TT, BH])
        ls = sb("ls", [P, TT, BH])
        cumq = sb("cumq", [P, TT, BH])
        top8 = sb("top8", [P, 8])

        def view(at, *shape):
            n = int(np.prod(shape))
            v = arena[:, at:at + n]
            if len(shape) == 2:
                v = v.rearrange("p (a b) -> p a b", b=shape[1])
            if len(shape) == 3:
                v = v.rearrange("p (a b c) -> p a b c", b=shape[1], c=shape[2])
            return v

        SOFT = 9992
        q_st = [act_hi[:, KD + 2 * i:KD + 2 * i + 2, :] for i in range(2)]
        k_st = [act_lo[:, KD + 2 * i:KD + 2 * i + 2, :] for i in range(2)]
        k_rest = [act_lo[:, KD - 1, :], act_hi[:, KD - 1, :]]
        v_sb = x_sb
        biases = view(8192, 4, BIAS_W)
        s_ring = view(SOFT, 4, S)
        pT = view(SOFT + 4 * S, 3, S)
        oT_hi, oT_lo = act_hi[:, 0:KD, :], act_lo[:, 0:KD, :]
        m_sb = view(0, TT, D)
        xn = view(4096, 2, D)
        junk = view(6144, D)
        sg = view(7168, 2, S)
        a_sb = view(8192, 2, S)
        av = view(0, TT, W)
        a_mix = view(2048, KW, S)
        a_sz = view(4096, 2, S)
        a_y = view(4096 + 2 * S, 2, S)
        qi = view(6144, 2, S)
        ki = view(6144 + 2 * S, S)
        a_ws = view(6144 + 3 * S, KW, P)
        sel_at = [8192 + P * (t * (t + 1) // 2) for t in range(TT)]
        sel = [view(sel_at[t], P * (t + 1)) for t in range(TT)]
        a_bs = view(9472, KW, P)
        q_junk = view(SOFT, TT, W)
        relu_d = view(SOFT, 2, S)
        lsx = view(SOFT, BH, TT, P)
        c_raw = view(SOFT + 4 * S, TT, P)
        tri = view(SOFT + 5 * S, S)
        c_sb = g_pre[:, 0:S].rearrange("p (a b) -> p a b", b=P)
        cT = g_pre[:, S:2 * S]
        dqk = x_sb[:, :, :].rearrange("p t (a s) -> p (t a) s", s=S)
        dv = view(2048, TT, W)
        negcumk = view(4096, BH, S)
        sz = view(6144, KW, S)
        c_acc = view(0, S)
        c_sz = view(S, S)
        c_y = view(9472, S + 2)
        qlat = view(0, BH, S)
        bq = view(4096, KW, S)
        wukT = g_post[:, 0:S].rearrange("p (a b) -> p a b", b=P)
        wuv = g_post[:, S:2 * S].rearrange("p (a b) -> p a b", b=P)
        olat = view(4096 + 2 * S, S)
        merged = dqk
        sig = view(2048, 4, S)
        tmp = view(4096, 2, S)
        slot = {br: i % 3 for i, br in enumerate(ORDER)}
        y_hi = [act_hi[:, KW * i:KW * i + KW, :] for i in range(3)]
        y_lo = [act_lo[:, KW * i:KW * i + KW, :] for i in range(3)]
        mT_hi, mT_lo = act_hi[:, KW:3 * KW, :], act_lo[:, KW:3 * KW, :]

        bank = [ctx.enter_context(nc.psum_tensor(f"bank{i}", [P, S], F32)) for i in range(4)]
        sc = [ctx.enter_context(nc.psum_tensor(f"sc{i}", [P, S], F32)) for i in range(2)]
        tp = ctx.enter_context(nc.psum_tensor("tp", [P, S], F32))
        ob = ctx.enter_context(nc.psum_tensor("ob", [P, S], F32))

        xp = [sc[0], sc[1], tp, ob]

        x2_dram = nc.dram_tensor("x2_dram", (S, D), F32, kind="Internal").ap()

        w_loaded = [sem(f"w_loaded{i}") for i in range(RING)]
        w_rounded, w_split, w_used = sem("w_rounded"), sem("w_split"), sem("w_used")
        bank_full = sem("bank_full")
        bank_free = [sem(f"bank_free{i}") for i in range(4)]
        x_tile = [sem(f"x_tile{t}") for t in range(TT)]
        x_loaded, gpre_loaded, gpost_loaded, const_loaded = sem("x_loaded"), sem("gpre_loaded"), sem("gpost_loaded"), sem("const_loaded")
        x2_spilled, x2_loaded, aconst_loaded, out_stored = sem("x2_spilled"), sem("x2_loaded"), sem("aconst_loaded"), sem("out_stored")
        latent_loaded = sem("latent_loaded")
        masks_made, ident_made, tri_made = sem("masks_made"), sem("ident_made"), sem("tri_made")
        sumsq_done, var_begun, var_done, rstd_done = sem("sumsq_done"), sem("var_begun"), sem("var_done"), sem("rstd_done")
        gained, x_updated, xn_done = sem("gained"), sem("x_updated"), sem("xn_done")
        xpose_done, xT_rounded, xT_split = sem("xpose_done"), sem("xT_rounded"), sem("xT_split")
        bias_loaded = [sem(f"bias_loaded{i}") for i in range(4)]
        bias_ready = sem("bias_ready")
        q_rounded, k_rounded, first_split = sem("q_rounded"), sem("k_rounded"), sem("first_split")
        sc_ready, sc_free, part_done, s_ready = sem("sc_ready"), sem("sc_free"), sem("part_done"), sem("s_ready")
        max_ready, p_ready, rinv_ready, pn_ready = sem("max_ready"), sem("p_ready"), sem("rinv_ready"), sem("pn_ready")
        tp_ready, pT_ready, pv_done = sem("tp_ready"), sem("pT_ready"), sem("pv_done")
        o_free, o_rounded = sem("o_free"), sem("o_rounded")
        olat_ready, ydsa_ready = sem("olat_ready"), sem("ydsa_ready")
        act_rounded, act_split = sem("act_rounded"), sem("act_split")
        c_copied, wi_ready, f_abs, f_exp, f_log, f_ls, lsx_ready = (sem(n) for n in ("c_copied", "wi_ready", "f_abs", "f_exp", "f_log", "f_ls", "lsx_ready"))
        c_ready, prep_ready, prep_free = sem("c_ready"), sem("prep_ready"), sem("prep_free")
        score_added, score_masked, topk_step = sem("score_added"), sem("score_masked"), sem("topk_step")
        y_ready = {br: sem(f"y_ready_{br}") for br in "ac"}
        y_rounded = {br: sem(f"y_rounded_{br}") for br in ORDER}
        y_split = {br: sem(f"y_split_{br}") for br in ORDER}
        gate_add = sem("gate_add")
        merged_rounded, merged_split = sem("merged_rounded"), sem("merged_split")
        mean_ready, av_centred, ln_scaled, ln_done = (sem(n) for n in ("mean_ready", "av_centred", "ln_scaled", "ln_done"))
        mix_masked = sem("mix_masked")
        conv_step, conv_zero = sem("conv_step"), sem("conv_zero")
        out_ready = sem("out_ready")

        def freed(e):
            return bank_free[e % 4], e // 4 + 1

        def block_done(eng, b):
            what, count = DONE[b]
            eng.wait_ge(w_used if what == "w_used" else bank_full, count)

        def step(steps, n):
            for _ in range(n):
                next(steps, None)

        def step_between(steps, n, *others):
            for _ in range(n):
                next(steps, None)
                for other in others:
                    next(other, None)

        def part_columns(i):
            return slice(BLK // PARTS * i, BLK // PARTS * (i + 1))

        stream = dram["weights"]
        pre_use = {"pre0": 0, "pre1": 1, "pre2": 2}
        halves = ("post1", "post2", "final")

        PREP_MIX = 0
        PREP_CT = PREP_MIX + KW
        PREP_IDX = PREP_CT + 1
        PREP_CUM = PREP_IDX + IDX_H * (TT - 1)
        PREP_QLAT = PREP_CUM + BH + 1
        N_PREP = PREP_QLAT + BH
        O_FOX = HEADS // 2
        O_DSA = O_FOX + BH

        block = ctx.enter_context(nc.Block())

        @block.sync
        def _(sp):
            def load(b):
                if b >= RING:
                    sp.wait_ge(w_split, b - RING + 1)
                sp.dma_start(w_raw[b % RING][:, :], stream[b, :, :]).then_inc(w_loaded[b % RING], 16)

            x_tok = dram["x"].rearrange("(t p) d -> p t d", p=P)
            x2_tok = x2_dram.rearrange("(t p) d -> p t d", p=P)
            out_tok = out.rearrange("(t p) d -> p t d", p=P)

            sp.dma_start(x_sb[:, 0, :], x_tok[:, 0, :]).then_inc(x_tile[0], 16)
            sp.dma_start(g_pre[:, :], dram["g_pre_mix"].partition_broadcast(P)).then_inc(gpre_loaded, 16)
            sp.dma_start(x_sb[:, 1, :], x_tok[:, 1, :]).then_inc(x_tile[1], 16)
            for b in range(N_BLOCKS):
                if b == 2:
                    sp.dma_start(g_post[:, :], dram["g_post_mix"].partition_broadcast(P)).then_inc(gpost_loaded, 16)
                    sp.dma_start(kvg[:, :], dram["kvg"].partition_broadcast(P)).then_inc(const_loaded, 16)
                    sp.dma_start(bf[:, :], dram["bf"].partition_broadcast(P)).then_inc(const_loaded, 16)
                    sp.dma_start(convw[:, :, :], dram["convw"]).then_inc(const_loaded, 16)
                if b == FIRST["qk2"]:
                    sp.wait_ge(xn_done, TT)
                    sp.dma_start(g_pre[:, :], dram["g_pre_ffn"].partition_broadcast(P)).then_inc(gpre_loaded, 16)
                if b == FIRST["gu0"]:
                    sp.wait_ge(pv_done, U_FOX)
                    sp.dma_start(x_sb[:, :, :], x_tok).then_inc(x_loaded, 16)
                if b == FIRST["gu0"] + 5:
                    sp.wait_ge(x_updated, TT)
                    sp.dma_start(g_post[:, :], dram["g_post_ffn"].partition_broadcast(P)).then_inc(gpost_loaded, 16)
                    sp.wait_ge(xn_done, 2 * TT)
                    sp.dma_start(g_pre[:, :], dram["norm_g"].partition_broadcast(P)).then_inc(gpre_loaded, 16)
                if b == FIRST["ki"]:
                    sp.wait_ge(x_updated, 2 * TT)
                    sp.dma_start(g_post[:, 0:W], dram["ln_g"].partition_broadcast(P)).then_inc(gpost_loaded, 16)
                    sp.dma_start(g_post[:, W:2 * W], dram["ln_b"].partition_broadcast(P)).then_inc(gpost_loaded, 16)
                    sp.dma_start(a_bs, dram["gm_b"].partition_broadcast(P)).then_inc(aconst_loaded, 16)
                    sp.dma_start(a_ws, dram["gm_wT"]).then_inc(aconst_loaded, 16)
                if b == FIRST["a_uz"] + 1:
                    sp.dma_start(x2_tok, x_sb[:, :, :]).then_inc(x2_spilled, 16)
                if b == FIRST["d_k"]:
                    sp.wait_ge(ln_done, TT)
                    sp.dma_start(wukT, dram["wukT"]).then_inc(latent_loaded, 16)
                    sp.dma_start(wuv, dram["wuv"]).then_inc(latent_loaded, 16)
                if b == FIRST["gate_b0"]:
                    sp.wait_ge(ydsa_ready, BH)
                    sp.dma_start(g_post[:, :], dram["final_g"].partition_broadcast(P)).then_inc(gpost_loaded, 16)
                load(b)
                if b < 2:
                    sp.dma_start(x_sb[:, 2 + b, :], x_tok[:, 2 + b, :]).then_inc(x_tile[2 + b], 16)
            sp.wait_ge(merged_split, KD)
            sp.wait_ge(x2_spilled, 16)
            sp.dma_start(x_sb[:, :, :], x2_tok).then_inc(x2_loaded, 16)
            for t in range(TT):
                sp.wait_ge(out_ready, t + 1)
                sp.dma_start(out_tok[:, t, :], m_sb[:, t, :]).then_inc(out_stored, 16)
            sp.wait_ge(out_stored, 16 * TT)

        @block.gpsimd
        def _(pool):
            nc.gpsimd.memset(minus_half[:, :], -0.5).then_inc(masks_made, 1)
            nc.gpsimd.memset(ident[:, :], 0.0).then_inc(ident_made, 1)
            nc.gpsimd.memset(cmask[:, :], 0.0).then_inc(masks_made, 1)
            pool.wait_ge(ident_made, 1)
            nc.gpsimd.affine_select(out=ident[:, :], in_=ident[:, :], compare_op=ALU.not_equal, fill=1.0, base=0,
                                    pattern=[[-1, P]], channel_multiplier=1).then_inc(ident_made, 1)
            pool.wait_ge(masks_made, 2)
            nc.gpsimd.affine_select(out=cmask[:, :], in_=cmask[:, :], compare_op=ALU.is_ge, fill=NEG, base=0,
                                    pattern=[[-1, P]], channel_multiplier=1).then_inc(masks_made, 1)

            def reciprocal_roots(*names):
                for n, (name, _) in enumerate(NORMS):
                    if name in names:
                        pool.wait_ge(var_done, n + 1)
                        nc.gpsimd.tensor_tensor(rstd[:, n:n + 1], var[:, n:n + 1], minus_half[:, :], ALU.pow).then_inc(rstd_done, 1)

            reciprocal_roots("pre0")
            for h in range(HEADS):
                pool.wait_ge(bias_loaded[h % 4], 16 * (h // 4 + 1))
                nc.gpsimd.memset(biases[0:CHUNK, h % 4, BIAS_W - CHUNK:BIAS_W], NEG).then_inc(bias_ready, 1)
            reciprocal_roots("post1", "pre1")
            pool.wait_ge(pv_done, U_FOX)
            nc.gpsimd.memset(tri, 1.0).then_inc(tri_made, 1)
            pool.wait_ge(tri_made, 1)
            nc.gpsimd.affine_select(out=tri[:, 0:P], in_=tri[:, 0:P], compare_op=ALU.is_ge, fill=0.0, base=0,
                                    pattern=[[1, P]], channel_multiplier=-1).then_inc(tri_made, 1)
            reciprocal_roots("post2", "pre2")
            reciprocal_roots("ln")
            reciprocal_roots("c")
            pool.wait_ge(aconst_loaded, 32)
            nc.gpsimd.affine_select(out=a_ws, in_=a_ws, compare_op=ALU.is_ge, fill=0.0, base=0, pattern=[[0, KW], [1, P]],
                                    channel_multiplier=-1).then_inc(mix_masked, 1)
            for t in range(1, TT):
                pool.wait_ge(score_added, IDX_H * t)
                nc.gpsimd.affine_select(out=sel[t][:, P * t:P * (t + 1)], in_=sel[t][:, P * t:P * (t + 1)], compare_op=ALU.is_ge,
                                        fill=ACAUSAL, base=0, pattern=[[-1, P]], channel_multiplier=1).then_inc(score_masked, 1)
            reciprocal_roots("final")

        @block.scalar
        def _(act):
            def split_parts(b):
                if b >= N_BLOCKS:
                    return
                act.wait_ge(w_loaded[b % RING], 16 * (b // RING + 1))
                if b >= RING:
                    block_done(act, b - RING)
                for i in range(PARTS):
                    nc.scalar.activation(w_hi[b % RING][:, part_columns(i)], w_raw[b % RING][:, part_columns(i)], ACT.Copy).then_inc(w_rounded, 1)
                    yield

            def split(b):
                step(split_parts(b), PARTS)

            def read_out(dst, e, func=ACT.Copy):
                act.wait_ge(bank_full, e + 1)
                nc.scalar.activation(dst, bank[e % 4][:, :], func).then_inc(bank_free[e % 4], 1)

            def sum_squares(name, t, src, place=None):
                n = SCOL[name, t]
                if n:
                    act.wait_ge(sumsq_done, n)
                nc.scalar.activation(junk[:, 0:src.shape[-1]] if place is None else place, src, ACT.Square,
                                     accum_out=sumsq[:, n:n + 1]).then_inc(sumsq_done, 1)

            def round_xT(name, t):
                for j in range(2):
                    q = 2 * (TT * pre_use[name] + t) + j
                    act.wait_ge(xpose_done, q + 1)
                    nc.scalar.activation(xT_hi[:, 4 * j:4 * j + 4, P * t:P * t + P], xp[q % 4][:, :].rearrange("p (c s) -> p c s", s=P),
                                         ACT.Copy).then_inc(xT_rounded, 1)

            def norms(r, squares_b, late):
                for i in range(TT + 2):
                    if i < TT:
                        squares_b(i)
                    if 0 <= i - 1 < TT:
                        act.wait_ge(x_updated, TT * (r - 1) + i)
                        sum_squares(f"pre{r}", i - 1, x_sb[:, i - 1, :])
                    if i == TT:
                        split(late)
                    if i >= 2:
                        round_xT(f"pre{r}", i - 2)

            def attention(lo, hi, o_done):
                for i in range(lo, hi + 6):
                    if lo <= i - 5 < hi:
                        o_done(i - 5)
                    if i < hi:
                        kind, h, t = UNITS[i]
                        nk = P * (t + 1)
                        if kind == "mha" and t == 0:
                            bias_load(h + 2)
                        if kind == "fox" or (kind == "mha" and t >= 2):
                            act.wait_ge(sc_ready, i + 1)
                            if i >= 4:
                                act.wait_ge(tp_ready, i - 3)
                        if kind == "mha" and t >= 2:
                            act.wait_ge(bias_ready, h + 1)
                            nc.scalar.activation(s_ring[:, i % 4, 0:nk - BIAS_W], sc[i % 2][:, 0:nk - BIAS_W], ACT.Identity,
                                                 bias=biases[:, h % 4, 0:1], scale=HD ** -0.5).then_inc(part_done, 1)
                        if kind == "fox":
                            nc.scalar.activation(s_ring[:, i % 4, 0:nk], sc[i % 2][:, 0:nk], ACT.Identity,
                                                 bias=cumq[:, t, h:h + 1], scale=BD ** -0.5).then_inc(sc_free, 1)
                    if lo <= i - 1 < hi:
                        u = i - 1
                        nk = P * (UNITS[u][2] + 1)
                        act.wait_ge(max_ready, u + 1)
                        if u >= 4:
                            act.wait_ge(rinv_ready, u - 3)
                        nc.scalar.activation(s_ring[:, u % 4, 0:nk], s_ring[:, u % 4, 0:nk], ACT.Exp, bias=negmax[:, u % 4:u % 4 + 1],
                                             accum_out=psums[:, u % 4:u % 4 + 1]).then_inc(p_ready, 1)
                    if lo <= i - 2 < hi:
                        u = i - 2
                        nk = P * (UNITS[u][2] + 1)
                        act.wait_ge(tp_ready, u + 1)
                        if u >= 3:
                            act.wait_ge(pv_done, u - 2)
                        nc.scalar.activation(pT[:, u % 3, 0:nk], tp[:, 0:nk], ACT.Copy).then_inc(pT_ready, 1)
                    yield

            def bias_load(h):
                if h < HEADS:
                    if h >= 4:
                        act.wait_ge(s_ready, TT * (h - 3))
                        act.wait_ge(part_done, 2 * (h - 3))
                    act.dma_start(biases[:, h % 4, :], dram["bias"][h, :, :]).then_inc(bias_loaded[h % 4], 16)

            def first_squares(t):
                act.wait_ge(x_tile[t], 16)
                sum_squares("pre0", t, x_sb[:, t, :])

            first_squares(0)
            first_squares(1)
            round_xT("pre0", 0)
            split(0)
            first_squares(2)
            round_xT("pre0", 1)
            first_squares(3)
            split(1)
            round_xT("pre0", 2)
            round_xT("pre0", 3)
            bias_load(0)
            bias_load(1)

            for h in range(2):
                b = FIRST[f"v{h}"]
                split(b + 2)
                for t in range(TT):
                    read_out(v_sb[:, t, W * h:W * h + W], USE[f"v{h}"] + t)
                split(b + 3)

            def pair_out(u):
                if u % (2 * TT) == 2 * TT - 1:
                    act.wait_ge(pv_done, u + 1)
                    nc.scalar.activation(oT_hi[:, u // (2 * TT), :], ob[:, :], ACT.Copy).then_inc(o_rounded, 1)

            pair = (slice(0, HD), slice(HD, P))

            def queries_out(i):
                e = USE[f"qk{i}"]
                for c in range(2):
                    act.wait_ge(bank_full, e + 1)
                    nc.scalar.activation(q_st[i % 2][pair[c], c, :], bank[e % 4][pair[c], :], ACT.Copy).then_inc(q_rounded, 1)
                    yield

            def keys_out(i):
                e = USE[f"qk{i}"] + 1
                for c in range(2):
                    act.wait_ge(bank_full, e + 1)
                    for place in range(2):
                        nc.scalar.activation(k_st[i % 2][pair[place], c, :], bank[e % 4][pair[c], :], ACT.Copy).then_inc(k_rounded, 1)
                    yield

            mha = attention(0, U_FOX, pair_out)
            step(queries_out(0), 2)
            step(keys_out(0), 2)
            keys, parts = iter(()), split_parts(FIRST["qk0"] + 2)
            for i in range(1, HEADS // QK_HEADS):
                step(keys, 1)
                step_between(mha, len(MHA_FIRST_AT if i == 1 else MHA_AT), keys, parts)
                queries = queries_out(i)
                step(queries, 1)
                step_between(mha, len(MHA_AT), queries, parts)
                keys, parts = keys_out(i), split_parts(FIRST[f"qk{i}"] + 2)
            step(keys, 1)

            step_between(mha, 4 * TT, keys, parts)
            split(FIRST["wo0"] + 2)
            for t in range(TT):
                act.wait_ge(bank_full, USE["wo0"] + t + 1)
                sum_squares("post1a", t, bank[(USE["wo0"] + t) % 4][:, :])
            split(FIRST["wo0"] + 3)
            split(FIRST["wo1"] + 2)

            def squares_wo1(t):
                act.wait_ge(bank_full, USE["wo1"] + t + 1)
                sum_squares("post1b", t, bank[(USE["wo1"] + t) % 4][:, :])

            norms(1, squares_wo1, FIRST["wo1"] + 3)

            for f in range(2):
                for i in range(FH):
                    n = FH * f + i
                    b, e = FIRST[f"gu{f}"] + i, USE[f"gu{f}"] + 2 * i
                    if n >= 2:
                        act.wait_ge(act_split, n - 1)
                    read_out(sg[:, n % 2, :], e, ACT.Silu)
                    act.wait_ge(*freed(e + 1))
                    nc.scalar.activation(act_hi[:, i, :], a_sb[:, n % 2, :], ACT.Copy).then_inc(act_rounded, 1)
                    split(b + 2)
                for h in range(2):
                    b, e = FIRST[f"down{f}{h}"], USE[f"down{f}{h}"]
                    split(b + 2)
                    split(b + 3)
                    if f == 0:
                        for t in range(TT):
                            read_out(m_sb[:, t, W * h:W * h + W], e + t)
                        split(b + 4)
                    elif h == 0:
                        for t in range(TT):
                            act.wait_ge(*freed(e + t))
                            sum_squares("post2a", t, m_sb[:, t, 0:W])
                        split(b + 4)

            def squares_down11(t):
                act.wait_ge(*freed(USE["down11"] + t))
                sum_squares("post2b", t, m_sb[:, t, W:2 * W])

            norms(2, squares_down11, FIRST["down11"] + 4)

            split(FIRST["a_v"] + 2)
            for t in range(TT):
                e = USE["a_v"] + t
                act.wait_ge(bank_full, e + 1)
                nc.scalar.activation(av[:, t, :], bank[e % 4][:, :], ACT.Copy, accum_out=mean[:, t:t + 1]).then_inc(bank_free[e % 4], 1)
            split(FIRST["a_v"] + 3)
            for t in range(TT):
                act.wait_ge(av_centred, t + 1)
                sum_squares("ln", t, av[:, t, :], q_junk[:, t, :])
            for t in range(TT):
                e = USE["cwf"] + t
                act.wait_ge(bank_full, e + 1)
                nc.scalar.activation(c_raw[:, t, :], bank[e % 4][:, 0:P], ACT.Copy).then_inc(c_copied, 1)
            split(FIRST["cwf"] + 2)
            for t in range(TT):
                act.wait_ge(c_copied, t + 1)
                sum_squares("c", t, c_raw[:, t, :], q_junk[:, t, 0:P])
            act.wait_ge(f_abs, 1)
            nc.scalar.activation(fl[:, :, :], fna[:, :, :], ACT.Exp).then_inc(f_exp, 1)
            act.wait_ge(f_exp, 1)
            nc.scalar.activation(fl[:, :, :], fl[:, :, :], ACT.Ln, bias=1.0).then_inc(f_log, 1)
            for c in range(2):
                read_out(qi[:, c, :], USE["qi"] + c)
            split(FIRST["qi"] + 2)
            read_out(ki, USE["ki"])
            split(FIRST["ki"] + 2)

            def round_y(br, j, src):
                act.wait_ge(y_ready[br], j + 1)
                nc.scalar.activation(y_hi[slot[br]][:, j, :], src, ACT.Copy).then_inc(y_rounded[br], 1)

            def small_products():
                def prep_out(n, dst, func, src, scale=1.0):
                    act.wait_ge(prep_ready, n + 1)
                    nc.scalar.activation(dst, src(sc[n % 2]), func, scale=scale).then_inc(prep_free, 1)

                prep_out(PREP_CT, cT, ACT.Copy, lambda z: z[:, :])
                yield
                for t in range(1, TT):
                    for h in range(IDX_H):
                        j = IDX_H * (t - 1) + h
                        if j >= 2:
                            act.wait_ge(score_added, j - 1)
                        prep_out(PREP_IDX + j, relu_d[:, j % 2, 0:P * (t + 1)], ACT.Relu, lambda z: z[:, 0:P * (t + 1)], IDX_D ** -0.5)
                        yield
                act.wait_ge(y_split["a"], KW)
                for h in range(BH):
                    prep_out(PREP_CUM + h, negcumk[:, h, :], ACT.Copy, lambda z: z[:, :], -1.0)
                    yield
                prep_out(PREP_CUM + BH, cumq[:, :, :], ACT.Copy, lambda z: z[:, 0:TT * BH].rearrange("p (t h) -> p t h", h=BH))
                yield
                act.wait_ge(y_split["c"], KW)
                for h in range(BH):
                    prep_out(PREP_QLAT + h, qlat[:, h, :], ACT.Copy, lambda z: z[:, :])
                    yield

            small = small_products()
            for j in range(KW):
                e = USE["a_uz"] + 2 * j
                step(small, (len(IDX_AT if j else IDX_FIRST_AT) + len(IDX_AT)) if j < TT - 1 else 0)
                if j >= 2:
                    act.wait_ge(y_split["a"], j - 1)
                read_out(a_sz[:, j % 2, :], e + 1, ACT.Silu)
                round_y("a", j, a_y[:, j % 2, :])
                split(FIRST["a_uz"] + j + 2)
            act.wait_ge(x2_spilled, 16)
            for key, base in (("d_q", 0), ("d_k", BH)):
                for i in range(2):
                    for c in range(2):
                        if key == "d_k":
                            step(small, 1 if i + c else 2)
                        read_out(dqk[:, base + 2 * i + c, :], USE[key] + 2 * i + c)
                    split(FIRST[key] + i + 2)
            split(FIRST["d_v"] + 2)
            for t in range(TT):
                read_out(dv[:, t, :], USE["d_v"] + t)
            split(FIRST["d_v"] + 3)
            for i in range(2):
                for c in range(2):
                    read_out(sz[:, 2 * i + c, :], USE["d_z"] + 2 * i + c, ACT.Silu)
                split(FIRST["d_z"] + i + 2)

            def fox_out(u):
                if u % TT == TT - 1:
                    h = (u - U_FOX) // TT
                    act.wait_ge(o_free, O_FOX + h + 1)
                    nc.scalar.activation(y_hi[slot["d"]][:, h, :], sz[:, h, :], ACT.Copy).then_inc(y_rounded["d"], 1)

            fox = attention(U_FOX, U_DSA, fox_out)
            parts = iter(())
            n_at = len(PAIR_AT)
            for j in range(KW):
                b, e = FIRST["c"] + 2 * j, USE["c"] + 4 * j
                step_between(fox, n_at, parts)
                if j == 0:
                    act.wait_ge(conv_zero, 1)
                else:
                    act.wait_ge(conv_step, 3 * j)
                read_out(c_y[:, 2:2 + S], e)
                step_between(fox, 1, parts)
                if j:
                    round_y("c", j - 1, c_acc)
                step_between(fox, n_at - 1, parts)
                parts = split_parts(b + 2)
                step_between(fox, 2 * n_at, parts)
                if j:
                    act.wait_ge(y_ready["c"], j)
                read_out(c_sz, e + 3, ACT.Silu)
                parts = split_parts(b + 3)
            step(parts, PARTS)
            round_y("c", KW - 1, c_acc)
            step(fox, U_DSA)

            for i in range(2):
                for c in range(2):
                    read_out(bq[:, 2 * i + c, :], USE["b_q"] + 2 * i + c)
                split(FIRST["b_q"] + i + 2)
            act.wait_ge(y_split["d"], BH)
            for i in range(2):
                for c in range(2):
                    step(small, 1)
                    read_out(sz[:, 2 * i + c, :], USE["b_z"] + 2 * i + c, ACT.Silu)
                split(FIRST["b_z"] + i + 2)

            def dsa_out(u):
                if u % TT == TT - 1:
                    h = (u - U_DSA) // TT
                    act.wait_ge(pv_done, u + 1)
                    if h >= 1:
                        act.wait_ge(ydsa_ready, h)
                    nc.scalar.activation(olat, ob[:, :], ACT.Copy).then_inc(olat_ready, 1)

            def gates(br):
                r = ORDER.index(br)
                for half in range(2):
                    b, e = FIRST[f"gate_{br}{half}"], USE[f"gate_{br}{half}"]
                    for i in range(2):
                        parts = split_parts(b + i + 1) if i or half or r else iter(())
                        step_between(dsa, 2 * len(PAIR_AT), parts)
                        step(parts, PARTS)
                        for c in range(2):
                            if half or r:
                                last = f"branch_{br}0" if half else f"branch_{ORDER[r - 1]}1"
                                act.wait_ge(*freed(USE[last] + 2 * i + c))
                            read_out(sig[:, 2 * i + c, :], e + 2 * i + c, ACT.Sigmoid)
                    split(b + 3)
                    if br == ORDER[-1]:
                        for j in range(4 * half, 4 * half + 4):
                            act.wait_ge(gate_add, KD * (N_BRANCH - 2) + j + 1)
                            nc.scalar.activation(mT_hi[:, j, :], merged[:, j, :], ACT.Copy).then_inc(merged_rounded, 1)

            dsa = attention(U_DSA, N_UNITS, dsa_out)
            gates("a")
            gates("d")
            block_done(act, FIRST["branch_a1"])
            for j in range(KW):
                act.wait_ge(o_free, O_DSA + j + 1)
                nc.scalar.activation(y_hi[slot["b"]][:, j, :], sz[:, j, :], ACT.Copy).then_inc(y_rounded["b"], 1)
            gates("c")
            gates("b")
            split(FIRST["out0"] + 1)
            for h in range(2):
                split(FIRST[f"out{h}"] + 2)
                split(FIRST[f"out{h}"] + 3)
                for t in range(TT):
                    act.wait_ge(*freed(USE[f"out{h}"] + t))
                    sum_squares("final" + "ab"[h], t, x_sb[:, t, W * h:W * h + W])

        @block.vector
        def _(dve):
            def split_parts(b):
                if b >= N_BLOCKS:
                    return
                for i in range(PARTS):
                    dve.wait_ge(w_rounded, PARTS * b + i + 1)
                    last = nc.vector.tensor_tensor(w_lo[b % RING][:, part_columns(i)], w_raw[b % RING][:, part_columns(i)], w_hi[b % RING][:, part_columns(i)].bitcast(F32),
                                                   ALU.subtract)
                    if i == PARTS - 1:
                        last.then_inc(w_split, 1)
                    yield

            def split(b):
                step(split_parts(b), PARTS)

            def begin_variance(name, t):
                n, first = NCOL[name, t], SCOL[name + "a", t]
                dve.wait_ge(sumsq_done, first + 1)
                nc.vector.tensor_scalar(var[:, n:n + 1], sumsq[:, first:first + 1], 1.0 / D, EPS, ALU.mult, ALU.add).then_inc(var_begun, 1)

            def variance(name, t, width):
                n = NCOL[name, t]
                if name in halves:
                    second = SCOL[name + "b", t]
                    dve.wait_ge(sumsq_done, second + 1)
                    dve.wait_ge(var_begun, TT * halves.index(name) + t + 1)
                    nc.vector.scalar_tensor_tensor(out=var[:, n:n + 1], in0=sumsq[:, second:second + 1], scalar=1.0 / width, in1=var[:, n:n + 1],
                                                   op0=ALU.mult, op1=ALU.add).then_inc(var_done, 1)
                else:
                    only = SCOL[name, t]
                    dve.wait_ge(sumsq_done, only + 1)
                    nc.vector.tensor_scalar(var[:, n:n + 1], sumsq[:, only:only + 1], 1.0 / width, EPS, ALU.mult, ALU.add).then_inc(var_done, 1)

            def scale_rows(out_, in_, name, t, other, op=ALU.mult):
                n = NCOL[name, t]
                dve.wait_ge(rstd_done, n + 1)
                return nc.vector.scalar_tensor_tensor(out=out_, in0=in_, scalar=rstd[:, n:n + 1], in1=other, op0=ALU.mult, op1=op)

            def scale_pre(name, t):
                q = TT * pre_use[name] + t
                dve.wait_ge(gpre_loaded, 16 * (pre_use[name] + 1))
                if q >= 2:
                    dve.wait_ge(xpose_done, 2 * (q - 1))
                scale_rows(xn[:, t % 2, :], x_sb[:, t, :], name, t, g_pre[:, :]).then_inc(xn_done, 1)

            def split_xT(name, t):
                for j in range(2):
                    q = 2 * (TT * pre_use[name] + t) + j
                    dve.wait_ge(xT_rounded, q + 1)
                    part = (slice(None), slice(4 * j, 4 * j + 4), slice(P * t, P * t + P))
                    nc.vector.tensor_tensor(xT_lo[part], xp[q % 4][:, :].rearrange("p (c s) -> p c s", s=P), xT_hi[part].bitcast(F32),
                                            ALU.subtract).then_inc(xT_split, 1)

            def norms(r, gain_b, late):
                for i in range(TT + 2):
                    if i < TT:
                        gain_b(i)
                        variance(f"post{r}", i, D)
                    if 0 <= i - 1 < TT:
                        variance(f"pre{r}", i - 1, D)
                    if i == TT - 1:
                        split_xT(f"pre{r}", i - 2)
                    if i < TT:
                        dve.wait_ge(x_loaded, 16)
                        scale_rows(x_sb[:, i, :], m_sb[:, i, :], f"post{r}", i, x_sb[:, i, :], ALU.add).then_inc(x_updated, 1)
                    if 0 <= i - 1 < TT:
                        dve.wait_ge(x_updated, TT * (r - 1) + i)
                        scale_pre(f"pre{r}", i - 1)
                    if i == TT:
                        split(late)
                    if i >= 2 and i != TT - 1:
                        split_xT(f"pre{r}", i - 2)

            def attention(lo, hi, o_done):
                for i in range(lo, hi + 6):
                    if lo <= i - 5 < hi and UNITS[i - 5][0] != "dsa":
                        o_done(i - 5)
                    if i < hi:
                        kind, h, t = UNITS[i]
                        nk = P * (t + 1)
                        s = s_ring[:, i % 4, 0:nk]
                        if kind == "fox":
                            dve.wait_ge(sc_free, i - U_FOX + 1)
                            nc.vector.tensor_tensor(s, s, negcumk[:, h, 0:nk], ALU.add).then_inc(part_done, 1)
                            dve.wait_ge(part_done, HEADS * 2 + i - U_FOX + 1)
                            nc.vector.tensor_tensor(s[:, nk - P:nk], s[:, nk - P:nk], cmask[:, :], ALU.add).then_inc(s_ready, 1)
                        else:
                            dve.wait_ge(sc_ready, i + 1)
                            if i >= 4:
                                dve.wait_ge(tp_ready, i - 3)
                        if kind == "mha":
                            w = min(nk, BIAS_W)
                            dve.wait_ge(bias_ready, h + 1)
                            if t >= 2:
                                dve.wait_ge(part_done, 2 * h + t - 1)
                            nc.vector.scalar_tensor_tensor(out=s[:, nk - w:nk], in0=sc[i % 2][:, nk - w:nk], scalar=HD ** -0.5,
                                                           in1=biases[:, h % 4, BIAS_W - w:BIAS_W], op0=ALU.mult,
                                                           op1=ALU.add).then_inc(s_ready, 1)
                        if kind == "dsa":
                            nc.vector.scalar_tensor_tensor(out=s, in0=sc[i % 2][:, 0:nk], scalar=BD ** -0.5,
                                                           in1=cmask[:, :] if t == 0 else sel[t], op0=ALU.mult,
                                                           op1=ALU.add).then_inc(s_ready, 1)
                        dve.wait_ge(s_ready, i + 1)
                        if i >= 4:
                            dve.wait_ge(p_ready, i - 3)
                        nc.vector.reduce_max(negmax[:, i % 4:i % 4 + 1], s, AX_X, negate=True).then_inc(max_ready, 1)
                    if lo <= i - 5 < hi and UNITS[i - 5][0] == "dsa":
                        o_done(i - 5)
                    if lo <= i - 1 < hi:
                        u = i - 1
                        nk = P * (UNITS[u][2] + 1)
                        dve.wait_ge(p_ready, u + 1)
                        nc.vector.reciprocal(rinv[:, u % 4:u % 4 + 1], psums[:, u % 4:u % 4 + 1]).then_inc(rinv_ready, 1)
                        dve.wait_ge(rinv_ready, u + 1)
                        nc.vector.tensor_scalar(s_ring[:, u % 4, 0:nk], s_ring[:, u % 4, 0:nk], rinv[:, u % 4:u % 4 + 1], None,
                                                ALU.mult).then_inc(pn_ready, 1)
                    yield

            variance("pre0", 0, D)
            scale_pre("pre0", 0)
            variance("pre0", 1, D)
            scale_pre("pre0", 1)
            split_xT("pre0", 0)
            split(0)
            variance("pre0", 2, D)
            split_xT("pre0", 1)
            variance("pre0", 3, D)
            scale_pre("pre0", 2)
            split(1)
            scale_pre("pre0", 3)
            split_xT("pre0", 2)
            split_xT("pre0", 3)
            for b in range(FIRST["v0"], FIRST["qk0"]):
                split(b + 2)

            def pair_out(u):
                if u % (2 * TT) == 2 * TT - 1:
                    hp = u // (2 * TT)
                    dve.wait_ge(o_rounded, hp + 1)
                    nc.vector.tensor_tensor(oT_lo[:, hp, :], ob[:, :], oT_hi[:, hp, :].bitcast(F32), ALU.subtract).then_inc(o_free, 1)

            pair = (slice(0, HD), slice(HD, P))

            def queries_split(i):
                e, q = USE[f"qk{i}"], q_st[i % 2]
                for c in range(2):
                    dve.wait_ge(q_rounded, 2 * i + c + 1)
                    nc.vector.tensor_tensor(q[pair[1 - c], c, :], bank[e % 4][pair[c], :], q[pair[c], c, :].bitcast(F32), ALU.subtract)\
                        .then_inc(bank_free[e % 4] if c else first_split, 1)
                    yield

            def keys_split(i):
                e, k = USE[f"qk{i}"] + 1, k_st[i % 2]
                for c in range(2):
                    dve.wait_ge(k_rounded, 4 * i + 2 * c + 2)
                    nc.vector.tensor_tensor(k_rest[i % 2][pair[c], :], bank[e % 4][pair[c], :], k[pair[c], c, :].bitcast(F32), ALU.subtract)\
                        .then_inc(bank_free[e % 4] if c else first_split, 1)
                    yield

            mha = attention(0, U_FOX, pair_out)
            step(queries_split(0), 2)
            step(keys_split(0), 2)
            keys, parts = iter(()), split_parts(FIRST["qk0"] + 2)
            for i in range(1, HEADS // QK_HEADS):
                step(keys, 1)
                step_between(mha, len(MHA_FIRST_AT if i == 1 else MHA_AT), keys, parts)
                queries = queries_split(i)
                step(queries, 1)
                step_between(mha, len(MHA_AT), queries, parts)
                keys, parts = keys_split(i), split_parts(FIRST[f"qk{i}"] + 2)
            step(keys, 1)

            def gain_wo(h, t):
                e = USE[f"wo{h}"] + t
                dve.wait_ge(gpost_loaded, 16)
                dve.wait_ge(sumsq_done, SCOL["post1" + "ab"[h], t] + 1)
                part = slice(W * h, W * h + W)
                nc.vector.tensor_tensor(m_sb[:, t, part], bank[e % 4][:, :], g_post[:, part], ALU.mult).then_inc(bank_free[e % 4], 1)
                dve.wait_ge(*freed(e))

            step_between(mha, 4 * TT, keys, parts)
            split(FIRST["wo0"] + 2)
            for t in range(TT):
                begin_variance("post1", t)
                gain_wo(0, t)
            split(FIRST["wo0"] + 3)
            split(FIRST["wo1"] + 2)
            norms(1, lambda t: gain_wo(1, t), FIRST["wo1"] + 3)

            def add_down(h, t):
                e = USE[f"down1{h}"] + t
                dve.wait_ge(*freed(USE[f"down0{h}"] + t))
                dve.wait_ge(bank_full, e + 1)
                part = m_sb[:, t, W * h:W * h + W]
                nc.vector.tensor_tensor(part, part, bank[e % 4][:, :], ALU.add).then_inc(bank_free[e % 4], 1)

            def gain_down(h, t):
                dve.wait_ge(gpost_loaded, 32)
                dve.wait_ge(sumsq_done, SCOL["post2" + "ab"[h], t] + 1)
                part = slice(W * h, W * h + W)
                nc.vector.tensor_tensor(m_sb[:, t, part], m_sb[:, t, part], g_post[:, part], ALU.mult).then_inc(gained, 1)
                dve.wait_ge(gained, TT * h + t + 1)

            for f in range(2):
                for i in range(FH):
                    n = FH * f + i
                    e = USE[f"gu{f}"] + 2 * i
                    dve.wait_ge(*freed(e))
                    dve.wait_ge(bank_full, e + 2)
                    nc.vector.tensor_tensor(a_sb[:, n % 2, :], sg[:, n % 2, :], bank[(e + 1) % 4][:, :], ALU.mult).then_inc(bank_free[(e + 1) % 4], 1)
                    dve.wait_ge(act_rounded, n + 1)
                    nc.vector.tensor_tensor(act_lo[:, i, :], a_sb[:, n % 2, :], act_hi[:, i, :].bitcast(F32), ALU.subtract).then_inc(act_split, 1)
                    split(FIRST[f"gu{f}"] + i + 2)
                for h in range(2):
                    b = FIRST[f"down{f}{h}"]
                    split(b + 2)
                    split(b + 3)
                    if f == 0:
                        split(b + 4)
                    elif h == 0:
                        for t in range(TT + 1):
                            if t < TT:
                                add_down(0, t)
                            if t:
                                begin_variance("post2", t - 1)
                                gain_down(0, t - 1)
                        split(b + 4)

            def gain_down11(t):
                add_down(1, t)
                gain_down(1, t)

            norms(2, gain_down11, FIRST["down11"] + 4)

            split(FIRST["a_v"] + 2)
            for t in range(TT):
                dve.wait_ge(*freed(USE["a_v"] + t))
                nc.vector.tensor_scalar(mean[:, t:t + 1], mean[:, t:t + 1], 1.0 / W, None, ALU.mult).then_inc(mean_ready, 1)
                dve.wait_ge(mean_ready, t + 1)
                nc.vector.tensor_scalar(av[:, t, :], av[:, t, :], mean[:, t:t + 1], None, ALU.subtract).then_inc(av_centred, 1)
            split(FIRST["a_v"] + 3)
            for t in range(TT):
                variance("ln", t, W)
            dve.wait_ge(const_loaded, 16 * 3)
            for t in range(TT):
                e = USE["cwf"] + t
                dve.wait_ge(c_copied, t + 1)
                nc.vector.tensor_scalar(wi[:, t, :], bank[e % 4][:, P:P + IDX_H], IDX_H ** -0.5, None, ALU.mult).then_inc(wi_ready, 1)
                nc.vector.tensor_tensor(fb[:, t, :], bank[e % 4][:, P + IDX_H:P + IDX_H + BH], bf[:, :], ALU.add)\
                    .then_inc(bank_free[e % 4], 1)
            split(FIRST["cwf"] + 2)
            for t in range(TT):
                dve.wait_ge(*freed(USE["cwf"] + t))
            nc.vector.scalar_tensor_tensor(out=fna[:, :, :], in0=fb[:, :, :], scalar=-1.0, in1=fb[:, :, :], op0=ALU.mult, op1=ALU.min).then_inc(f_abs, 1)
            for t in range(TT):
                variance("c", t, P)
            dve.wait_ge(xn_done, 3 * TT)
            for t in range(TT):
                scale_rows(c_sb[:, t, :], c_raw[:, t, :], "c", t, kvg[:, :]).then_inc(c_ready, 1)
            dve.wait_ge(gpost_loaded, 16 * 4)
            for t in range(TT):
                scale_rows(av[:, t, :], av[:, t, :], "ln", t, g_post[:, 0:W]).then_inc(ln_scaled, 1)
                dve.wait_ge(ln_scaled, t + 1)
                nc.vector.tensor_tensor(av[:, t, :], av[:, t, :], g_post[:, W:2 * W], ALU.add).then_inc(ln_done, 1)
            dve.wait_ge(f_log, 1)
            nc.vector.scalar_tensor_tensor(out=ls[:, :, :], in0=fb[:, :, :], scalar=0.0, in1=fl[:, :, :], op0=ALU.min, op1=ALU.subtract).then_inc(f_ls, 1)
            split(FIRST["qi"] + 2)
            dve.wait_ge(aconst_loaded, 32)
            for g in range(KW):
                n = PREP_MIX + g
                dve.wait_ge(prep_ready, n + 1)
                nc.vector.tensor_tensor(a_mix[:, g, :].rearrange("p (c t) -> p c t", t=P), sc[n % 2][:, :].rearrange("p (c t) -> p c t", t=P),
                                        a_bs[:, g:g + 1, :].broadcast_to([P, TT, P]), ALU.add).then_inc(prep_free, 1)
            split(FIRST["ki"] + 2)

            def small_products():
                dve.wait_ge(wi_ready, TT)
                for t in range(1, TT):
                    for h in range(IDX_H):
                        j = IDX_H * (t - 1) + h
                        dve.wait_ge(prep_free, PREP_IDX + j + 1)
                        r = relu_d[:, j % 2, 0:P * (t + 1)]
                        if h == 0:
                            ins = nc.vector.tensor_scalar(sel[t], r, wi[:, t, h:h + 1], None, ALU.mult)
                        else:
                            dve.wait_ge(score_added, j)
                            ins = nc.vector.scalar_tensor_tensor(out=sel[t], in0=r, scalar=wi[:, t, h:h + 1], in1=sel[t], op0=ALU.mult, op1=ALU.add)
                        ins.then_inc(score_added, 1)
                        yield

            def split_y(br, j, src):
                dve.wait_ge(y_rounded[br], j + 1)
                nc.vector.tensor_tensor(y_lo[slot[br]][:, j, :], src, y_hi[slot[br]][:, j, :].bitcast(F32), ALU.subtract).then_inc(y_split[br], 1)

            small = small_products()
            for j in range(KW):
                e = USE["a_uz"] + 2 * j
                step(small, 2 * len(IDX_AT) if j < TT - 1 else 0)
                dve.wait_ge(prep_free, PREP_MIX + j + 1)
                dve.wait_ge(bank_full, e + 1)
                nc.vector.tensor_tensor(a_mix[:, j, :], a_mix[:, j, :], bank[e % 4][:, :], ALU.mult).then_inc(bank_free[e % 4], 1)
                dve.wait_ge(*freed(e))
                dve.wait_ge(*freed(e + 1))
                if j >= 2:
                    dve.wait_ge(y_split["a"], j - 1)
                nc.vector.tensor_tensor(a_y[:, j % 2, :], a_mix[:, j, :], a_sz[:, j % 2, :], ALU.mult).then_inc(y_ready["a"], 1)
                split_y("a", j, a_y[:, j % 2, :])
                split(FIRST["a_uz"] + j + 2)
            dve.wait_ge(f_ls, 1)
            dve.wait_ge(score_added, IDX_H * (TT - 1))
            for h in range(BH):
                nc.vector.tensor_copy(lsx[:, h, :, :], ls[:, :, h:h + 1].broadcast_to([P, TT, P])).then_inc(lsx_ready, 1)

            def selection():
                n = 0
                for t in range(1, TT):
                    dve.wait_ge(score_masked, t)
                    for r in range(TOPK // 8):
                        nc.vector.max(top8[:, :], sel[t]).then_inc(topk_step, 1)
                        n += 1
                        dve.wait_ge(topk_step, n)
                        nc.vector.match_replace(sel[t], top8[:, :], sel[t], TAKEN).then_inc(topk_step, 1)
                        n += 1
                        dve.wait_ge(topk_step, n)
                        if r == TOPK // 8 - 1:
                            nc.vector.tensor_scalar(sel[t], sel[t], TAKEN, NEG, ALU.not_equal, ALU.mult).then_inc(topk_step, 1)
                            n += 1
                            dve.wait_ge(topk_step, n)
                        yield

            rounds = selection()
            for b in range(FIRST["d_q"], FIRST["c"]):
                step(rounds, 5)
                split(b + 2)

            def fox_out(u):
                if u % TT == TT - 1:
                    h = (u - U_FOX) // TT
                    dve.wait_ge(pv_done, u + 1)
                    if h == 0:
                        for c in range(KW):
                            dve.wait_ge(*freed(USE["d_z"] + c))
                    nc.vector.tensor_tensor(sz[:, h, :], ob[:, :], sz[:, h, :], ALU.mult).then_inc(o_free, 1)
                    split_y("d", h, sz[:, h, :])

            fox = attention(U_FOX, U_DSA, fox_out)
            parts = iter(())
            dve.wait_ge(prep_free, PREP_CT)
            nc.vector.memset(c_y[:, 0:2], 0.0).then_inc(conv_zero, 1)
            dve.wait_ge(conv_zero, 1)

            def convolution():
                def gate(j):
                    e = USE["c"] + 4 * j
                    dve.wait_ge(conv_step, 3 * j + 3)
                    dve.wait_ge(bank_full, e + 3)
                    nc.vector.tensor_tensor(c_acc, c_acc, bank[(e + 2) % 4][:, :], ALU.mult).then_inc(bank_free[(e + 2) % 4], 1)
                    yield
                    dve.wait_ge(*freed(e + 2))
                    dve.wait_ge(*freed(e + 3))
                    nc.vector.tensor_tensor(c_acc, c_acc, c_sz, ALU.mult).then_inc(y_ready["c"], 1)
                    yield
                    yield
                    split_y("c", j, c_acc)
                    yield

                for j in range(KW):
                    e = USE["c"] + 4 * j
                    if j:
                        yield from gate(j - 1)
                    else:
                        yield from iter((None,) * 4)
                    dve.wait_ge(*freed(e))
                    dve.wait_ge(bank_full, e + 2)
                    nc.vector.tensor_tensor(c_y[:, 2:2 + S], c_y[:, 2:2 + S], bank[(e + 1) % 4][:, :], ALU.mult).then_inc(bank_free[(e + 1) % 4], 1)
                    yield
                    dve.wait_ge(*freed(e + 1))
                    if j:
                        dve.wait_ge(y_split["c"], j)
                    nc.vector.tensor_scalar(c_acc, c_y[:, 0:S], convw[:, j, 0:1], None, ALU.mult).then_inc(conv_step, 1)
                    yield
                    for i in (1, 2):
                        dve.wait_ge(conv_step, 3 * j + i)
                        nc.vector.scalar_tensor_tensor(out=c_acc, in0=c_y[:, i:i + S], scalar=convw[:, j, i:i + 1], in1=c_acc, op0=ALU.mult,
                                                       op1=ALU.add).then_inc(conv_step, 1)
                        yield
                yield from gate(KW - 1)

            conv = convolution()
            for b in range(FIRST["c"], FIRST["b_q"]):
                step_between(fox, 2 * len(PAIR_AT), parts, conv)
                parts = split_parts(b + 2)
            step(parts, PARTS)
            step(conv, 4)
            step(fox, U_DSA)
            for b in range(FIRST["b_q"], FIRST["gate_a0"]):
                step(rounds, 2)
                split(b + 2)
            step(rounds, TT * TOPK)

            def dsa_out(u):
                if u % TT == TT - 1:
                    h = (u - U_DSA) // TT
                    dve.wait_ge(ydsa_ready, h + 1)
                    if h == 0:
                        for c in range(KW):
                            dve.wait_ge(*freed(USE["b_z"] + c))
                    nc.vector.tensor_tensor(sz[:, h, :], ob[:, :], sz[:, h, :], ALU.mult).then_inc(o_free, 1)

            def gates(br):
                r = ORDER.index(br)
                for half in range(2):
                    b, e = FIRST[f"branch_{br}{half}"], USE[f"branch_{br}{half}"]
                    for i in range(2):
                        parts = split_parts(b + i - 1) if i or half or r else iter(())
                        step_between(dsa, 2 * len(PAIR_AT), parts)
                        step(parts, PARTS)
                    split(b + 1)
                    for c in range(4):
                        j = 4 * half + c
                        dve.wait_ge(*freed(USE[f"gate_{br}{half}"] + c))
                        dve.wait_ge(bank_full, e + c + 1)
                        if r >= 1 and 4 * (2 * r + half) + c >= KD + 2:
                            dve.wait_ge(gate_add, KD * (r - 1) + j - 1)
                        dst = merged[:, j, :] if r == 0 else tmp[:, c % 2, :]
                        nc.vector.tensor_tensor(dst, sig[:, c, :], bank[(e + c) % 4][:, :], ALU.mult).then_inc(bank_free[(e + c) % 4], 1)
                        dve.wait_ge(*freed(e + c))
                        if r:
                            nc.vector.tensor_tensor(merged[:, j, :], merged[:, j, :], tmp[:, c % 2, :], ALU.add).then_inc(gate_add, 1)
                    if br == ORDER[-1]:
                        for j in range(4 * half, 4 * half + 4):
                            dve.wait_ge(merged_rounded, j + 1)
                            nc.vector.tensor_tensor(mT_lo[:, j, :], merged[:, j, :], mT_hi[:, j, :].bitcast(F32), ALU.subtract).then_inc(merged_split, 1)

            dsa = attention(U_DSA, N_UNITS, dsa_out)
            gates("a")
            gates("d")
            for j in range(BH):
                split_y("b", j, sz[:, j, :])
            gates("c")
            gates("b")
            split(FIRST["out0"] + 1)
            for h in range(2):
                split(FIRST[f"out{h}"] + 2)
                dve.wait_ge(x2_loaded, 16)
                for t in range(TT):
                    e = USE[f"out{h}"] + t
                    dve.wait_ge(bank_full, e + 1)
                    part = x_sb[:, t, W * h:W * h + W]
                    nc.vector.tensor_tensor(part, part, bank[e % 4][:, :], ALU.add).then_inc(bank_free[e % 4], 1)
                    if h == 0:
                        begin_variance("final", t)
                    else:
                        dve.wait_ge(gpost_loaded, 16 * 5)
                        variance("final", t, D)
                        scale_rows(m_sb[:, t, :], x_sb[:, t, :], "final", t, g_post[:, :]).then_inc(out_ready, 1)
                split(FIRST[f"out{h}"] + 3)

        @block.tensor
        def _(pe):
            def product(ps, hi_l, lo_l, hi_r, lo_r, first, last):
                nc.tensor.matmul(ps, hi_l, hi_r, start=first, stop=False)
                nc.tensor.matmul(ps, hi_l, lo_r, start=False, stop=False)
                return nc.tensor.matmul(ps, lo_l, hi_r, start=False, stop=last)

            def open_bank(e):
                if e >= 4:
                    pe.wait_ge(bank_free[e % 4], e // 4)

            def feature_chunk(b, e, c, wid, kc, rhs_hi, rhs_lo, tok=slice(0, S), full=True, steps=None, at=()):
                for k in range(kc):
                    w = slice(wid * k + P * c, wid * k + P * c + P)
                    last = product(bank[e % 4][:, tok], w_hi[b % RING][:, w], w_lo[b % RING][:, w], rhs_hi[:, k, tok], rhs_lo[:, k, tok],
                                   k == 0, k == kc - 1)
                    if full and k == kc - 1:
                        last.then_inc(bank_full, 1)
                    if k in at:
                        step(steps, 1)

            def feature_major(b, e, chunks, kc, rhs_hi, rhs_lo, steps=None, at=((),) * 4):
                pe.wait_ge(w_split, b + 1)
                for c in range(chunks):
                    open_bank(e + c)
                    feature_chunk(b, e + c, c, P * chunks, kc, rhs_hi, rhs_lo, steps=steps, at=at[c])

            def token_major(b, e, counts, wid, lhs_hi, lhs_lo, before=None, after=None):
                k0, total = 0, sum(counts)
                for i, kc in enumerate(counts):
                    for t in range(TT):
                        if i == 0:
                            open_bank(e + t)
                        if before:
                            before(i, t)
                        if t == 0:
                            pe.wait_ge(w_split, b + i + 1)
                        for k in range(kc):
                            w = slice(wid * k, wid * k + wid)
                            tok = slice(P * t, P * t + P)
                            last = product(bank[(e + t) % 4][:, 0:wid], lhs_hi[:, k0 + k, tok], lhs_lo[:, k0 + k, tok], w_hi[(b + i) % RING][:, w],
                                           w_lo[(b + i) % RING][:, w], k0 + k == 0, k0 + k == total - 1)
                            if k == kc - 1 and i == len(counts) - 1:
                                last.then_inc(bank_full, 1)
                            if k == kc - 1 and i < len(counts) - 1 and t == TT - 1:
                                last.then_inc(w_used, 1)
                            if after:
                                after(i, t)
                    k0 += kc

            def transpose_tile(name, t):
                T = TT * pre_use[name] + t
                pe.wait_ge(xn_done, T + 1)
                for j in range(2):
                    q = 2 * T + j
                    if q >= 4:
                        pe.wait_ge(xT_split, q - 3)
                    for i in range(4):
                        last = nc.tensor.transpose(xp[q % 4][:, P * i:P * i + P], xn[:, t % 2, P * (4 * j + i):P * (4 * j + i) + P], ident[:, :])
                    last.then_inc(xpose_done, 1)

            def tiles_ready(name, t):
                pe.wait_ge(xT_split, 2 * (TT * pre_use[name] + t))

            def as_normed(name):
                def before(i, t):
                    if i == 0:
                        if t == 0:
                            transpose_tile(name, 0)
                        if t < TT - 1:
                            transpose_tile(name, t + 1)
                        tiles_ready(name, t + 1)
                return before

            def attention(lo, hi, operands, group, begin, finish):
                for i in range(lo, hi + 6):
                    if i < hi:
                        kind, h, t = UNITS[i]
                        score_parts, _ = operands(h, t)
                        if i >= 2:
                            if UNITS[i - 2][0] == "fox":
                                pe.wait_ge(sc_free, i - 2 - U_FOX + 1)
                            else:
                                pe.wait_ge(s_ready, i - 1)
                        for n, (q, k) in enumerate(score_parts):
                            last = nc.tensor.matmul(sc[i % 2][:, 0:P * (t + 1)], q, k, start=n == 0, stop=n == len(score_parts) - 1)
                        last.then_inc(sc_ready, 1)
                    if lo <= i - 2 < hi:
                        u = i - 2
                        t = UNITS[u][2]
                        pe.wait_ge(pn_ready, u + 1)
                        if u >= 1:
                            pe.wait_ge(pT_ready, u)
                        for j in range(t + 1):
                            last = nc.tensor.transpose(tp[:, P * j:P * j + P], s_ring[:, u % 4, P * j:P * j + P], ident[:, :])
                        last.then_inc(tp_ready, 1)
                    if lo <= i - 5 < hi and (i - 5 - lo) % group == group - 1:
                        finish((i - 5 - lo) // group)
                    if lo <= i - 4 < hi:
                        u = i - 4
                        _, h, t = UNITS[u]
                        _, (vals, dst) = operands(h, t)
                        pe.wait_ge(pT_ready, u + 1)
                        if (u - lo) % group == 0:
                            begin((u - lo) // group)
                        for j in range(t + 1):
                            last = nc.tensor.matmul(dst, vals(j), pT[:, u % 3, P * j:P * j + P], start=j == 0, stop=j == t)
                        last.then_inc(pv_done, 1)
                    yield

            pe.wait_ge(ident_made, 2)
            for h in range(2):
                token_major(FIRST[f"v{h}"], USE[f"v{h}"], (4, 4), W, xT_hi, xT_lo, as_normed("pre0") if h == 0 else None)

            def mha_operands(h, t):
                i, c = h // QK_HEADS, h % QK_HEADS
                if t == 0 and c == 0:
                    pe.wait_ge(first_split, 2 * i + 2)
                if t == 0 and c == 1:
                    pe.wait_ge(*freed(USE[f"qk{i}"]))
                    pe.wait_ge(*freed(USE[f"qk{i}"] + 1))
                rows = slice(HD * c, HD * c + HD)
                tok, keys = slice(P * t, P * t + P), slice(0, P * (t + 1))
                return (((q_st[i % 2][:, c, tok], k_st[i % 2][:, c, keys]), (q_st[i % 2][rows, c, tok], k_rest[i % 2][rows, keys])),
                        (lambda j: v_sb[:, j, HD * h:HD * h + HD], ob[rows, tok]))

            def mha_begin(g):
                if g == 0:
                    for e in range(USE["v0"], USE["qk0"]):
                        pe.wait_ge(*freed(e))
                else:
                    pe.wait_ge(o_free, g)

            mha = attention(0, U_FOX, mha_operands, 2 * TT, mha_begin, lambda g: None)
            for i in range(HEADS // QK_HEADS):
                at = (((), ()), (MHA_FIRST_AT, MHA_AT), (MHA_AT, MHA_AT))[min(i, 2)]
                feature_major(FIRST[f"qk{i}"], USE[f"qk{i}"], 2, KD, xT_hi, xT_lo, mha, at)

            def heads_ready(i, t):
                if t == 0:
                    pe.wait_ge(o_free, HEADS // 4 * (i + 1))

            def last_heads(i, t):
                if i == 0:
                    step(mha, 1)

            token_major(FIRST["wo0"], USE["wo0"], (4, 4), W, oT_hi, oT_lo, heads_ready, last_heads)
            token_major(FIRST["wo1"], USE["wo1"], (4, 4), W, oT_hi, oT_lo)

            for half in range(2):
                tok = slice(S // 2 * half, S // 2 * half + S // 2)
                for i in range(2):
                    b, e = FIRST["gu0"] + i, USE["gu0"] + 2 * i
                    if half == 0:
                        transpose_tile("pre1", 2 * i)
                        if i == 0:
                            transpose_tile("pre1", 1)
                            tiles_ready("pre1", 2)
                        pe.wait_ge(w_split, b + 1)
                    elif i == 0:
                        tiles_ready("pre1", TT)
                    for c in range(2):
                        if half == 0:
                            if i == c == 1:
                                transpose_tile("pre1", 3)
                            open_bank(e + c)
                        feature_chunk(b, e + c, c, 2 * P, KD, xT_hi, xT_lo, tok, full=half == 1)
            for f in range(2):
                for i in range(2 * (1 - f), FH):
                    feature_major(FIRST[f"gu{f}"] + i, USE[f"gu{f}"] + 2 * i, 2, KD, xT_hi, xT_lo)
                def gated_ready(i, t):
                    if t == 0:
                        pe.wait_ge(act_split, FH * f + min(FH, 4 * (i + 1)))

                for h in range(2):
                    token_major(FIRST[f"down{f}{h}"], USE[f"down{f}{h}"], (4, 4, 3), W, act_hi, act_lo, gated_ready)

            token_major(FIRST["a_v"], USE["a_v"], (4, 4), W, xT_hi, xT_lo, as_normed("pre2"))
            token_major(FIRST["cwf"], USE["cwf"], (KD,), P + IDX_H + BH, xT_hi, xT_lo)
            feature_major(FIRST["qi"], USE["qi"], 2, KD, xT_hi, xT_lo)

            def small_products():
                pe.wait_ge(mix_masked, 1)
                pe.wait_ge(ln_done, TT)
                for g in range(KW):
                    n = PREP_MIX + g
                    if g >= 2:
                        pe.wait_ge(prep_free, n - 1)
                    for t in range(TT):
                        last = nc.tensor.matmul(sc[n % 2][:, P * t:P * t + P], av[:, t, P * g:P * g + P], a_ws[:, g, :], start=True, stop=True)
                    last.then_inc(prep_ready, 1)
                    yield
                pe.wait_ge(prep_free, PREP_CT)
                for t in range(TT):
                    pe.wait_ge(c_ready, t + 1)
                    last = nc.tensor.transpose(sc[PREP_CT % 2][:, P * t:P * t + P], c_sb[:, t, :], ident[:, :])
                last.then_inc(prep_ready, 1)
                yield
                for c in range(2):
                    pe.wait_ge(*freed(USE["qi"] + c))
                pe.wait_ge(*freed(USE["ki"]))
                for t in range(1, TT):
                    for h in range(IDX_H):
                        n = PREP_IDX + IDX_H * (t - 1) + h
                        pe.wait_ge(prep_free, n - 1)
                        rows = slice(IDX_D * (h % 2), IDX_D * (h % 2) + IDX_D)
                        nc.tensor.matmul(sc[n % 2][:, 0:P * (t + 1)], qi[rows, h // 2, P * t:P * t + P], ki[rows, 0:P * (t + 1)], start=True,
                                         stop=True).then_inc(prep_ready, 1)
                        yield
                pe.wait_ge(tri_made, 2)
                for h in range(BH):
                    n = PREP_CUM + h
                    pe.wait_ge(lsx_ready, h + 1)
                    pe.wait_ge(prep_free, n - 1)
                    for t in range(TT):
                        last = nc.tensor.matmul(sc[n % 2][:, P * t:S], lsx[:, h, t, :], tri[:, 0:S - P * t], start=t == 0, stop=t == TT - 1)
                    last.then_inc(prep_ready, 1)
                    yield
                n = PREP_CUM + BH
                pe.wait_ge(prep_free, n - 1)
                for t in range(TT):
                    for j in range(t + 1):
                        ones = tri[:, 0:P] if j == t else tri[:, P:2 * P]
                        last = nc.tensor.matmul(sc[n % 2][:, BH * t:BH * t + BH], ones, ls[:, j, :], start=j == 0, stop=j == t)
                last.then_inc(prep_ready, 1)
                yield
                pe.wait_ge(latent_loaded, 32)
                for h in range(BH):
                    n = PREP_QLAT + h
                    pe.wait_ge(*freed(USE["b_q"] + h))
                    pe.wait_ge(prep_free, n - 1)
                    nc.tensor.matmul(sc[n % 2][:, :], wukT[:, h, :], bq[:, h, :], start=True, stop=True).then_inc(prep_ready, 1)
                    yield

            small = small_products()
            feature_major(FIRST["ki"], USE["ki"], 1, KD, xT_hi, xT_lo, small, (MIX_AT,))
            for j in range(KW):
                at = (IDX_AT if j else IDX_FIRST_AT, IDX_AT) if j < TT - 1 else ((), ())
                feature_major(FIRST["a_uz"] + j, USE["a_uz"] + 2 * j, 2, KD, xT_hi, xT_lo, small, at)
            for i in range(2):
                feature_major(FIRST["d_q"] + i, USE["d_q"] + 2 * i, 2, KD, xT_hi, xT_lo)
            for i in range(2):
                feature_major(FIRST["d_k"] + i, USE["d_k"] + 2 * i, 2, KD, xT_hi, xT_lo, small, (ONE_AT if i else PAIR_AT, ONE_AT))
            token_major(FIRST["d_v"], USE["d_v"], (4, 4), W, xT_hi, xT_lo)
            for i in range(2):
                feature_major(FIRST["d_z"] + i, USE["d_z"] + 2 * i, 2, KD, xT_hi, xT_lo)

            def fox_operands(h, t):
                return (((dqk[:, h, P * t:P * t + P], dqk[:, BH + h, 0:P * (t + 1)]),),
                        (lambda j: dv[:, j, BD * h:BD * h + BD], ob[:, P * t:P * t + P]))

            for e in range(USE["d_z"], USE["d_z"] + 4):
                pe.wait_ge(*freed(e))
            pe.wait_ge(prep_free, PREP_QLAT)

            fox = attention(U_FOX, U_DSA, fox_operands, TT, lambda g: pe.wait_ge(o_free, O_FOX + g), lambda g: None)
            for i in range(2 * KW):
                feature_major(FIRST["c"] + i, USE["c"] + 2 * i, 2, KD, xT_hi, xT_lo, fox, (PAIR_AT, PAIR_AT))
            step(fox, U_DSA)

            for i in range(2):
                feature_major(FIRST["b_q"] + i, USE["b_q"] + 2 * i, 2, KD, xT_hi, xT_lo)
            for i in range(2):
                feature_major(FIRST["b_z"] + i, USE["b_z"] + 2 * i, 2, KD, xT_hi, xT_lo, small, (ONE_AT, ONE_AT))

            def dsa_operands(h, t):
                return (((qlat[:, h, P * t:P * t + P], cT[:, 0:P * (t + 1)]),), (lambda j: c_sb[:, j, :], ob[:, P * t:P * t + P]))

            def dsa_finish(g):
                pe.wait_ge(olat_ready, g + 1)
                nc.tensor.matmul(ob[:, :], wuv[:, g, :], olat, start=True, stop=True).then_inc(ydsa_ready, 1)

            def gates(br):
                ys = slot[br]
                for half in range(2):
                    for i in range(2):
                        feature_major(FIRST[f"gate_{br}{half}"] + i, USE[f"gate_{br}{half}"] + 2 * i, 2, KD, xT_hi, xT_lo, dsa, (PAIR_AT, PAIR_AT))
                    pe.wait_ge(y_split[br], KW)
                    feature_major(FIRST[f"branch_{br}{half}"], USE[f"branch_{br}{half}"], 4, KW, y_hi[ys], y_lo[ys])

            pe.wait_ge(prep_free, N_PREP)
            dsa = attention(U_DSA, N_UNITS, dsa_operands, TT, lambda g: pe.wait_ge(o_free, O_DSA + g), dsa_finish)
            for br in ORDER:
                gates(br)

            def merged_ready(i, t):
                if t == 0:
                    pe.wait_ge(merged_split, 4 * (i + 1))

            for h in range(2):
                token_major(FIRST[f"out{h}"], USE[f"out{h}"], (4, 4), W, mT_hi, mT_lo, merged_ready)


def pack_rows(w, rows, cols):
    part = w[rows][:, cols]
    part = part.reshape(-1, P, part.shape[1]).transpose(1, 0, 2).reshape(P, -1)
    out = np.zeros((P, BLK), w.dtype)
    out[:, :part.shape[1]] = part
    return out


def weight_stream(a):
    blocks = []
    r = lambda *x: np.concatenate([np.arange(*p) for p in x])
    w_qkv, w_in = a["w_qkv"][0], a["w_in_2"][0]
    every = np.arange(D)

    def token_blocks(w, rows, cols, step=4):
        for k in range(0, len(rows), step * P):
            blocks.append(pack_rows(w, rows[k:k + step * P], cols))

    for h in range(2):
        token_blocks(w_qkv, every, r((2 * D + W * h, 2 * D + W * h + W)))
    for i in range(HEADS // QK_HEADS):
        blocks.append(pack_rows(w_qkv, every, r((P * i, P * i + P), (D + P * i, D + P * i + P))))
    for h in range(2):
        token_blocks(a["w_o"][0], every, r((W * h, W * h + W)))
    gu = np.stack([a["w_gate"][0].reshape(D, FC, P), a["w_up"][0].reshape(D, FC, P)], 2).reshape(D, 2 * FF)
    for f in range(2):
        for i in range(FH * f, FH * f + FH):
            blocks.append(pack_rows(gu, every, r((256 * i, 256 * i + 256))))
        for h in range(2):
            token_blocks(a["w_down"][0], np.arange(FH * f * P, FH * (f + 1) * P), r((W * h, W * h + W)))
    col = {n: np.arange(*c) for n, c in COL.items()}

    def cols(*names):
        c = np.concatenate([col[n] for n in names])
        for i in range(0, len(c), 256):
            blocks.append(pack_rows(w_in, every, c[i:i + 256]))

    def pairs(x, y, j):
        blocks.append(pack_rows(w_in, every, np.concatenate([col[x][P * j:P * j + P], col[y][P * j:P * j + P]])))

    token_blocks(w_in, every, col["a_v"])
    cols("b_c", "b_wi", "d_f")
    cols("b_qi")
    cols("b_ki", "b_ki")
    for j in range(KW):
        pairs("a_u", "a_z", j)
    cols("d_q")
    cols("d_k")
    token_blocks(w_in, every, col["d_v"])
    cols("d_z")
    for j in range(KW):
        pairs("c_c", "c_x", j)
        pairs("c_b", "c_z", j)
    cols("b_q")
    cols("b_z")
    for br in ORDER:
        n = BRANCH[br]
        for half in range(2):
            for i in range(2):
                at = col["gates"][0] + D * n + W * half + 256 * i
                blocks.append(pack_rows(w_in, every, r((at, at + 256))))
            blocks.append(pack_rows(a["w_branch_2"][0, n], np.arange(W), r((W * half, W * half + W))))
    for h in range(2):
        token_blocks(a["w_out_2"][0], every, r((W * h, W * h + W)))
    assert len(blocks) == N_BLOCKS, (len(blocks), N_BLOCKS)
    return np.stack(blocks)


def kernel(**inputs):
    import concourse.bacc as bacc
    from concourse.bass_utils import run_bass_kernel_spmd

    a = {k: np.asarray(v) for k, v in inputs.items()}
    clip = np.clip(P + np.arange(P)[:, None] - np.arange(BIAS_W)[None, :], 1 - CHUNK, REL_CLIP) + CHUNK - 1
    arrays = {
        "weights": weight_stream(a),
        "x": a["x"][0],
        "bias": a["rel_bias"][0][:, clip],
        "g_pre_mix": a["g_pre_mix"][0], "g_post_mix": a["g_post_mix"][0],
        "g_pre_ffn": a["g_pre_ffn"][0], "g_post_ffn": a["g_post_ffn"][0],
        "norm_g": a["norm_g_2"][0], "final_g": a["final_g_2"],
        "ln_g": a["gm_ln_g_2"][0], "ln_b": a["gm_ln_b_2"][0],
        "gm_b": a["gm_b_s_2"][0], "gm_wT": a["gm_w_s_2"][0].transpose(2, 0, 1),
        "kvg": a["dsa_kv_g_2"][0], "bf": a["fox_b_f_2"][0],
        "wukT": a["dsa_w_uk_2"][0].transpose(2, 0, 1), "wuv": a["dsa_w_uv_2"][0].transpose(1, 0, 2),
        "convw": a["conv_w_2"][0].reshape(3, KW, P).transpose(2, 1, 0),
    }
    nc = bacc.Bacc("TRN2", target_bir_lowering=False, num_devices=1)
    feeds, dram = {}, {}
    for name, v in arrays.items():
        v = np.ascontiguousarray(v)
        feeds[f"in_{name}"] = v
        dram[name] = nc.dram_tensor(f"in_{name}", v.shape, mybir.dt.from_np(v.dtype), kind="ExternalInput").ap()
    out = nc.dram_tensor("out_0", (S, D), F32, kind="ExternalOutput").ap()
    build(nc, dram, out)
    r = run_bass_kernel_spmd(nc, [feeds], core_ids=[0])
    return r.results[0]["out_0"].reshape(1, S, D)
```

```python
from contextlib import ExitStack

import numpy as np

import concourse.bass as bass
from concourse import mybir

F32 = mybir.dt.float32
F32R = mybir.dt.float32r
ACT = mybir.ActivationFunctionType
ALU = mybir.AluOpType
AX_X = mybir.AxisListType.X

P = 128
S = 512
TT = S // P
D = 1024
KD = D // P
HEADS, HD = 16, 64
CHUNK = 64
REL_CLIP = 128
BIAS_W = 2 * P
FF = 2816
FC = FF // P
FH = FC // 2
W = 512
KW = W // P
BH, BD = 4, 128
IDX_H, IDX_D = 4, 64
TOPK = min(256, S // 4)
N_BRANCH = 4
EPS = 1e-6
NEG = -1e30
TAKEN, ACAUSAL = -3.4e38, -3.0e38
BLK = 2048
RING = 2
PARTS = 4

_SPLITS = [("a_u", W), ("a_v", W), ("a_z", W), ("b_q", W), ("b_c", P), ("b_qi", IDX_H * IDX_D), ("b_ki", IDX_D),
           ("b_wi", IDX_H), ("b_z", W), ("c_b", W), ("c_c", W), ("c_x", W), ("c_z", W), ("d_q", W), ("d_k", W),
           ("d_v", W), ("d_f", BH), ("d_z", W), ("gates", N_BRANCH * D)]
COL = {}
_at = 0
for _name, _width in _SPLITS:
    COL[_name] = (_at, _at + _width)
    _at += _width

ORDER = "adcb"
BRANCH = {"a": 0, "b": 1, "c": 2, "d": 3}


FEATURE_MAJOR = {"b_q", "d_q", "d_k", "d_z", "b_z"} | {f"gate_{br}{i}" for br in ORDER for i in range(2)}
QK_HEADS = P // HD
GU_LOOP = ((2, 3), (0, 4))
MHA_AT, MHA_FIRST_AT, MIX_AT, IDX_FIRST_AT, IDX_AT, PAIR_AT, ONE_AT = (2, 4, 6, 7), (3, 5, 7), (4, 5, 6, 7), (0, 3, 6), (0, 4), (0, 4), (0,)


def plan():
    first, use, done, gains, n, e, open_blocks = {}, {}, [], [], 0, 0, 0

    def add(name, blocks, uses, norm=None):
        nonlocal n, e, open_blocks
        first[name], use[name] = n, e
        for i in range(blocks):
            token = uses == TT and blocks == 2 and name not in FEATURE_MAJOR
            gains.append(None if norm is None else (norm, KD // 2 * i, W) if token else (norm, 0, BLK // KD))
            if uses % blocks or (token and i < blocks - 1):
                open_blocks += 1
                done.append(("w_used", open_blocks))
            else:
                done.append(("bank_full", e + uses * (i + 1) // blocks))
        if done[-1][0] == "w_used":
            open_blocks -= 1
            done[-1] = ("bank_full", e + uses)
        n += blocks
        e += uses

    for h in range(2):
        add(f"v{h}", 2, TT)
    for i in range(HEADS // QK_HEADS):
        add(f"qk{i}", 1, 2)
    for h in range(2):
        add(f"wo{h}", 2, TT)
    for f in range(2):
        add(f"gu{f}", FH, 2 * FH, 0)
        for h in range(2):
            add(f"down{f}{h}", 3, TT)
    add("a_v", 2, TT, 1)
    add("cwf", 1, TT, 1)
    add("qi", 1, 2, 1)
    add("ki", 1, 1, 1)
    add("a_uz", 4, 8, 1)
    add("d_q", 2, 4, 1)
    add("d_k", 2, 4, 1)
    add("d_v", 2, TT, 1)
    add("d_z", 2, 4, 1)
    add("c", 8, 16, 1)
    add("b_q", 2, 4, 1)
    add("b_z", 2, 4, 1)
    for br in ORDER:
        for half in range(2):
            add(f"gate_{br}{half}", 2, 4, 1)
            add(f"branch_{br}{half}", 1, 4)
    for h in range(2):
        add(f"out{h}", 2, TT)
    return first, use, done, gains


FIRST, USE, DONE, GAINS = plan()
N_BLOCKS = len(DONE)

UNITS = [("mha", h, t) for h in range(HEADS) for t in range(TT)]
UNITS += [("fox", h, t) for h in range(BH) for t in range(TT)]
UNITS += [("dsa", h, t) for h in range(BH) for t in range(TT)]
U_FOX = HEADS * TT
U_DSA = U_FOX + BH * TT
N_UNITS = len(UNITS)

NORMS = [("pre0", t) for t in range(TT)]
for _r in (1, 2):
    _seq = [(f"post{_r}", 0)]
    for _t in range(1, TT):
        _seq += [(f"post{_r}", _t), (f"pre{_r}", _t - 1)]
    NORMS += _seq + [(f"pre{_r}", TT - 1)]
NORMS += [("ln", t) for t in range(TT)] + [("c", t) for t in range(TT)] + [("final", t) for t in range(TT)]
NCOL = {n: i for i, n in enumerate(NORMS)}

SQUARES = []
for _name, _t in NORMS:
    if _name in ("post1", "post2", "final") and _t == 0:
        SQUARES += [(_name + "a", t) for t in range(TT)]
    SQUARES.append((_name + "b" if _name in ("post1", "post2", "final") else _name, _t))
SCOL = {n: i for i, n in enumerate(SQUARES)}


def build(nc, dram, out):
    ctx = ExitStack()
    with ctx:
        def sb(name, shape, dt=F32):
            return ctx.enter_context(nc.sbuf_tensor(name, shape, dt))

        def sem(name):
            return ctx.enter_context(nc.semaphore(name))

        w_raw = [sb(f"w_raw{i}", [P, BLK]) for i in range(RING)]
        w_hi = [sb(f"w_hi{i}", [P, BLK], F32R) for i in range(RING)]
        w_lo = [sb(f"w_lo{i}", [P, BLK], F32R) for i in range(RING)]
        xT_hi = sb("xT_hi", [P, KD, S], F32R)
        xT_lo = sb("xT_lo", [P, KD, S], F32R)
        act_hi = sb("act_hi", [P, 3 * KW, S], F32R)
        act_lo = sb("act_lo", [P, 3 * KW, S], F32R)
        x_sb = sb("x_sb", [P, TT, D])
        g_first = sb("g_first", [P, D])
        gcol = sb("gcol", [P, 2, KD])
        g_post = sb("g_post", [P, D])
        arena = sb("arena", [P, 13576])
        ident = sb("ident", [P, P])
        cmask = sb("cmask", [P, P])
        kvg = sb("kvg", [P, P])
        convw = sb("convw", [P, KW, 3])
        bf = sb("bf", [P, BH])
        minus_half = sb("minus_half", [P, 1])
        sumsq = sb("sumsq", [P, len(SQUARES)])
        var = sb("var", [P, len(NORMS)])
        rstd = sb("rstd", [P, len(NORMS)])
        mean = sb("mean", [P, TT])
        negmax = sb("negmax", [P, 4])
        psums = sb("psums", [P, 4])
        rinv = sb("rinv", [P, 4])
        wi = sb("wi", [P, TT, IDX_H])
        fb = sb("fb", [P, TT, BH])
        fna = sb("fna", [P, TT, BH])
        fl = sb("fl", [P, TT, BH])
        ls = sb("ls", [P, TT, BH])
        cumq = sb("cumq", [P, TT, BH])
        top8 = sb("top8", [P, 8])

        def view(at, *shape):
            n = int(np.prod(shape))
            v = arena[:, at:at + n]
            if len(shape) == 2:
                v = v.rearrange("p (a b) -> p a b", b=shape[1])
            if len(shape) == 3:
                v = v.rearrange("p (a b c) -> p a b c", b=shape[1], c=shape[2])
            return v

        SOFT = 9992
        q_st = [act_hi[:, KD + 2 * i:KD + 2 * i + 2, :] for i in range(2)]
        k_st = [act_lo[:, KD + 2 * i:KD + 2 * i + 2, :] for i in range(2)]
        k_rest = [act_lo[:, KD - 1, :], act_hi[:, KD - 1, :]]
        v_sb = x_sb
        biases = view(8192, 4, BIAS_W)
        s_ring = view(SOFT, 4, S)
        pT = view(SOFT + 4 * S, 3, S)
        oT_hi, oT_lo = act_hi[:, 0:KD, :], act_lo[:, 0:KD, :]
        m_sb = view(0, TT, D)
        xn = view(4096, 2, D)
        junk = view(6144, D)
        sg = view(7168, 2, S)
        a_sb = view(8192, 2, S)
        av = view(0, TT, W)
        a_mix = view(2048, KW, S)
        a_sz = view(4096, 2, S)
        a_y = view(4096 + 2 * S, 2, S)
        qi_st, ki_st, ki_rest = act_hi[:, KW:KW + IDX_H, :], act_hi[:, 2 * KW, :], act_lo[:, 2 * KW, :]
        a_ws = view(6144 + 3 * S, KW, P)
        sel_at = [8192 + P * (t * (t + 1) // 2) for t in range(TT)]
        sel = [view(sel_at[t], P * (t + 1)) for t in range(TT)]
        a_bs = view(9472, KW, P)
        q_junk = view(SOFT, TT, W)
        relu_d = view(SOFT, 2, S)
        cum_rows = view(SOFT + 2 * S, S)[0:BH, :]
        c_raw = view(SOFT + 4 * S, TT, P)
        tri = view(SOFT + 5 * S, S)
        c_sb = g_first[:, 0:S].rearrange("p (a b) -> p a b", b=P)
        cT = g_first[:, S:2 * S]
        dqk = x_sb[:, :, :].rearrange("p t (a s) -> p (t a) s", s=S)
        dv = view(2048, TT, W)
        negcumk = view(4096, BH, S)
        sz = view(6144, KW, S)
        c_acc = view(0, S)
        c_sz = view(S, S)
        c_y = view(9472, S + 2)
        qlat = view(0, BH, S)
        bq = view(4096, KW, S)
        wukT = g_post[:, 0:S].rearrange("p (a b) -> p a b", b=P)
        wuv = g_post[:, S:2 * S].rearrange("p (a b) -> p a b", b=P)
        olat = view(4096 + 2 * S, S)
        merged = dqk
        sig = view(2048, 4, S)
        tmp = view(4096, 2, S)
        slot = {br: i % 3 for i, br in enumerate(ORDER)}
        y_hi = [act_hi[:, KW * i:KW * i + KW, :] for i in range(3)]
        y_lo = [act_lo[:, KW * i:KW * i + KW, :] for i in range(3)]
        pair = (slice(0, HD), slice(HD, P))
        mT_hi, mT_lo = act_hi[:, KW:3 * KW, :], act_lo[:, KW:3 * KW, :]

        bank = [ctx.enter_context(nc.psum_tensor(f"bank{i}", [P, S], F32)) for i in range(4)]
        sc = [ctx.enter_context(nc.psum_tensor(f"sc{i}", [P, S], F32)) for i in range(2)]
        tp = ctx.enter_context(nc.psum_tensor("tp", [P, S], F32))
        ob = ctx.enter_context(nc.psum_tensor("ob", [P, S], F32))

        xp = [sc[0], sc[1], tp, ob]

        cum_dram = nc.dram_tensor("cum_dram", (BH, S), F32, kind="Internal").ap()
        x2_dram = nc.dram_tensor("x2_dram", (S, D), F32, kind="Internal").ap()

        w_loaded = [sem(f"w_loaded{i}") for i in range(RING)]
        w_rounded, w_split, w_used = sem("w_rounded"), sem("w_split"), sem("w_used")
        bank_full = sem("bank_full")
        bank_free = [sem(f"bank_free{i}") for i in range(4)]
        x_tile = [sem(f"x_tile{t}") for t in range(TT)]
        x_loaded = sem("x_loaded")
        gains_loaded = sem("gains_loaded")
        gcol_loaded = sem("gcol_loaded")
        gpost_loaded = sem("gpost_loaded")
        const_loaded = sem("const_loaded")
        x2_spilled, x2_loaded, aconst_loaded, out_stored = sem("x2_spilled"), sem("x2_loaded"), sem("aconst_loaded"), sem("out_stored")
        latent_loaded = sem("latent_loaded")
        cum_stored, cum_loaded = sem("cum_stored"), sem("cum_loaded")
        qi_rounded, ki_rounded = sem("qi_rounded"), sem("ki_rounded")
        masks_made, ident_made, tri_made = sem("masks_made"), sem("ident_made"), sem("tri_made")
        sumsq_done, var_begun, var_done, rstd_done = sem("sumsq_done"), sem("var_begun"), sem("var_done"), sem("rstd_done")
        gained, x_updated, xn_done = sem("gained"), sem("x_updated"), sem("xn_done")
        xpose_done, xT_rounded, xT_split = sem("xpose_done"), sem("xT_rounded"), sem("xT_split")
        bias_loaded = [sem(f"bias_loaded{i}") for i in range(4)]
        bias_ready = sem("bias_ready")
        q_rounded, k_rounded, first_split = sem("q_rounded"), sem("k_rounded"), sem("first_split")
        sc_ready, sc_free, part_done, s_ready = sem("sc_ready"), sem("sc_free"), sem("part_done"), sem("s_ready")
        max_ready, p_ready, rinv_ready, pn_ready = sem("max_ready"), sem("p_ready"), sem("rinv_ready"), sem("pn_ready")
        tp_ready, pT_ready, pv_done = sem("tp_ready"), sem("pT_ready"), sem("pv_done")
        o_free, o_rounded = sem("o_free"), sem("o_rounded")
        olat_ready, ydsa_ready = sem("olat_ready"), sem("ydsa_ready")
        act_rounded, act_split = sem("act_rounded"), sem("act_split")
        c_copied, wi_ready, f_abs, f_exp, f_log, f_ls = (sem(n) for n in ("c_copied", "wi_ready", "f_abs", "f_exp", "f_log", "f_ls"))
        c_ready, prep_ready, prep_free = sem("c_ready"), sem("prep_ready"), sem("prep_free")
        score_added, score_masked, topk_step = sem("score_added"), sem("score_masked"), sem("topk_step")
        y_ready = {br: sem(f"y_ready_{br}") for br in "ac"}
        y_rounded = {br: sem(f"y_rounded_{br}") for br in ORDER}
        y_split = {br: sem(f"y_split_{br}") for br in ORDER}
        gate_add = sem("gate_add")
        merged_rounded, merged_split = sem("merged_rounded"), sem("merged_split")
        mean_ready, av_centred, ln_scaled, ln_done = (sem(n) for n in ("mean_ready", "av_centred", "ln_scaled", "ln_done"))
        mix_masked = sem("mix_masked")
        conv_step, conv_zero = sem("conv_step"), sem("conv_zero")
        out_ready = sem("out_ready")

        def freed(e, turn=0):
            return bank_free[e % 4], e // 4 + 1 + turn

        def block_done(eng, b, turn=0):
            what, count = DONE[b]
            eng.wait_ge(w_used if what == "w_used" else bank_full, count + 4 * turn)

        def step(steps, n):
            for _ in range(n):
                next(steps, None)

        def step_between(steps, n, *others):
            for _ in range(n):
                next(steps, None)
                for other in others:
                    next(other, None)

        def part_columns(i):
            return slice(BLK // PARTS * i, BLK // PARTS * (i + 1))

        def pieces(b, i):
            if GAINS[b] is None:
                return [(part_columns(i), None)]
            norm, k0, wid = GAINS[b]
            ks = range(BLK // PARTS // wid * i, BLK // PARTS // wid * (i + 1))
            return [(slice(wid * k, wid * k + wid), gcol[:, norm, k0 + k:k0 + k + 1]) for k in ks]

        stream = dram["weights"]
        pre_use = {"pre0": 0, "pre1": 1, "pre2": 2}
        halves = ("post1", "post2", "final")

        PREP_MIX = 0
        PREP_CT = PREP_MIX + KW
        PREP_IDX = PREP_CT + 1
        PREP_CUM = PREP_IDX + IDX_H * (TT - 1)
        PREP_QLAT = PREP_CUM + 2
        N_PREP = PREP_QLAT + BH
        O_FOX = HEADS // 2
        O_DSA = O_FOX + BH

        block = ctx.enter_context(nc.Block())

        @block.sync
        def _(sp):
            def load(b, turn=0):
                if b >= RING:
                    sp.wait_ge(w_split, PARTS * (b - RING + 1) + PARTS * RING * turn)
                sp.dma_start(w_raw[b % RING][:, :], stream[b + RING * turn, :, :]).then_inc(w_loaded[b % RING], 16)

            def loads(b, end):
                turns = (end - b) // RING
                if turns > 1:
                    with sp.Fori(0, turns) as turn:
                        for i in range(RING):
                            load(b + i, turn)
                    b += RING * turns
                for last in range(b, end):
                    load(last)

            x_tok = dram["x"].rearrange("(t p) d -> p t d", p=P)
            x2_tok = x2_dram.rearrange("(t p) d -> p t d", p=P)
            out_tok = out.rearrange("(t p) d -> p t d", p=P)

            sp.dma_start(x_sb[:, 0, :], x_tok[:, 0, :]).then_inc(x_tile[0], 16)
            sp.dma_start(g_first[:, :], dram["g_first"].partition_broadcast(P)).then_inc(gains_loaded, 16)
            sp.dma_start(x_sb[:, 1, :], x_tok[:, 1, :]).then_inc(x_tile[1], 16)
            for b in range(RING):
                load(b)
                sp.dma_start(x_sb[:, 2 + b, :], x_tok[:, 2 + b, :]).then_inc(x_tile[2 + b], 16)
            sp.dma_start(g_post[:, :], dram["g_post_mix"].partition_broadcast(P)).then_inc(gpost_loaded, 16)
            sp.dma_start(gcol[:, :, :], dram["gcol"]).then_inc(gcol_loaded, 16)
            sp.dma_start(kvg[:, :], dram["kvg"].partition_broadcast(P)).then_inc(const_loaded, 16)
            sp.dma_start(bf[:, :], dram["bf"].partition_broadcast(P)).then_inc(const_loaded, 16)
            sp.dma_start(convw[:, :, :], dram["convw"]).then_inc(const_loaded, 16)
            loads(RING, FIRST["gu0"])
            sp.wait_ge(pv_done, U_FOX)
            sp.dma_start(x_sb[:, :, :], x_tok).then_inc(x_loaded, 16)
            loads(FIRST["gu0"], FIRST["gu0"] + 5)
            sp.wait_ge(x_updated, TT)
            sp.dma_start(g_post[:, :], dram["g_post_ffn"].partition_broadcast(P)).then_inc(gpost_loaded, 16)
            loads(FIRST["gu0"] + 5, FIRST["ki"])
            sp.wait_ge(x_updated, 2 * TT)
            sp.dma_start(g_post[:, 0:W], dram["ln_g"].partition_broadcast(P)).then_inc(gpost_loaded, 16)
            sp.dma_start(g_post[:, W:2 * W], dram["ln_b"].partition_broadcast(P)).then_inc(gpost_loaded, 16)
            sp.dma_start(a_bs, dram["gm_b"].partition_broadcast(P)).then_inc(aconst_loaded, 16)
            sp.dma_start(a_ws, dram["gm_wT"]).then_inc(aconst_loaded, 16)
            loads(FIRST["ki"], FIRST["a_uz"] + 1)
            sp.dma_start(x2_tok, x_sb[:, :, :]).then_inc(x2_spilled, 16)
            loads(FIRST["a_uz"] + 1, FIRST["d_k"])
            sp.wait_ge(ln_done, TT)
            sp.dma_start(wukT, dram["wukT"]).then_inc(latent_loaded, 16)
            sp.dma_start(wuv, dram["wuv"]).then_inc(latent_loaded, 16)
            loads(FIRST["d_k"], FIRST["d_z"])
            sp.wait_ge(prep_free, PREP_CUM + 1)
            sp.dma_start(cum_dram, cum_rows).then_inc(cum_stored, 16)
            sp.wait_ge(y_split["a"], KW)
            sp.wait_ge(cum_stored, 16)
            sp.dma_start(arena[:, 4096:4096 + BH * S], cum_dram.rearrange("h s -> (h s)").partition_broadcast(P)).then_inc(cum_loaded, 16)
            loads(FIRST["d_z"], FIRST["gate_b0"])
            sp.wait_ge(ydsa_ready, BH)
            sp.dma_start(g_post[:, :], dram["final_g"].partition_broadcast(P)).then_inc(gpost_loaded, 16)
            loads(FIRST["gate_b0"], N_BLOCKS)
            sp.wait_ge(merged_split, KD)
            sp.wait_ge(x2_spilled, 16)
            sp.dma_start(x_sb[:, :, :], x2_tok).then_inc(x2_loaded, 16)
            for t in range(TT):
                sp.wait_ge(out_ready, t + 1)
                sp.dma_start(out_tok[:, t, :], m_sb[:, t, :]).then_inc(out_stored, 16)
            sp.wait_ge(out_stored, 16 * TT)

        @block.gpsimd
        def _(pool):
            nc.gpsimd.memset(minus_half[:, :], -0.5).then_inc(masks_made, 1)
            nc.gpsimd.memset(ident[:, :], 0.0).then_inc(ident_made, 1)
            nc.gpsimd.memset(cmask[:, :], 0.0).then_inc(masks_made, 1)
            pool.wait_ge(ident_made, 1)
            nc.gpsimd.affine_select(out=ident[:, :], in_=ident[:, :], compare_op=ALU.not_equal, fill=1.0, base=0,
                                    pattern=[[-1, P]], channel_multiplier=1).then_inc(ident_made, 1)
            pool.wait_ge(masks_made, 2)
            nc.gpsimd.affine_select(out=cmask[:, :], in_=cmask[:, :], compare_op=ALU.is_ge, fill=NEG, base=0,
                                    pattern=[[-1, P]], channel_multiplier=1).then_inc(masks_made, 1)

            def reciprocal_roots(*names):
                for n, (name, _) in enumerate(NORMS):
                    if name in names:
                        pool.wait_ge(var_done, n + 1)
                        nc.gpsimd.tensor_tensor(rstd[:, n:n + 1], var[:, n:n + 1], minus_half[:, :], ALU.pow).then_inc(rstd_done, 1)

            reciprocal_roots("pre0")
            for h in range(HEADS):
                pool.wait_ge(bias_loaded[h % 4], 16 * (h // 4 + 1))
                nc.gpsimd.memset(biases[0:CHUNK, h % 4, BIAS_W - CHUNK:BIAS_W], NEG).then_inc(bias_ready, 1)
            reciprocal_roots("post1", "pre1")
            pool.wait_ge(pv_done, U_FOX)
            nc.gpsimd.memset(tri, 1.0).then_inc(tri_made, 1)
            pool.wait_ge(tri_made, 1)
            nc.gpsimd.affine_select(out=tri[:, 0:P], in_=tri[:, 0:P], compare_op=ALU.is_ge, fill=0.0, base=0,
                                    pattern=[[1, P]], channel_multiplier=-1).then_inc(tri_made, 1)
            reciprocal_roots("post2", "pre2")
            reciprocal_roots("ln")
            reciprocal_roots("c")
            pool.wait_ge(aconst_loaded, 32)
            nc.gpsimd.affine_select(out=a_ws, in_=a_ws, compare_op=ALU.is_ge, fill=0.0, base=0, pattern=[[0, KW], [1, P]],
                                    channel_multiplier=-1).then_inc(mix_masked, 1)
            for t in range(1, TT):
                pool.wait_ge(score_added, IDX_H * t)
                nc.gpsimd.affine_select(out=sel[t][:, P * t:P * (t + 1)], in_=sel[t][:, P * t:P * (t + 1)], compare_op=ALU.is_ge,
                                        fill=ACAUSAL, base=0, pattern=[[-1, P]], channel_multiplier=1).then_inc(score_masked, 1)
            reciprocal_roots("final")

        @block.scalar
        def _(act):
            def split_parts(b, turn=0):
                if b >= N_BLOCKS:
                    return
                act.wait_ge(w_loaded[b % RING], 16 * (b // RING + 1) + 16 * turn)
                if b >= RING:
                    block_done(act, b - RING, turn)
                if b == FIRST["gu0"]:
                    act.wait_ge(gcol_loaded, 16)
                for i in range(PARTS):
                    for cols, gain in pieces(b, i):
                        last = nc.scalar.activation(w_hi[b % RING][:, cols], w_raw[b % RING][:, cols], ACT.Copy, scale=1.0 if gain is None else gain)
                    last.then_inc(w_rounded, 1)
                    yield

            def split(b, turn=0):
                step(split_parts(b, turn), PARTS)

            def read_out(dst, e, func=ACT.Copy, turn=0):
                act.wait_ge(bank_full, e + 1 + 4 * turn)
                nc.scalar.activation(dst, bank[e % 4][:, :], func).then_inc(bank_free[e % 4], 1)

            def sum_squares(name, t, src, place=None):
                n = SCOL[name, t]
                if n:
                    act.wait_ge(sumsq_done, n)
                nc.scalar.activation(junk[:, 0:src.shape[-1]] if place is None else place, src, ACT.Square,
                                     accum_out=sumsq[:, n:n + 1]).then_inc(sumsq_done, 1)

            def round_xT(name, t):
                for j in range(2):
                    q = 2 * (TT * pre_use[name] + t) + j
                    act.wait_ge(xpose_done, q + 1)
                    nc.scalar.activation(xT_hi[:, 4 * j:4 * j + 4, P * t:P * t + P], xp[q % 4][:, :].rearrange("p (c s) -> p c s", s=P),
                                         ACT.Copy).then_inc(xT_rounded, 1)

            def norms(r, squares_b, late):
                name = f"pre{r}"
                for i in range(TT + 2):
                    if i < TT:
                        squares_b(i)
                    if 0 <= i - 1 < TT:
                        act.wait_ge(x_updated, TT * (r - 1) + i)
                        sum_squares(name, i - 1, x_sb[:, i - 1, :])
                    if i == TT and r == 1:
                        split(late)
                    if i >= 2:
                        round_xT(name, i - 2)
                    if 0 <= i - 1 < TT:
                        t, n = i - 1, NCOL[name, i - 1]
                        act.wait_ge(rstd_done, n + 1)
                        if t >= 2:
                            act.wait_ge(xpose_done, 2 * (TT * pre_use[name] + t - 1))
                        nc.scalar.activation(xn[:, t % 2, :], x_sb[:, t, :], ACT.Copy, scale=rstd[:, n:n + 1]).then_inc(xn_done, 1)
                    if i == TT and r == 2:
                        split(late)

            def attention(lo, hi, o_done):
                for i in range(lo, hi + 7):
                    if lo <= i - 6 < hi:
                        o_done(i - 6)
                    if i < hi:
                        kind, h, t = UNITS[i]
                        nk = P * (t + 1)
                        if kind == "mha" and t == 0:
                            bias_load(h + 2)
                        if kind == "fox" or (kind == "mha" and t >= 2):
                            act.wait_ge(sc_ready, i + 1)
                            if i >= 4:
                                act.wait_ge(tp_ready, i - 3)
                        if kind == "mha" and t >= 2:
                            act.wait_ge(bias_ready, h + 1)
                            nc.scalar.activation(s_ring[:, i % 4, 0:nk - BIAS_W], sc[i % 2][:, 0:nk - BIAS_W], ACT.Identity,
                                                 bias=biases[:, h % 4, 0:1], scale=HD ** -0.5).then_inc(part_done, 1)
                        if kind == "fox":
                            nc.scalar.activation(s_ring[:, i % 4, 0:nk], sc[i % 2][:, 0:nk], ACT.Identity,
                                                 bias=cumq[:, t, h:h + 1], scale=BD ** -0.5).then_inc(sc_free, 1)
                    if lo <= i - 1 < hi:
                        u = i - 1
                        nk = P * (UNITS[u][2] + 1)
                        act.wait_ge(max_ready, u + 1)
                        if u >= 4:
                            act.wait_ge(rinv_ready, u - 3)
                        nc.scalar.activation(s_ring[:, u % 4, 0:nk], s_ring[:, u % 4, 0:nk], ACT.Exp, bias=negmax[:, u % 4:u % 4 + 1],
                                             accum_out=psums[:, u % 4:u % 4 + 1]).then_inc(p_ready, 1)
                    if lo <= i - 3 < hi:
                        u = i - 3
                        nk = P * (UNITS[u][2] + 1)
                        act.wait_ge(tp_ready, u + 1)
                        if u >= 3:
                            act.wait_ge(pv_done, u - 2)
                        nc.scalar.activation(pT[:, u % 3, 0:nk], tp[:, 0:nk], ACT.Copy).then_inc(pT_ready, 1)
                    yield

            def bias_load(h):
                if h < HEADS:
                    if h >= 4:
                        act.wait_ge(s_ready, TT * (h - 3))
                        act.wait_ge(part_done, 2 * (h - 3))
                    act.dma_start(biases[:, h % 4, :], dram["bias"][h, :, :]).then_inc(bias_loaded[h % 4], 16)

            def first_squares(t):
                act.wait_ge(x_tile[t], 16)
                sum_squares("pre0", t, x_sb[:, t, :])

            first_squares(0)
            first_squares(1)
            round_xT("pre0", 0)
            split(0)
            first_squares(2)
            round_xT("pre0", 1)
            first_squares(3)
            split(1)
            round_xT("pre0", 2)
            round_xT("pre0", 3)
            bias_load(0)
            bias_load(1)

            for h in range(2):
                b = FIRST[f"v{h}"]
                split(b + 2)
                for t in range(TT):
                    read_out(v_sb[:, t, W * h:W * h + W], USE[f"v{h}"] + t)
                split(b + 3)

            def pair_out(u):
                if u % (2 * TT) == 2 * TT - 1:
                    act.wait_ge(pv_done, u + 1)
                    nc.scalar.activation(oT_hi[:, u // (2 * TT), :], ob[:, :], ACT.Copy).then_inc(o_rounded, 1)


            def queries_out(i):
                e = USE[f"qk{i}"]
                for c in range(2):
                    act.wait_ge(bank_full, e + 1)
                    nc.scalar.activation(q_st[i % 2][pair[c], c, :], bank[e % 4][pair[c], :], ACT.Copy).then_inc(q_rounded, 1)
                    yield

            def keys_out(i):
                e = USE[f"qk{i}"] + 1
                for c in range(2):
                    act.wait_ge(bank_full, e + 1)
                    for place in range(2):
                        nc.scalar.activation(k_st[i % 2][pair[place], c, :], bank[e % 4][pair[c], :], ACT.Copy).then_inc(k_rounded, 1)
                    yield

            mha = attention(0, U_FOX, pair_out)
            step(queries_out(0), 2)
            step(keys_out(0), 2)
            keys, parts = iter(()), split_parts(FIRST["qk0"] + 2)
            for i in range(1, HEADS // QK_HEADS):
                step(keys, 1)
                step_between(mha, len(MHA_FIRST_AT if i == 1 else MHA_AT), keys, parts)
                queries = queries_out(i)
                step(queries, 1)
                step_between(mha, len(MHA_AT), queries, parts)
                keys, parts = keys_out(i), split_parts(FIRST[f"qk{i}"] + 2)
            step(keys, 1)

            step_between(mha, 4 * TT, keys, parts)
            split(FIRST["wo0"] + 2)
            for t in range(TT):
                act.wait_ge(bank_full, USE["wo0"] + t + 1)
                sum_squares("post1a", t, bank[(USE["wo0"] + t) % 4][:, :])
            split(FIRST["wo0"] + 3)
            split(FIRST["wo1"] + 2)

            def squares_wo1(t):
                act.wait_ge(bank_full, USE["wo1"] + t + 1)
                sum_squares("post1b", t, bank[(USE["wo1"] + t) % 4][:, :])

            norms(1, squares_wo1, FIRST["wo1"] + 3)

            def gated_chunk(f, i, turn=0):
                n = FH * f + i
                b, e = FIRST[f"gu{f}"] + i, USE[f"gu{f}"] + 2 * i
                if n >= 2:
                    act.wait_ge(act_split, n - 1 + 2 * turn)
                read_out(sg[:, n % 2, :], e, ACT.Silu, turn)
                act.wait_ge(*freed(e + 1, turn))
                nc.scalar.activation(act_hi[:, i + 2 * turn, :], a_sb[:, n % 2, :], ACT.Copy).then_inc(act_rounded, 1)
                split(b + 2, turn)

            for f in range(2):
                for i in range(GU_LOOP[f][0]):
                    gated_chunk(f, i)
                with act.Fori(0, GU_LOOP[f][1]) as turn:
                    for i in range(2):
                        gated_chunk(f, GU_LOOP[f][0] + i, turn)
                for i in range(GU_LOOP[f][0] + 2 * GU_LOOP[f][1], FH):
                    gated_chunk(f, i)
                for h in range(2):
                    b, e = FIRST[f"down{f}{h}"], USE[f"down{f}{h}"]
                    split(b + 2)
                    split(b + 3)
                    if f == 0:
                        for t in range(TT):
                            read_out(m_sb[:, t, W * h:W * h + W], e + t)
                        split(b + 4)
                    elif h == 0:
                        for t in range(TT):
                            act.wait_ge(*freed(e + t))
                            sum_squares("post2a", t, m_sb[:, t, 0:W])
                        split(b + 4)

            def squares_down11(t):
                act.wait_ge(*freed(USE["down11"] + t))
                sum_squares("post2b", t, m_sb[:, t, W:2 * W])

            norms(2, squares_down11, FIRST["down11"] + 4)

            split(FIRST["a_v"] + 2)
            for t in range(TT):
                e = USE["a_v"] + t
                act.wait_ge(bank_full, e + 1)
                nc.scalar.activation(av[:, t, :], bank[e % 4][:, :], ACT.Copy, accum_out=mean[:, t:t + 1]).then_inc(bank_free[e % 4], 1)
            split(FIRST["a_v"] + 3)
            for t in range(TT):
                act.wait_ge(av_centred, t + 1)
                sum_squares("ln", t, av[:, t, :], q_junk[:, t, :])
            for t in range(TT):
                e = USE["cwf"] + t
                act.wait_ge(bank_full, e + 1)
                nc.scalar.activation(c_raw[:, t, :], bank[e % 4][:, 0:P], ACT.Copy).then_inc(c_copied, 1)
            split(FIRST["cwf"] + 2)
            for t in range(TT):
                act.wait_ge(c_copied, t + 1)
                sum_squares("c", t, c_raw[:, t, :], q_junk[:, t, 0:P])
            act.wait_ge(f_abs, 1)
            nc.scalar.activation(fl[:, :, :], fna[:, :, :], ACT.Exp).then_inc(f_exp, 1)
            act.wait_ge(f_exp, 1)
            nc.scalar.activation(fl[:, :, :], fl[:, :, :], ACT.Ln, bias=1.0).then_inc(f_log, 1)
            for c in range(2):
                e = USE["qi"] + c
                act.wait_ge(bank_full, e + 1)
                for p in range(2):
                    nc.scalar.activation(qi_st[pair[p], 2 * c + p, :], bank[e % 4][pair[p], :], ACT.Copy).then_inc(qi_rounded, 1)
            split(FIRST["qi"] + 2)
            act.wait_ge(bank_full, USE["ki"] + 1)
            nc.scalar.activation(ki_st, bank[USE["ki"] % 4][:, :], ACT.Copy).then_inc(ki_rounded, 1)
            split(FIRST["ki"] + 2)

            def round_y(br, j, src):
                act.wait_ge(y_ready[br], j + 1)
                nc.scalar.activation(y_hi[slot[br]][:, j, :], src, ACT.Copy).then_inc(y_rounded[br], 1)

            def small_products():
                def prep_out(n, dst, func, src, scale=1.0):
                    act.wait_ge(prep_ready, n + 1)
                    nc.scalar.activation(dst, src(sc[n % 2]), func, scale=scale).then_inc(prep_free, 1)

                prep_out(PREP_CT, cT, ACT.Copy, lambda z: z[:, :])
                yield
                for t in range(1, TT):
                    for h in range(IDX_H):
                        j = IDX_H * (t - 1) + h
                        if j >= 2:
                            act.wait_ge(score_added, j - 1)
                        prep_out(PREP_IDX + j, relu_d[:, j % 2, 0:P * (t + 1)], ACT.Relu, lambda z: z[:, 0:P * (t + 1)], IDX_D ** -0.5)
                        yield
                prep_out(PREP_CUM, cum_rows, ACT.Copy, lambda z: z[0:BH, :], -1.0)
                yield
                prep_out(PREP_CUM + 1, cumq[:, :, :], ACT.Copy, lambda z: z[:, 0:TT * BH].rearrange("p (t h) -> p t h", h=BH))
                yield
                act.wait_ge(y_split["c"], KW)
                for h in range(BH):
                    prep_out(PREP_QLAT + h, qlat[:, h, :], ACT.Copy, lambda z: z[:, :])
                    yield

            small = small_products()
            for j in range(KW):
                e = USE["a_uz"] + 2 * j
                step(small, (len(IDX_AT if j else IDX_FIRST_AT) + len(IDX_AT)) if j < TT - 1 else 0)
                if j >= 2:
                    act.wait_ge(y_split["a"], j - 1)
                read_out(a_sz[:, j % 2, :], e + 1, ACT.Silu)
                round_y("a", j, a_y[:, j % 2, :])
                split(FIRST["a_uz"] + j + 2)
            act.wait_ge(x2_spilled, 16)
            for key, base in (("d_q", 0), ("d_k", BH)):
                for i in range(2):
                    for c in range(2):
                        if key == "d_q" and i == 0:
                            step(small, 1)
                        read_out(dqk[:, base + 2 * i + c, :], USE[key] + 2 * i + c)
                    split(FIRST[key] + i + 2)
            split(FIRST["d_v"] + 2)
            for t in range(TT):
                read_out(dv[:, t, :], USE["d_v"] + t)
            split(FIRST["d_v"] + 3)
            for i in range(2):
                for c in range(2):
                    read_out(sz[:, 2 * i + c, :], USE["d_z"] + 2 * i + c, ACT.Silu)
                split(FIRST["d_z"] + i + 2)

            def fox_out(u):
                if u % TT == TT - 1:
                    h = (u - U_FOX) // TT
                    act.wait_ge(o_free, O_FOX + h + 1)
                    nc.scalar.activation(y_hi[slot["d"]][:, h, :], sz[:, h, :], ACT.Copy).then_inc(y_rounded["d"], 1)

            fox = attention(U_FOX, U_DSA, fox_out)
            parts = iter(())
            n_at = len(PAIR_AT)
            for j in range(KW):
                b, e = FIRST["c"] + 2 * j, USE["c"] + 4 * j
                step_between(fox, n_at, parts)
                if j == 0:
                    act.wait_ge(conv_zero, 1)
                else:
                    act.wait_ge(conv_step, 3 * j)
                read_out(c_y[:, 2:2 + S], e)
                step_between(fox, 1, parts)
                if j:
                    round_y("c", j - 1, c_acc)
                step_between(fox, n_at - 1, parts)
                parts = split_parts(b + 2)
                step_between(fox, 2 * n_at, parts)
                if j:
                    act.wait_ge(y_ready["c"], j)
                read_out(c_sz, e + 3, ACT.Silu)
                parts = split_parts(b + 3)
            step(parts, PARTS)
            round_y("c", KW - 1, c_acc)
            step(fox, U_DSA)

            for i in range(2):
                for c in range(2):
                    read_out(bq[:, 2 * i + c, :], USE["b_q"] + 2 * i + c)
                split(FIRST["b_q"] + i + 2)
            act.wait_ge(y_split["d"], BH)
            for i in range(2):
                for c in range(2):
                    step(small, 1)
                    read_out(sz[:, 2 * i + c, :], USE["b_z"] + 2 * i + c, ACT.Silu)
                split(FIRST["b_z"] + i + 2)

            def dsa_out(u):
                if u % TT == TT - 1:
                    h = (u - U_DSA) // TT
                    act.wait_ge(pv_done, u + 1)
                    if h >= 1:
                        act.wait_ge(ydsa_ready, h)
                    nc.scalar.activation(olat, ob[:, :], ACT.Copy).then_inc(olat_ready, 1)

            def gates(br):
                r = ORDER.index(br)
                for half in range(2):
                    b, e = FIRST[f"gate_{br}{half}"], USE[f"gate_{br}{half}"]
                    for i in range(2):
                        parts = split_parts(b + i + 1) if i or half or r else iter(())
                        step_between(dsa, 2 * len(PAIR_AT), parts)
                        step(parts, PARTS)
                        for c in range(2):
                            if half or r:
                                last = f"branch_{br}0" if half else f"branch_{ORDER[r - 1]}1"
                                act.wait_ge(*freed(USE[last] + 2 * i + c))
                            read_out(sig[:, 2 * i + c, :], e + 2 * i + c, ACT.Sigmoid)
                    split(b + 3)
                    if br == ORDER[-1]:
                        for j in range(4 * half, 4 * half + 4):
                            act.wait_ge(gate_add, KD * (N_BRANCH - 2) + j + 1)
                            nc.scalar.activation(mT_hi[:, j, :], merged[:, j, :], ACT.Copy).then_inc(merged_rounded, 1)

            dsa = attention(U_DSA, N_UNITS, dsa_out)
            gates("a")
            gates("d")
            block_done(act, FIRST["branch_a1"])
            for j in range(KW):
                act.wait_ge(o_free, O_DSA + j + 1)
                nc.scalar.activation(y_hi[slot["b"]][:, j, :], sz[:, j, :], ACT.Copy).then_inc(y_rounded["b"], 1)
            gates("c")
            gates("b")
            split(FIRST["out0"] + 1)
            for h in range(2):
                split(FIRST[f"out{h}"] + 2)
                split(FIRST[f"out{h}"] + 3)
                for t in range(TT):
                    act.wait_ge(*freed(USE[f"out{h}"] + t))
                    sum_squares("final" + "ab"[h], t, x_sb[:, t, W * h:W * h + W])

        @block.vector
        def _(dve):
            def split_parts(b, turn=0):
                if b >= N_BLOCKS:
                    return
                for i in range(PARTS):
                    dve.wait_ge(w_rounded, PARTS * b + i + 1 + PARTS * RING * turn)
                    for cols, gain in pieces(b, i):
                        hi = w_hi[b % RING][:, cols].bitcast(F32)
                        if gain is None:
                            last = nc.vector.tensor_tensor(w_lo[b % RING][:, cols], w_raw[b % RING][:, cols], hi, ALU.subtract)
                        else:
                            last = nc.vector.scalar_tensor_tensor(out=w_lo[b % RING][:, cols], in0=w_raw[b % RING][:, cols], scalar=gain, in1=hi,
                                                                  op0=ALU.mult, op1=ALU.subtract)
                    last.then_inc(w_split, 1)
                    yield

            def split(b, turn=0):
                step(split_parts(b, turn), PARTS)

            def begin_variance(name, t):
                n, first = NCOL[name, t], SCOL[name + "a", t]
                dve.wait_ge(sumsq_done, first + 1)
                nc.vector.tensor_scalar(var[:, n:n + 1], sumsq[:, first:first + 1], 1.0 / D, EPS, ALU.mult, ALU.add).then_inc(var_begun, 1)

            def variance(name, t, width):
                n = NCOL[name, t]
                if name in halves:
                    second = SCOL[name + "b", t]
                    dve.wait_ge(sumsq_done, second + 1)
                    dve.wait_ge(var_begun, TT * halves.index(name) + t + 1)
                    nc.vector.scalar_tensor_tensor(out=var[:, n:n + 1], in0=sumsq[:, second:second + 1], scalar=1.0 / width, in1=var[:, n:n + 1],
                                                   op0=ALU.mult, op1=ALU.add).then_inc(var_done, 1)
                else:
                    only = SCOL[name, t]
                    dve.wait_ge(sumsq_done, only + 1)
                    nc.vector.tensor_scalar(var[:, n:n + 1], sumsq[:, only:only + 1], 1.0 / width, EPS, ALU.mult, ALU.add).then_inc(var_done, 1)

            def scale_rows(out_, in_, name, t, other, op=ALU.mult):
                n = NCOL[name, t]
                dve.wait_ge(rstd_done, n + 1)
                return nc.vector.scalar_tensor_tensor(out=out_, in0=in_, scalar=rstd[:, n:n + 1], in1=other, op0=ALU.mult, op1=op)

            def scale_first(t):
                if t >= 2:
                    dve.wait_ge(xpose_done, 2 * (t - 1))
                dve.wait_ge(gains_loaded, 16)
                scale_rows(xn[:, t % 2, :], x_sb[:, t, :], "pre0", t, g_first[:, :]).then_inc(xn_done, 1)

            def split_xT(name, t):
                for j in range(2):
                    q = 2 * (TT * pre_use[name] + t) + j
                    dve.wait_ge(xT_rounded, q + 1)
                    part = (slice(None), slice(4 * j, 4 * j + 4), slice(P * t, P * t + P))
                    nc.vector.tensor_tensor(xT_lo[part], xp[q % 4][:, :].rearrange("p (c s) -> p c s", s=P), xT_hi[part].bitcast(F32),
                                            ALU.subtract).then_inc(xT_split, 1)

            def norms(r, add_b, gain_b, late):
                dve.wait_ge(x_loaded, 16)
                for i in range(TT + 2):
                    if i < TT:
                        add_b(i)
                    if 0 <= i - 1 < TT:
                        t = i - 1
                        scale_rows(x_sb[:, t, :], m_sb[:, t, :], f"post{r}", t, x_sb[:, t, :], ALU.add).then_inc(x_updated, 1)
                    if i < TT:
                        gain_b(i)
                        variance(f"post{r}", i, D)
                    if 0 <= i - 1 < TT:
                        variance(f"pre{r}", i - 1, D)
                    if i == TT and r == 1:
                        split(late)
                    if i >= 2:
                        split_xT(f"pre{r}", i - 2)
                    if i == TT and r == 2:
                        split(late)

            def attention(lo, hi, o_done):
                for i in range(lo, hi + 7):
                    if lo <= i - 6 < hi:
                        o_done(i - 6)
                    if i < hi:
                        kind, h, t = UNITS[i]
                        nk = P * (t + 1)
                        s = s_ring[:, i % 4, 0:nk]
                        if kind == "fox":
                            dve.wait_ge(sc_free, i - U_FOX + 1)
                            dve.wait_ge(cum_loaded, 16)
                            nc.vector.tensor_tensor(s, s, negcumk[:, h, 0:nk], ALU.add).then_inc(part_done, 1)
                            dve.wait_ge(part_done, HEADS * 2 + i - U_FOX + 1)
                            nc.vector.tensor_tensor(s[:, nk - P:nk], s[:, nk - P:nk], cmask[:, :], ALU.add).then_inc(s_ready, 1)
                        else:
                            dve.wait_ge(sc_ready, i + 1)
                            if i >= 4:
                                dve.wait_ge(tp_ready, i - 3)
                        if kind == "mha":
                            w = min(nk, BIAS_W)
                            dve.wait_ge(bias_ready, h + 1)
                            if t >= 2:
                                dve.wait_ge(part_done, 2 * h + t - 1)
                            nc.vector.scalar_tensor_tensor(out=s[:, nk - w:nk], in0=sc[i % 2][:, nk - w:nk], scalar=HD ** -0.5,
                                                           in1=biases[:, h % 4, BIAS_W - w:BIAS_W], op0=ALU.mult,
                                                           op1=ALU.add).then_inc(s_ready, 1)
                        if kind == "dsa":
                            nc.vector.scalar_tensor_tensor(out=s, in0=sc[i % 2][:, 0:nk], scalar=BD ** -0.5,
                                                           in1=cmask[:, :] if t == 0 else sel[t], op0=ALU.mult,
                                                           op1=ALU.add).then_inc(s_ready, 1)
                        dve.wait_ge(s_ready, i + 1)
                        if i >= 4:
                            dve.wait_ge(p_ready, i - 3)
                        nc.vector.reduce_max(negmax[:, i % 4:i % 4 + 1], s, AX_X, negate=True).then_inc(max_ready, 1)
                    if lo <= i - 1 < hi:
                        u = i - 1
                        nk = P * (UNITS[u][2] + 1)
                        dve.wait_ge(p_ready, u + 1)
                        nc.vector.reciprocal(rinv[:, u % 4:u % 4 + 1], psums[:, u % 4:u % 4 + 1]).then_inc(rinv_ready, 1)
                        dve.wait_ge(rinv_ready, u + 1)
                        nc.vector.tensor_scalar(s_ring[:, u % 4, 0:nk], s_ring[:, u % 4, 0:nk], rinv[:, u % 4:u % 4 + 1], None,
                                                ALU.mult).then_inc(pn_ready, 1)
                    yield

            variance("pre0", 0, D)
            scale_first(0)
            variance("pre0", 1, D)
            scale_first(1)
            split_xT("pre0", 0)
            split(0)
            variance("pre0", 2, D)
            split_xT("pre0", 1)
            variance("pre0", 3, D)
            scale_first(2)
            split(1)
            scale_first(3)
            split_xT("pre0", 2)
            split_xT("pre0", 3)
            for b in range(FIRST["v0"], FIRST["qk0"]):
                split(b + 2)

            def pair_out(u):
                if u % (2 * TT) == 2 * TT - 1:
                    hp = u // (2 * TT)
                    dve.wait_ge(o_rounded, hp + 1)
                    nc.vector.tensor_tensor(oT_lo[:, hp, :], ob[:, :], oT_hi[:, hp, :].bitcast(F32), ALU.subtract).then_inc(o_free, 1)


            def queries_split(i):
                e, q = USE[f"qk{i}"], q_st[i % 2]
                for c in range(2):
                    dve.wait_ge(q_rounded, 2 * i + c + 1)
                    nc.vector.tensor_tensor(q[pair[1 - c], c, :], bank[e % 4][pair[c], :], q[pair[c], c, :].bitcast(F32), ALU.subtract)\
                        .then_inc(bank_free[e % 4] if c else first_split, 1)
                    yield

            def keys_split(i):
                e, k = USE[f"qk{i}"] + 1, k_st[i % 2]
                for c in range(2):
                    dve.wait_ge(k_rounded, 4 * i + 2 * c + 2)
                    nc.vector.tensor_tensor(k_rest[i % 2][pair[c], :], bank[e % 4][pair[c], :], k[pair[c], c, :].bitcast(F32), ALU.subtract)\
                        .then_inc(bank_free[e % 4] if c else first_split, 1)
                    yield

            mha = attention(0, U_FOX, pair_out)
            step(queries_split(0), 2)
            step(keys_split(0), 2)
            keys, parts = iter(()), split_parts(FIRST["qk0"] + 2)
            for i in range(1, HEADS // QK_HEADS):
                step(keys, 1)
                step_between(mha, len(MHA_FIRST_AT if i == 1 else MHA_AT), keys, parts)
                queries = queries_split(i)
                step(queries, 1)
                step_between(mha, len(MHA_AT), queries, parts)
                keys, parts = keys_split(i), split_parts(FIRST[f"qk{i}"] + 2)
            step(keys, 1)

            def gain_wo(h, t):
                e = USE[f"wo{h}"] + t
                dve.wait_ge(gpost_loaded, 16)
                dve.wait_ge(sumsq_done, SCOL["post1" + "ab"[h], t] + 1)
                part = slice(W * h, W * h + W)
                nc.vector.tensor_tensor(m_sb[:, t, part], bank[e % 4][:, :], g_post[:, part], ALU.mult).then_inc(bank_free[e % 4], 1)
                dve.wait_ge(*freed(e))

            step_between(mha, 4 * TT, keys, parts)
            split(FIRST["wo0"] + 2)
            for t in range(TT):
                begin_variance("post1", t)
                gain_wo(0, t)
            split(FIRST["wo0"] + 3)
            split(FIRST["wo1"] + 2)
            norms(1, lambda t: None, lambda t: gain_wo(1, t), FIRST["wo1"] + 3)

            def add_down(h, t):
                e = USE[f"down1{h}"] + t
                dve.wait_ge(*freed(USE[f"down0{h}"] + t))
                dve.wait_ge(bank_full, e + 1)
                part = m_sb[:, t, W * h:W * h + W]
                nc.vector.tensor_tensor(part, part, bank[e % 4][:, :], ALU.add).then_inc(bank_free[e % 4], 1)

            def gain_down(h, t):
                dve.wait_ge(gpost_loaded, 32)
                dve.wait_ge(sumsq_done, SCOL["post2" + "ab"[h], t] + 1)
                part = slice(W * h, W * h + W)
                nc.vector.tensor_tensor(m_sb[:, t, part], m_sb[:, t, part], g_post[:, part], ALU.mult).then_inc(gained, 1)
                dve.wait_ge(gained, TT * h + t + 1)

            def gated_chunk(f, i, turn=0):
                n = FH * f + i
                e = USE[f"gu{f}"] + 2 * i
                dve.wait_ge(*freed(e, turn))
                dve.wait_ge(bank_full, e + 2 + 4 * turn)
                nc.vector.tensor_tensor(a_sb[:, n % 2, :], sg[:, n % 2, :], bank[(e + 1) % 4][:, :], ALU.mult).then_inc(bank_free[(e + 1) % 4], 1)
                dve.wait_ge(act_rounded, n + 1 + 2 * turn)
                at = i + 2 * turn
                nc.vector.tensor_tensor(act_lo[:, at, :], a_sb[:, n % 2, :], act_hi[:, at, :].bitcast(F32), ALU.subtract).then_inc(act_split, 1)
                split(FIRST[f"gu{f}"] + i + 2, turn)

            for f in range(2):
                for i in range(GU_LOOP[f][0]):
                    gated_chunk(f, i)
                with dve.Fori(0, GU_LOOP[f][1]) as turn:
                    for i in range(2):
                        gated_chunk(f, GU_LOOP[f][0] + i, turn)
                for i in range(GU_LOOP[f][0] + 2 * GU_LOOP[f][1], FH):
                    gated_chunk(f, i)
                for h in range(2):
                    b = FIRST[f"down{f}{h}"]
                    split(b + 2)
                    split(b + 3)
                    if f == 0:
                        split(b + 4)
                    elif h == 0:
                        for t in range(TT + 1):
                            if t < TT:
                                add_down(0, t)
                            if t:
                                begin_variance("post2", t - 1)
                                gain_down(0, t - 1)
                        split(b + 4)

            norms(2, lambda t: add_down(1, t), lambda t: gain_down(1, t), FIRST["down11"] + 4)

            split(FIRST["a_v"] + 2)
            for t in range(TT):
                dve.wait_ge(*freed(USE["a_v"] + t))
                nc.vector.tensor_scalar(mean[:, t:t + 1], mean[:, t:t + 1], 1.0 / W, None, ALU.mult).then_inc(mean_ready, 1)
                dve.wait_ge(mean_ready, t + 1)
                nc.vector.tensor_scalar(av[:, t, :], av[:, t, :], mean[:, t:t + 1], None, ALU.subtract).then_inc(av_centred, 1)
            split(FIRST["a_v"] + 3)
            for t in range(TT):
                variance("ln", t, W)
            dve.wait_ge(const_loaded, 16 * 3)
            for t in range(TT):
                e = USE["cwf"] + t
                dve.wait_ge(c_copied, t + 1)
                nc.vector.tensor_scalar(wi[:, t, :], bank[e % 4][:, P:P + IDX_H], IDX_H ** -0.5, None, ALU.mult).then_inc(wi_ready, 1)
                nc.vector.tensor_tensor(fb[:, t, :], bank[e % 4][:, P + IDX_H:P + IDX_H + BH], bf[:, :], ALU.add)\
                    .then_inc(bank_free[e % 4], 1)
            split(FIRST["cwf"] + 2)
            for t in range(TT):
                dve.wait_ge(*freed(USE["cwf"] + t))
            nc.vector.scalar_tensor_tensor(out=fna[:, :, :], in0=fb[:, :, :], scalar=-1.0, in1=fb[:, :, :], op0=ALU.mult, op1=ALU.min).then_inc(f_abs, 1)
            for t in range(TT):
                variance("c", t, P)
            dve.wait_ge(xn_done, TT)
            for t in range(TT):
                scale_rows(c_sb[:, t, :], c_raw[:, t, :], "c", t, kvg[:, :]).then_inc(c_ready, 1)
            dve.wait_ge(gpost_loaded, 16 * 4)
            for t in range(TT):
                scale_rows(av[:, t, :], av[:, t, :], "ln", t, g_post[:, 0:W]).then_inc(ln_scaled, 1)
                dve.wait_ge(ln_scaled, t + 1)
                nc.vector.tensor_tensor(av[:, t, :], av[:, t, :], g_post[:, W:2 * W], ALU.add).then_inc(ln_done, 1)
            dve.wait_ge(f_log, 1)
            nc.vector.scalar_tensor_tensor(out=ls[:, :, :], in0=fb[:, :, :], scalar=0.0, in1=fl[:, :, :], op0=ALU.min, op1=ALU.subtract).then_inc(f_ls, 1)
            for c in range(2):
                e = USE["qi"] + c
                for p in range(2):
                    dve.wait_ge(qi_rounded, 2 * c + p + 1)
                    last = nc.vector.tensor_tensor(qi_st[pair[1 - p], 2 * c + p, :], bank[e % 4][pair[p], :], qi_st[pair[p], 2 * c + p, :].bitcast(F32),
                                                   ALU.subtract)
                last.then_inc(bank_free[e % 4], 1)
            parts = split_parts(FIRST["qi"] + 2)
            dve.wait_ge(aconst_loaded, 32)
            for g in range(KW):
                n = PREP_MIX + g
                dve.wait_ge(prep_ready, n + 1)
                nc.vector.tensor_tensor(a_mix[:, g, :].rearrange("p (c t) -> p c t", t=P), sc[n % 2][:, :].rearrange("p (c t) -> p c t", t=P),
                                        a_bs[:, g:g + 1, :].broadcast_to([P, TT, P]), ALU.add).then_inc(prep_free, 1)
                step(parts, PARTS // KW)
            dve.wait_ge(ki_rounded, 1)
            nc.vector.tensor_tensor(ki_rest, bank[USE["ki"] % 4][:, :], ki_st.bitcast(F32), ALU.subtract).then_inc(bank_free[USE["ki"] % 4], 1)
            split(FIRST["ki"] + 2)

            def small_products():
                dve.wait_ge(wi_ready, TT)
                for t in range(1, TT):
                    for h in range(IDX_H):
                        j = IDX_H * (t - 1) + h
                        dve.wait_ge(prep_free, PREP_IDX + j + 1)
                        r = relu_d[:, j % 2, 0:P * (t + 1)]
                        if h == 0:
                            ins = nc.vector.tensor_scalar(sel[t], r, wi[:, t, h:h + 1], None, ALU.mult)
                        else:
                            dve.wait_ge(score_added, j)
                            ins = nc.vector.scalar_tensor_tensor(out=sel[t], in0=r, scalar=wi[:, t, h:h + 1], in1=sel[t], op0=ALU.mult, op1=ALU.add)
                        ins.then_inc(score_added, 1)
                        yield

            def split_y(br, j, src):
                dve.wait_ge(y_rounded[br], j + 1)
                nc.vector.tensor_tensor(y_lo[slot[br]][:, j, :], src, y_hi[slot[br]][:, j, :].bitcast(F32), ALU.subtract).then_inc(y_split[br], 1)

            small = small_products()
            for j in range(KW):
                e = USE["a_uz"] + 2 * j
                step(small, 2 * len(IDX_AT) if j < TT - 1 else 0)
                dve.wait_ge(prep_free, PREP_MIX + j + 1)
                dve.wait_ge(bank_full, e + 1)
                nc.vector.tensor_tensor(a_mix[:, j, :], a_mix[:, j, :], bank[e % 4][:, :], ALU.mult).then_inc(bank_free[e % 4], 1)
                dve.wait_ge(*freed(e))
                dve.wait_ge(*freed(e + 1))
                if j >= 2:
                    dve.wait_ge(y_split["a"], j - 1)
                nc.vector.tensor_tensor(a_y[:, j % 2, :], a_mix[:, j, :], a_sz[:, j % 2, :], ALU.mult).then_inc(y_ready["a"], 1)
                split_y("a", j, a_y[:, j % 2, :])
                split(FIRST["a_uz"] + j + 2)

            def selection():
                n = 0
                for t in range(1, TT):
                    dve.wait_ge(score_masked, t)
                    for r in range(TOPK // 8):
                        nc.vector.max(top8[:, :], sel[t]).then_inc(topk_step, 1)
                        n += 1
                        dve.wait_ge(topk_step, n)
                        nc.vector.match_replace(sel[t], top8[:, :], sel[t], TAKEN).then_inc(topk_step, 1)
                        n += 1
                        dve.wait_ge(topk_step, n)
                        if r == TOPK // 8 - 1:
                            nc.vector.tensor_scalar(sel[t], sel[t], TAKEN, NEG, ALU.not_equal, ALU.mult).then_inc(topk_step, 1)
                            n += 1
                            dve.wait_ge(topk_step, n)
                        yield

            rounds = selection()
            for b in range(FIRST["d_q"], FIRST["c"]):
                step(rounds, 5)
                split(b + 2)

            def fox_out(u):
                if u % TT == TT - 1:
                    h = (u - U_FOX) // TT
                    dve.wait_ge(pv_done, u + 1)
                    if h == 0:
                        for c in range(KW):
                            dve.wait_ge(*freed(USE["d_z"] + c))
                    nc.vector.tensor_tensor(sz[:, h, :], ob[:, :], sz[:, h, :], ALU.mult).then_inc(o_free, 1)
                    split_y("d", h, sz[:, h, :])

            fox = attention(U_FOX, U_DSA, fox_out)
            parts = iter(())
            dve.wait_ge(prep_free, PREP_CT)
            nc.vector.memset(c_y[:, 0:2], 0.0).then_inc(conv_zero, 1)
            dve.wait_ge(conv_zero, 1)

            def convolution():
                def gate(j):
                    e = USE["c"] + 4 * j
                    dve.wait_ge(conv_step, 3 * j + 3)
                    dve.wait_ge(bank_full, e + 3)
                    nc.vector.tensor_tensor(c_acc, c_acc, bank[(e + 2) % 4][:, :], ALU.mult).then_inc(bank_free[(e + 2) % 4], 1)
                    yield
                    dve.wait_ge(*freed(e + 2))
                    dve.wait_ge(*freed(e + 3))
                    nc.vector.tensor_tensor(c_acc, c_acc, c_sz, ALU.mult).then_inc(y_ready["c"], 1)
                    yield
                    yield
                    split_y("c", j, c_acc)
                    yield

                for j in range(KW):
                    e = USE["c"] + 4 * j
                    if j:
                        yield from gate(j - 1)
                    else:
                        yield from iter((None,) * 4)
                    dve.wait_ge(*freed(e))
                    dve.wait_ge(bank_full, e + 2)
                    nc.vector.tensor_tensor(c_y[:, 2:2 + S], c_y[:, 2:2 + S], bank[(e + 1) % 4][:, :], ALU.mult).then_inc(bank_free[(e + 1) % 4], 1)
                    yield
                    dve.wait_ge(*freed(e + 1))
                    if j:
                        dve.wait_ge(y_split["c"], j)
                    nc.vector.tensor_scalar(c_acc, c_y[:, 0:S], convw[:, j, 0:1], None, ALU.mult).then_inc(conv_step, 1)
                    yield
                    for i in (1, 2):
                        dve.wait_ge(conv_step, 3 * j + i)
                        nc.vector.scalar_tensor_tensor(out=c_acc, in0=c_y[:, i:i + S], scalar=convw[:, j, i:i + 1], in1=c_acc, op0=ALU.mult,
                                                       op1=ALU.add).then_inc(conv_step, 1)
                        yield
                yield from gate(KW - 1)

            conv = convolution()
            for b in range(FIRST["c"], FIRST["b_q"]):
                step_between(fox, 2 * len(PAIR_AT), parts, conv)
                parts = split_parts(b + 2)
            step(parts, PARTS)
            step(conv, 4)
            step(fox, U_DSA)
            for b in range(FIRST["b_q"], FIRST["gate_a0"]):
                step(rounds, 2)
                split(b + 2)
            step(rounds, TT * TOPK)

            def dsa_out(u):
                if u % TT == TT - 1:
                    h = (u - U_DSA) // TT
                    dve.wait_ge(ydsa_ready, h + 1)
                    if h == 0:
                        for c in range(KW):
                            dve.wait_ge(*freed(USE["b_z"] + c))
                    nc.vector.tensor_tensor(sz[:, h, :], ob[:, :], sz[:, h, :], ALU.mult).then_inc(o_free, 1)

            def gates(br):
                r = ORDER.index(br)
                for half in range(2):
                    b, e = FIRST[f"branch_{br}{half}"], USE[f"branch_{br}{half}"]
                    for i in range(2):
                        parts = split_parts(b + i - 1) if i or half or r else iter(())
                        step_between(dsa, 2 * len(PAIR_AT), parts)
                        step(parts, PARTS)
                    split(b + 1)
                    for c in range(4):
                        j = 4 * half + c
                        dve.wait_ge(*freed(USE[f"gate_{br}{half}"] + c))
                        dve.wait_ge(bank_full, e + c + 1)
                        if r >= 1 and 4 * (2 * r + half) + c >= KD + 2:
                            dve.wait_ge(gate_add, KD * (r - 1) + j - 1)
                        dst = merged[:, j, :] if r == 0 else tmp[:, c % 2, :]
                        nc.vector.tensor_tensor(dst, sig[:, c, :], bank[(e + c) % 4][:, :], ALU.mult).then_inc(bank_free[(e + c) % 4], 1)
                        dve.wait_ge(*freed(e + c))
                        if r:
                            nc.vector.tensor_tensor(merged[:, j, :], merged[:, j, :], tmp[:, c % 2, :], ALU.add).then_inc(gate_add, 1)
                    if br == ORDER[-1]:
                        for j in range(4 * half, 4 * half + 4):
                            dve.wait_ge(merged_rounded, j + 1)
                            nc.vector.tensor_tensor(mT_lo[:, j, :], merged[:, j, :], mT_hi[:, j, :].bitcast(F32), ALU.subtract).then_inc(merged_split, 1)

            dsa = attention(U_DSA, N_UNITS, dsa_out)
            gates("a")
            gates("d")
            for j in range(BH):
                split_y("b", j, sz[:, j, :])
            gates("c")
            gates("b")
            def add_out(h, t):
                e = USE[f"out{h}"] + t
                dve.wait_ge(bank_full, e + 1)
                place = x_sb[:, t, W * h:W * h + W]
                nc.vector.tensor_tensor(place, place, bank[e % 4][:, :], ALU.add).then_inc(bank_free[e % 4], 1)

            split(FIRST["out0"] + 1)
            split(FIRST["out0"] + 2)
            dve.wait_ge(x2_loaded, 16)
            for t in range(TT):
                add_out(0, t)
            split(FIRST["out0"] + 3)
            for t in range(TT):
                begin_variance("final", t)
            dve.wait_ge(gpost_loaded, 16 * 5)
            for t in range(TT + 1):
                if t < TT:
                    add_out(1, t)
                if t:
                    variance("final", t - 1, D)
                    scale_rows(m_sb[:, t - 1, :], x_sb[:, t - 1, :], "final", t - 1, g_post[:, :]).then_inc(out_ready, 1)

        @block.tensor
        def _(pe):
            def product(ps, hi_l, lo_l, hi_r, lo_r, first, last):
                nc.tensor.matmul(ps, hi_l, hi_r, start=first, stop=False)
                nc.tensor.matmul(ps, hi_l, lo_r, start=False, stop=False)
                return nc.tensor.matmul(ps, lo_l, hi_r, start=False, stop=last)

            def open_bank(e, turn=0):
                if e >= 4:
                    pe.wait_ge(bank_free[e % 4], e // 4 + turn)

            def feature_chunk(b, e, c, kc, rhs_hi, rhs_lo, tok=slice(0, S), full=True, steps=None, at=()):
                for k in range(kc):
                    w = slice(BLK // kc * k + P * c, BLK // kc * k + P * c + P)
                    last = product(bank[e % 4][:, tok], w_hi[b % RING][:, w], w_lo[b % RING][:, w], rhs_hi[:, k, tok], rhs_lo[:, k, tok],
                                   k == 0, k == kc - 1)
                    if full and k == kc - 1:
                        last.then_inc(bank_full, 1)
                    if k in at:
                        step(steps, 1)

            def feature_major(b, e, chunks, kc, rhs_hi, rhs_lo, steps=None, at=((),) * 4, turn=0):
                pe.wait_ge(w_split, PARTS * (b + 1) + PARTS * RING * turn)
                for c in range(chunks):
                    open_bank(e + c, turn)
                    feature_chunk(b, e + c, c, kc, rhs_hi, rhs_lo, steps=steps, at=at[c])

            def token_major(b, e, counts, wid, lhs_hi, lhs_lo, before=None, after=None):
                k0, total = 0, sum(counts)
                for i, kc in enumerate(counts):
                    for t in range(TT):
                        if i == 0:
                            open_bank(e + t)
                        if before:
                            before(i, t)
                        for k in range(kc):
                            if t == 0:
                                pe.wait_ge(w_split, PARTS * (b + i) + (k + 1 if kc <= PARTS else PARTS))
                            at = BLK // max(kc, KD // 2) * k
                            w = slice(at, at + wid)
                            tok = slice(P * t, P * t + P)
                            last = product(bank[(e + t) % 4][:, 0:wid], lhs_hi[:, k0 + k, tok], lhs_lo[:, k0 + k, tok], w_hi[(b + i) % RING][:, w],
                                           w_lo[(b + i) % RING][:, w], k0 + k == 0, k0 + k == total - 1)
                            if k == kc - 1 and i == len(counts) - 1:
                                last.then_inc(bank_full, 1)
                            if k == kc - 1 and i < len(counts) - 1 and t == TT - 1:
                                last.then_inc(w_used, 1)
                            if after:
                                after(i, t, k)
                    k0 += kc

            def transpose_tile(name, t):
                T = TT * pre_use[name] + t
                pe.wait_ge(xn_done, T + 1)
                for j in range(2):
                    q = 2 * T + j
                    if q >= 4:
                        pe.wait_ge(xT_split, q - 3)
                    for i in range(4):
                        last = nc.tensor.transpose(xp[q % 4][:, P * i:P * i + P], xn[:, t % 2, P * (4 * j + i):P * (4 * j + i) + P], ident[:, :])
                    last.then_inc(xpose_done, 1)

            def tiles_ready(name, t):
                pe.wait_ge(xT_split, 2 * (TT * pre_use[name] + t))

            def as_normed(name):
                def before(i, t):
                    if i == 0:
                        for ahead in range(t + 1 if t else 0, min(t + 2, TT) if name == "pre0" else 1):
                            transpose_tile(name, ahead)
                        tiles_ready(name, t + 1)

                def after(i, t, k):
                    if i == 0 and t < TT - 1 and k == 1 and name != "pre0":
                        transpose_tile(name, t + 1)
                return before, after

            def attention(lo, hi, operands, group, begin, finish):
                for i in range(lo, hi + 7):
                    if lo <= i - 6 < hi and (i - 6 - lo) % group == group - 1:
                        finish((i - 6 - lo) // group)
                    if i < hi:
                        kind, h, t = UNITS[i]
                        score_parts, _ = operands(h, t)
                        if i >= 2:
                            if UNITS[i - 2][0] == "fox":
                                pe.wait_ge(sc_free, i - 2 - U_FOX + 1)
                            else:
                                pe.wait_ge(s_ready, i - 1)
                        for n, (q, k) in enumerate(score_parts):
                            last = nc.tensor.matmul(sc[i % 2][:, 0:P * (t + 1)], q, k, start=n == 0, stop=n == len(score_parts) - 1)
                        last.then_inc(sc_ready, 1)
                    if lo <= i - 3 < hi:
                        u = i - 3
                        t = UNITS[u][2]
                        pe.wait_ge(pn_ready, u + 1)
                        if u >= 1:
                            pe.wait_ge(pT_ready, u)
                        for j in range(t + 1):
                            last = nc.tensor.transpose(tp[:, P * j:P * j + P], s_ring[:, u % 4, P * j:P * j + P], ident[:, :])
                        last.then_inc(tp_ready, 1)
                    if lo <= i - 5 < hi:
                        u = i - 5
                        _, h, t = UNITS[u]
                        _, (vals, dst) = operands(h, t)
                        pe.wait_ge(pT_ready, u + 1)
                        if (u - lo) % group == 0:
                            begin((u - lo) // group)
                        for j in range(t + 1):
                            last = nc.tensor.matmul(dst, vals(j), pT[:, u % 3, P * j:P * j + P], start=j == 0, stop=j == t)
                        last.then_inc(pv_done, 1)
                    yield

            pe.wait_ge(ident_made, 2)
            for h in range(2):
                token_major(FIRST[f"v{h}"], USE[f"v{h}"], (4, 4), W, xT_hi, xT_lo, *(as_normed("pre0") if h == 0 else ()))

            def mha_operands(h, t):
                i, c = h // QK_HEADS, h % QK_HEADS
                if t == 0 and c == 0:
                    pe.wait_ge(first_split, 2 * i + 2)
                if t == 0 and c == 1:
                    pe.wait_ge(*freed(USE[f"qk{i}"]))
                    pe.wait_ge(*freed(USE[f"qk{i}"] + 1))
                rows = slice(HD * c, HD * c + HD)
                tok, keys = slice(P * t, P * t + P), slice(0, P * (t + 1))
                return (((q_st[i % 2][:, c, tok], k_st[i % 2][:, c, keys]), (q_st[i % 2][rows, c, tok], k_rest[i % 2][rows, keys])),
                        (lambda j: v_sb[:, j, HD * h:HD * h + HD], ob[rows, tok]))

            def mha_begin(g):
                if g == 0:
                    for e in range(USE["v0"], USE["qk0"]):
                        pe.wait_ge(*freed(e))
                else:
                    pe.wait_ge(o_free, g)

            mha = attention(0, U_FOX, mha_operands, 2 * TT, mha_begin, lambda g: None)
            for i in range(HEADS // QK_HEADS):
                at = (((), ()), (MHA_FIRST_AT, MHA_AT), (MHA_AT, MHA_AT))[min(i, 2)]
                feature_major(FIRST[f"qk{i}"], USE[f"qk{i}"], 2, KD, xT_hi, xT_lo, mha, at)

            def heads_ready(i, t):
                if t == 0:
                    pe.wait_ge(o_free, HEADS // 4 * (i + 1))

            def last_heads(i, t, k):
                if i == 0:
                    step(mha, 1)

            token_major(FIRST["wo0"], USE["wo0"], (4, 4), W, oT_hi, oT_lo, heads_ready, last_heads)
            token_major(FIRST["wo1"], USE["wo1"], (4, 4), W, oT_hi, oT_lo)

            for half in range(2):
                tok = slice(S // 2 * half, S // 2 * half + S // 2)
                for i in range(2):
                    b, e = FIRST["gu0"] + i, USE["gu0"] + 2 * i
                    if half == 0:
                        transpose_tile("pre1", 2 * i)
                        if i == 0:
                            transpose_tile("pre1", 1)
                            tiles_ready("pre1", 2)
                        pe.wait_ge(w_split, PARTS * (b + 1))
                    elif i == 0:
                        tiles_ready("pre1", TT)
                    for c in range(2):
                        if half == 0:
                            if i == c == 1:
                                transpose_tile("pre1", 3)
                            open_bank(e + c)
                        feature_chunk(b, e + c, c, KD, xT_hi, xT_lo, tok, full=half == 1)
            for f in range(2):
                with pe.Fori(0, GU_LOOP[f][1]) as turn:
                    for i in range(GU_LOOP[f][0], GU_LOOP[f][0] + 2):
                        feature_major(FIRST[f"gu{f}"] + i, USE[f"gu{f}"] + 2 * i, 2, KD, xT_hi, xT_lo, turn=turn)
                for i in range(GU_LOOP[f][0] + 2 * GU_LOOP[f][1], FH):
                    feature_major(FIRST[f"gu{f}"] + i, USE[f"gu{f}"] + 2 * i, 2, KD, xT_hi, xT_lo)

                def gated_ready(i, t):
                    if t == 0:
                        pe.wait_ge(act_split, FH * f + min(FH, 4 * (i + 1)))

                for h in range(2):
                    token_major(FIRST[f"down{f}{h}"], USE[f"down{f}{h}"], (4, 4, 3), W, act_hi, act_lo, gated_ready)

            token_major(FIRST["a_v"], USE["a_v"], (4, 4), W, xT_hi, xT_lo, *as_normed("pre2"))
            token_major(FIRST["cwf"], USE["cwf"], (KD,), P + IDX_H + BH, xT_hi, xT_lo)
            feature_major(FIRST["qi"], USE["qi"], 2, KD, xT_hi, xT_lo)

            def small_products():
                pe.wait_ge(mix_masked, 1)
                pe.wait_ge(ln_done, TT)
                for g in range(KW):
                    n = PREP_MIX + g
                    if g >= 2:
                        pe.wait_ge(prep_free, n - 1)
                    for t in range(TT):
                        last = nc.tensor.matmul(sc[n % 2][:, P * t:P * t + P], av[:, t, P * g:P * g + P], a_ws[:, g, :], start=True, stop=True)
                    last.then_inc(prep_ready, 1)
                    yield
                pe.wait_ge(prep_free, PREP_CT)
                for t in range(TT):
                    pe.wait_ge(c_ready, t + 1)
                    last = nc.tensor.transpose(sc[PREP_CT % 2][:, P * t:P * t + P], c_sb[:, t, :], ident[:, :])
                last.then_inc(prep_ready, 1)
                yield
                for c in range(2):
                    pe.wait_ge(*freed(USE["qi"] + c))
                pe.wait_ge(*freed(USE["ki"]))
                for t in range(1, TT):
                    for h in range(IDX_H):
                        n = PREP_IDX + IDX_H * (t - 1) + h
                        pe.wait_ge(prep_free, n - 1)
                        rows = slice(IDX_D * (h % 2), IDX_D * (h % 2) + IDX_D)
                        tok, keys = slice(P * t, P * t + P), slice(0, P * (t + 1))
                        nc.tensor.matmul(sc[n % 2][:, keys], qi_st[:, h, tok], ki_st[:, keys], start=True, stop=False)
                        nc.tensor.matmul(sc[n % 2][:, keys], qi_st[rows, h, tok], ki_rest[rows, keys], start=False, stop=True).then_inc(prep_ready, 1)
                        yield
                pe.wait_ge(tri_made, 2)
                pe.wait_ge(f_ls, 1)
                n = PREP_CUM
                pe.wait_ge(prep_free, n - 1)
                for t in range(TT):
                    last = nc.tensor.matmul(sc[n % 2][0:BH, P * t:S], ls[:, t, :], tri[:, 0:S - P * t], start=t == 0, stop=t == TT - 1)
                last.then_inc(prep_ready, 1)
                yield
                n = PREP_CUM + 1
                pe.wait_ge(prep_free, n - 1)
                for t in range(TT):
                    for j in range(t + 1):
                        ones = tri[:, 0:P] if j == t else tri[:, P:2 * P]
                        last = nc.tensor.matmul(sc[n % 2][:, BH * t:BH * t + BH], ones, ls[:, j, :], start=j == 0, stop=j == t)
                last.then_inc(prep_ready, 1)
                yield
                pe.wait_ge(latent_loaded, 32)
                for h in range(BH):
                    n = PREP_QLAT + h
                    pe.wait_ge(*freed(USE["b_q"] + h))
                    pe.wait_ge(prep_free, n - 1)
                    nc.tensor.matmul(sc[n % 2][:, :], wukT[:, h, :], bq[:, h, :], start=True, stop=True).then_inc(prep_ready, 1)
                    yield

            small = small_products()
            feature_major(FIRST["ki"], USE["ki"], 1, KD, xT_hi, xT_lo, small, (MIX_AT,))
            for j in range(KW):
                at = (IDX_AT if j else IDX_FIRST_AT, IDX_AT) if j < TT - 1 else ((), ())
                feature_major(FIRST["a_uz"] + j, USE["a_uz"] + 2 * j, 2, KD, xT_hi, xT_lo, small, at)
            for i in range(2):
                feature_major(FIRST["d_q"] + i, USE["d_q"] + 2 * i, 2, KD, xT_hi, xT_lo, small, ((), ()) if i else (ONE_AT, ONE_AT))
            for i in range(2):
                feature_major(FIRST["d_k"] + i, USE["d_k"] + 2 * i, 2, KD, xT_hi, xT_lo)
            token_major(FIRST["d_v"], USE["d_v"], (4, 4), W, xT_hi, xT_lo)
            for i in range(2):
                feature_major(FIRST["d_z"] + i, USE["d_z"] + 2 * i, 2, KD, xT_hi, xT_lo)

            def fox_operands(h, t):
                return (((dqk[:, h, P * t:P * t + P], dqk[:, BH + h, 0:P * (t + 1)]),),
                        (lambda j: dv[:, j, BD * h:BD * h + BD], ob[:, P * t:P * t + P]))

            for e in range(USE["d_v"], USE["d_v"] + 4):
                pe.wait_ge(*freed(e))
            pe.wait_ge(prep_free, PREP_QLAT)

            fox = attention(U_FOX, U_DSA, fox_operands, TT, lambda g: pe.wait_ge(o_free, O_FOX + g), lambda g: None)
            for i in range(2 * KW):
                feature_major(FIRST["c"] + i, USE["c"] + 2 * i, 2, KD, xT_hi, xT_lo, fox, (PAIR_AT, PAIR_AT))
            step(fox, U_DSA)

            for i in range(2):
                feature_major(FIRST["b_q"] + i, USE["b_q"] + 2 * i, 2, KD, xT_hi, xT_lo)
            for i in range(2):
                feature_major(FIRST["b_z"] + i, USE["b_z"] + 2 * i, 2, KD, xT_hi, xT_lo, small, (ONE_AT, ONE_AT))

            def dsa_operands(h, t):
                return (((qlat[:, h, P * t:P * t + P], cT[:, 0:P * (t + 1)]),), (lambda j: c_sb[:, j, :], ob[:, P * t:P * t + P]))

            def dsa_finish(g):
                pe.wait_ge(olat_ready, g + 1)
                nc.tensor.matmul(ob[:, :], wuv[:, g, :], olat, start=True, stop=True).then_inc(ydsa_ready, 1)

            def gates(br):
                ys = slot[br]
                for half in range(2):
                    for i in range(2):
                        feature_major(FIRST[f"gate_{br}{half}"] + i, USE[f"gate_{br}{half}"] + 2 * i, 2, KD, xT_hi, xT_lo, dsa, (PAIR_AT, PAIR_AT))
                    pe.wait_ge(y_split[br], KW)
                    feature_major(FIRST[f"branch_{br}{half}"], USE[f"branch_{br}{half}"], 4, KW, y_hi[ys], y_lo[ys])

            pe.wait_ge(prep_free, N_PREP)
            dsa = attention(U_DSA, N_UNITS, dsa_operands, TT, lambda g: pe.wait_ge(o_free, O_DSA + g), dsa_finish)
            for br in ORDER:
                gates(br)

            def merged_ready(i, t):
                if t == 0:
                    pe.wait_ge(merged_split, 4 * (i + 1))

            for h in range(2):
                token_major(FIRST[f"out{h}"], USE[f"out{h}"], (4, 4), W, mT_hi, mT_lo, merged_ready)


def pack_rows(w, rows, cols):
    part = w[rows][:, cols].reshape(-1, P, len(cols)).transpose(1, 0, 2)
    chunks = max(part.shape[1], KD // 2)
    out = np.zeros((P, chunks, BLK // chunks), w.dtype)
    out[:, :part.shape[1], :len(cols)] = part
    return out.reshape(P, BLK)


def weight_stream(a):
    blocks = []
    r = lambda *x: np.concatenate([np.arange(*p) for p in x])
    w_qkv, w_in = a["w_qkv"][0], a["w_in_2"][0]
    every = np.arange(D)

    def token_blocks(w, rows, cols, step=4):
        for k in range(0, len(rows), step * P):
            blocks.append(pack_rows(w, rows[k:k + step * P], cols))

    for h in range(2):
        token_blocks(w_qkv, every, r((2 * D + W * h, 2 * D + W * h + W)))
    for i in range(HEADS // QK_HEADS):
        blocks.append(pack_rows(w_qkv, every, r((P * i, P * i + P), (D + P * i, D + P * i + P))))
    for h in range(2):
        token_blocks(a["w_o"][0], every, r((W * h, W * h + W)))
    gu = np.stack([a["w_gate"][0].reshape(D, FC, P), a["w_up"][0].reshape(D, FC, P)], 2).reshape(D, 2 * FF)
    for f in range(2):
        for i in range(FH * f, FH * f + FH):
            blocks.append(pack_rows(gu, every, r((256 * i, 256 * i + 256))))
        for h in range(2):
            token_blocks(a["w_down"][0], np.arange(FH * f * P, FH * (f + 1) * P), r((W * h, W * h + W)))
    col = {n: np.arange(*c) for n, c in COL.items()}

    def cols(*names):
        c = np.concatenate([col[n] for n in names])
        for i in range(0, len(c), 256):
            blocks.append(pack_rows(w_in, every, c[i:i + 256]))

    def pairs(x, y, j):
        blocks.append(pack_rows(w_in, every, np.concatenate([col[x][P * j:P * j + P], col[y][P * j:P * j + P]])))

    token_blocks(w_in, every, col["a_v"])
    cols("b_c", "b_wi", "d_f")
    cols("b_qi")
    cols("b_ki", "b_ki")
    for j in range(KW):
        pairs("a_u", "a_z", j)
    cols("d_q")
    cols("d_k")
    token_blocks(w_in, every, col["d_v"])
    cols("d_z")
    for j in range(KW):
        pairs("c_c", "c_x", j)
        pairs("c_b", "c_z", j)
    cols("b_q")
    cols("b_z")
    for br in ORDER:
        n = BRANCH[br]
        for half in range(2):
            for i in range(2):
                at = col["gates"][0] + D * n + W * half + 256 * i
                blocks.append(pack_rows(w_in, every, r((at, at + 256))))
            blocks.append(pack_rows(a["w_branch_2"][0, n], np.arange(W), r((W * half, W * half + W))))
    for h in range(2):
        token_blocks(a["w_out_2"][0], every, r((W * h, W * h + W)))
    assert len(blocks) == N_BLOCKS, (len(blocks), N_BLOCKS)
    return np.stack(blocks)


def kernel(**inputs):
    import concourse.bacc as bacc
    from concourse.bass_utils import run_bass_kernel_spmd

    a = {k: np.asarray(v) for k, v in inputs.items()}
    clip = np.clip(P + np.arange(P)[:, None] - np.arange(BIAS_W)[None, :], 1 - CHUNK, REL_CLIP) + CHUNK - 1
    arrays = {
        "weights": weight_stream(a),
        "x": a["x"][0],
        "bias": a["rel_bias"][0][:, clip],
        "g_first": a["g_pre_mix"][0],
        "gcol": np.stack([a["g_pre_ffn"][0], a["norm_g_2"][0]]).reshape(2, KD, P).transpose(2, 0, 1),
        "g_post_mix": a["g_post_mix"][0],
        "g_post_ffn": a["g_post_ffn"][0],
        "final_g": a["final_g_2"],
        "ln_g": a["gm_ln_g_2"][0], "ln_b": a["gm_ln_b_2"][0],
        "gm_b": a["gm_b_s_2"][0], "gm_wT": a["gm_w_s_2"][0].transpose(2, 0, 1),
        "kvg": a["dsa_kv_g_2"][0], "bf": a["fox_b_f_2"][0],
        "wukT": a["dsa_w_uk_2"][0].transpose(2, 0, 1), "wuv": a["dsa_w_uv_2"][0].transpose(1, 0, 2),
        "convw": a["conv_w_2"][0].reshape(3, KW, P).transpose(2, 1, 0),
    }
    nc = bacc.Bacc("TRN2", target_bir_lowering=False, num_devices=1)
    feeds, dram = {}, {}
    for name, v in arrays.items():
        v = np.ascontiguousarray(v)
        feeds[f"in_{name}"] = v
        dram[name] = nc.dram_tensor(f"in_{name}", v.shape, mybir.dt.from_np(v.dtype), kind="ExternalInput").ap()
    out = nc.dram_tensor("out_0", (S, D), F32, kind="ExternalOutput").ap()
    build(nc, dram, out)
    r = run_bass_kernel_spmd(nc, [feeds], core_ids=[0])
    return r.results[0]["out_0"].reshape(1, S, D)
```
